# Optimizing a Trainium2 kernel written in Bass

```python
import jax
import jax.numpy as jnp
from jax import lax
import numpy as np

D_MODEL = 1024
BATCH = 1
SEQ = 256
DEPTH = 2

HEAD_DIM = 64
A_GROUPS = 4
A_GROUP_CH = 128
A_WIDTH = A_GROUPS * A_GROUP_CH
CHUNK = 128
DILATED_PATTERNS = ((128, 1), (512, 4), (2048, 16))
B_HEADS_PER_GROUP = 4
B_HEADS = len(DILATED_PATTERNS) * B_HEADS_PER_GROUP
B_WIDTH = B_HEADS * HEAD_DIM
B_OUT = B_HEADS_PER_GROUP * HEAD_DIM
BLOCK = 128
ROPE_THETA = 500000.0
ROPE_DIMS = HEAD_DIM // 4
C_HEADS = 8
C_WIDTH = C_HEADS * HEAD_DIM
W_LORA = 64
A_LORA = 64
V_LORA = 32
G_LORA = 128
RWKV_GN_EPS = HEAD_DIM * 1e-5
IN_SPLIT_WIDTHS = (A_WIDTH, A_WIDTH, B_WIDTH, B_WIDTH, B_WIDTH, C_WIDTH, C_WIDTH, C_WIDTH)
IN_COLS = 2 * A_WIDTH + 3 * B_WIDTH + 3 * C_WIDTH
N_BRANCHES = 3
N_GROUPS = 4
EXPERTS_PER_GROUP = 4
N_EXPERTS = N_GROUPS * EXPERTS_PER_GROUP
EXPERT_FF = 512
TOP_K_IN_GROUP = 2
RMS_EPS = 1e-6
LN_EPS = 1e-5

kernel_name = 'hybrid_gated_mixers_hier_moe'

def rmsnorm(x, g):
    xf = x.astype(jnp.float32)
    y = xf * lax.rsqrt(jnp.mean(xf * xf, axis=-1, keepdims=True) + RMS_EPS)
    return (y * g.astype(jnp.float32)).astype(x.dtype)

def shift_prev(t):
    return jnp.pad(t, ((0, 0), (1, 0), (0, 0)))[:, :-1]

def split_heads(t, n_heads):
    return t.reshape(t.shape[:-1] + (n_heads, HEAD_DIM))

def partial_rotary(t, positions):
    half = ROPE_DIMS // 2
    inv_freq = ROPE_THETA ** (-jnp.arange(half, dtype=jnp.float32) / half)
    ang = positions.astype(jnp.float32)[..., None] * inv_freq
    cos = jnp.cos(ang)[:, :, None, :]
    sin = jnp.sin(ang)[:, :, None, :]
    tr = t[..., :ROPE_DIMS].astype(jnp.float32)
    t1, t2 = tr[..., :half], tr[..., half:]
    rot = jnp.concatenate([t1 * cos - t2 * sin, t2 * cos + t1 * sin], axis=-1).astype(t.dtype)
    return jnp.concatenate([rot, t[..., ROPE_DIMS:]], axis=-1)

def chunked_spatial_gating(u, v, ln_g, ln_b, w_s, b_s):
    Bn, S, _ = u.shape
    vf = v.astype(jnp.float32)
    mu = jnp.mean(vf, axis=-1, keepdims=True)
    var = jnp.mean(jnp.square(vf - mu), axis=-1, keepdims=True)
    vn = ((vf - mu) * lax.rsqrt(var + LN_EPS) * ln_g + ln_b).astype(v.dtype)
    vn = vn.reshape(Bn, S // CHUNK, CHUNK, A_GROUPS, A_GROUP_CH)
    causal = jnp.tril(jnp.ones((CHUNK, CHUNK), dtype=bool))
    w_causal = jnp.where(causal[None], w_s, jnp.zeros_like(w_s))
    mixed = jnp.einsum('gts,bnsgc->bntgc', w_causal, vn) + b_s.T[:, :, None]
    return u * mixed.reshape(Bn, S, A_WIDTH)

def dilated_window_attention(q, k, v, window, dilation):
    Bn, S, H, Dh = q.shape
    L = S // dilation
    nb = -(-L // BLOCK)
    Lp = nb * BLOCK
    steps = window // dilation

    def to_blocks(t):
        t = t.reshape(Bn, L, dilation, H, Dh).transpose(0, 2, 1, 3, 4)
        t = jnp.pad(t, ((0, 0), (0, 0), (0, Lp - L), (0, 0), (0, 0)))
        return t.reshape(Bn, dilation, nb, BLOCK, H, Dh)

    def with_prev(t):
        prev = jnp.pad(t, ((0, 0), (0, 0), (1, 0), (0, 0), (0, 0), (0, 0)))[:, :, :-1]
        return jnp.concatenate([prev, t], axis=3)

    qb = to_blocks(q)
    kw = with_prev(to_blocks(k))
    vw = with_prev(to_blocks(v))
    scores = jnp.einsum('brnqhd,brnkhd->brnhqk', qb, kw,
                        preferred_element_type=jnp.float32) * (Dh ** -0.5)
    qi = jnp.arange(BLOCK)[:, None]
    kj = jnp.arange(2 * BLOCK)[None, :]
    dist = BLOCK + qi - kj
    in_band = (dist >= 0) & (dist <= steps)
    has_key = (jnp.arange(nb) > 0)[:, None, None] | (kj >= BLOCK)[None]
    valid = in_band[None] & has_key
    scores = jnp.where(valid[None, None, :, None], scores, -jnp.inf)
    lse = jax.nn.logsumexp(scores, axis=-1)
    p = jnp.exp(scores - lse[..., None]).astype(v.dtype)
    out = jnp.einsum('brnhqk,brnkhd->brnqhd', p, vw)

    def from_blocks(t):
        tail = t.shape[4:]
        t = t.reshape((Bn, dilation, Lp) + tail)[:, :, :L]
        return jnp.swapaxes(t, 1, 2).reshape((Bn, S) + tail)

    return from_blocks(out), from_blocks(jnp.swapaxes(lse, -1, -2))

def dilated_attention_branch(q, k, v, positions):
    Bn, S = q.shape[:2]
    q = partial_rotary(q, positions)
    k = partial_rotary(k, positions)
    outs, lses = [], []
    for g, (window, dilation) in enumerate(DILATED_PATTERNS):
        hs = slice(g * B_HEADS_PER_GROUP, (g + 1) * B_HEADS_PER_GROUP)
        o, l = dilated_window_attention(q[:, :, hs], k[:, :, hs], v[:, :, hs], window, dilation)
        outs.append(o)
        lses.append(l)
    weights = jax.nn.softmax(jnp.stack(lses, axis=0), axis=0)
    out = jnp.sum(weights[..., None] * jnp.stack(outs, axis=0).astype(jnp.float32), axis=0)
    return out.reshape(Bn, S, B_OUT).astype(q.dtype)

def rwkv7_time_mix(h, r, k, v, v_first, mu_rkv, mu_wag, w0, w1, w2, a0, a1, a2, g1, g2,
                   k_k, k_a, r_k, ln_w, ln_b, vres):
    Bn, S, _ = h.shape
    f32 = jnp.float32
    r = r + (shift_prev(r) - r) * mu_rkv[0]
    k = k + (shift_prev(k) - k) * mu_rkv[1]
    v = v + (shift_prev(v) - v) * mu_rkv[2]
    dh = shift_prev(h) - h
    xw = h + dh * mu_wag[0]
    xa = h + dh * mu_wag[1]
    xg = h + dh * mu_wag[2]
    w_log = -jax.nn.softplus(-(w0 + jnp.tanh(xw @ w1) @ w2).astype(f32)) - 0.5
    decay = jnp.exp(-jnp.exp(w_log))
    a = jax.nn.sigmoid(a0 + (xa @ a1) @ a2)
    g = jax.nn.sigmoid(xg @ g1) @ g2
    if vres is not None:
        mu_v, v0, v1, v2 = vres
        xv = h + dh * mu_v
        v = v + (v_first - v) * jax.nn.sigmoid(v0 + (xv @ v1) @ v2)
    kk = split_heads(k * k_k, C_HEADS).astype(f32)
    kk = kk / jnp.maximum(jnp.sqrt(jnp.sum(kk * kk, axis=-1, keepdims=True)), 1e-12)
    k = k * (1 + (a - 1) * k_a)
    rh = split_heads(r, C_HEADS).astype(f32)
    kh = split_heads(k, C_HEADS).astype(f32)
    vh = split_heads(v, C_HEADS).astype(f32)
    ah = split_heads(a, C_HEADS).astype(f32)
    wh = split_heads(decay, C_HEADS)

    def step(state, inp):
        r_t, w_t, k_t, v_t, kk_t, a_t = inp
        sa = jnp.einsum('bhvk,bhk->bhv', state, -kk_t)
        state = (state * w_t[:, :, None, :] + sa[..., None] * (kk_t * a_t)[:, :, None, :]
                 + v_t[..., None] * k_t[:, :, None, :])
        return state, jnp.einsum('bhvk,bhk->bhv', state, r_t)

    xs = tuple(jnp.moveaxis(t, 1, 0) for t in (rh, wh, kh, vh, kk, ah))
    state0 = jnp.zeros((Bn, C_HEADS, HEAD_DIM, HEAD_DIM), f32)
    _, y = lax.scan(step, state0, xs)
    y = jnp.moveaxis(y, 0, 1)
    mu = jnp.mean(y, axis=-1, keepdims=True)
    var = jnp.mean(jnp.square(y - mu), axis=-1, keepdims=True)
    y = (y - mu) * lax.rsqrt(var + RWKV_GN_EPS)
    y = y * split_heads(ln_w, C_HEADS).astype(f32) + split_heads(ln_b, C_HEADS).astype(f32)
    bonus = jnp.sum(rh * kh * r_k.astype(f32), axis=-1, keepdims=True) * vh
    y = (y + bonus).reshape(Bn, S, C_WIDTH).astype(h.dtype)
    return y * g, v

def hierarchical_moe(x, wg, bg, we, be, w_gate, w_up, w_down):
    Bn, S, D = x.shape
    xt = x.reshape(Bn * S, D)
    group_prob = jax.nn.softmax((xt @ wg + bg).astype(jnp.float32), axis=-1)
    gp, gi = lax.top_k(group_prob, 1)
    expert_logits = (xt @ we + be).astype(jnp.float32).reshape(-1, N_GROUPS, EXPERTS_PER_GROUP)
    sel_logits = jnp.take_along_axis(expert_logits, gi[:, :, None], axis=1)[:, 0]
    ep, ei = lax.top_k(jax.nn.softmax(sel_logits, axis=-1), TOP_K_IN_GROUP)
    ep = ep / jnp.sum(ep, axis=-1, keepdims=True)
    in_group = jnp.sum(jax.nn.one_hot(ei, EXPERTS_PER_GROUP) * ep[..., None], axis=1)
    combine = jax.nn.one_hot(gi[:, 0], N_GROUPS)[:, :, None] * (gp * in_group)[:, None, :]
    combine = combine.reshape(-1, N_EXPERTS).astype(x.dtype)
    out = jnp.zeros_like(xt)
    for g in range(N_GROUPS):
        es = slice(g * EXPERTS_PER_GROUP, (g + 1) * EXPERTS_PER_GROUP)
        hid = (jax.nn.silu(jnp.einsum('nd,edf->nef', xt, w_gate[es]))
               * jnp.einsum('nd,edf->nef', xt, w_up[es]))
        out = out + jnp.einsum('nef,efd->nd', hid * combine[:, es, None], w_down[es])
    return out.reshape(Bn, S, D)

def setup_inputs(seed: int = 0) -> dict:
    key = jax.random.key(seed)
    ks = iter(jax.random.split(key, 48))
    f32 = jnp.float32
    D = D_MODEL
    L = DEPTH

    def normal(shape, scale):
        return jax.random.normal(next(ks), shape, f32) * scale

    def uniform(shape, lo, hi):
        return jax.random.uniform(next(ks), shape, f32, lo, hi)

    x = normal((BATCH, SEQ, D), 1.0)
    start = jax.random.randint(next(ks), (BATCH, 1), 0, 4096, dtype=jnp.int32)
    positions = start + jnp.arange(SEQ, dtype=jnp.int32)[None, :]
    return {
        'x': x,
        'positions': positions,
        'norm_mix_g': 1.0 + normal((L, D), 0.01),
        'w_in': normal((L, D, IN_COLS), D ** -0.5),
        'gmlp_ln_g': 1.0 + normal((L, A_WIDTH), 0.01),
        'gmlp_ln_b': normal((L, A_WIDTH), 0.01),
        'gmlp_ws': normal((L, A_GROUPS, CHUNK, CHUNK), CHUNK ** -0.5),
        'gmlp_bs': 1.0 + normal((L, A_GROUPS, CHUNK), 0.01),
        'rwkv_mu_rkv': uniform((L, 3, C_WIDTH), 0.0, 1.0),
        'rwkv_mu_wag': uniform((L, 3, D), 0.0, 1.0),
        'rwkv_w0': uniform((L, C_WIDTH), -4.0, 1.0),
        'rwkv_w1': normal((L, D, W_LORA), D ** -0.5),
        'rwkv_w2': normal((L, W_LORA, C_WIDTH), 0.1 * W_LORA ** -0.5),
        'rwkv_a0': normal((L, C_WIDTH), 0.5),
        'rwkv_a1': normal((L, D, A_LORA), D ** -0.5),
        'rwkv_a2': normal((L, A_LORA, C_WIDTH), 0.5 * A_LORA ** -0.5),
        'rwkv_g1': normal((L, D, G_LORA), D ** -0.5),
        'rwkv_g2': normal((L, G_LORA, C_WIDTH), G_LORA ** -0.5),
        'rwkv_k_k': 0.85 + normal((L, C_WIDTH), 0.05),
        'rwkv_k_a': 1.0 + normal((L, C_WIDTH), 0.05),
        'rwkv_r_k': normal((L, C_HEADS, HEAD_DIM), 0.1),
        'rwkv_ln_w': 1.0 + normal((L, C_WIDTH), 0.01),
        'rwkv_ln_b': normal((L, C_WIDTH), 0.01),
        'rwkv_mu_v': uniform((L - 1, D), 0.0, 1.0),
        'rwkv_v0': normal((L - 1, C_WIDTH), 0.5),
        'rwkv_v1': normal((L - 1, D, V_LORA), D ** -0.5),
        'rwkv_v2': normal((L - 1, V_LORA, C_WIDTH), 0.5 * V_LORA ** -0.5),
        'w_branch_a': normal((L, A_WIDTH, D), A_WIDTH ** -0.5),
        'w_branch_b': normal((L, B_OUT, D), B_OUT ** -0.5),
        'w_branch_c': normal((L, C_WIDTH, D), C_WIDTH ** -0.5),
        'w_gate': normal((L, D, N_BRANCHES * D), D ** -0.5),
        'b_gate': normal((L, N_BRANCHES * D), 0.01),
        'w_out': normal((L, D, D), D ** -0.5),
        'norm_ffn_g': 1.0 + normal((L, D), 0.01),
        'router_group_w': normal((L, D, N_GROUPS), D ** -0.5),
        'router_group_b': normal((L, N_GROUPS), 0.01),
        'router_expert_w': normal((L, D, N_EXPERTS), D ** -0.5),
        'router_expert_b': normal((L, N_EXPERTS), 0.01),
        'expert_w_gate': normal((L, N_EXPERTS, D, EXPERT_FF), D ** -0.5),
        'expert_w_up': normal((L, N_EXPERTS, D, EXPERT_FF), D ** -0.5),
        'expert_w_down': normal((L, N_EXPERTS, EXPERT_FF, D), EXPERT_FF ** -0.5),
        'final_norm_g': 1.0 + normal((D,), 0.01),
    }

def reference(x, positions, norm_mix_g, w_in, gmlp_ln_g, gmlp_ln_b, gmlp_ws, gmlp_bs,
              rwkv_mu_rkv, rwkv_mu_wag, rwkv_w0, rwkv_w1, rwkv_w2, rwkv_a0, rwkv_a1, rwkv_a2,
              rwkv_g1, rwkv_g2, rwkv_k_k, rwkv_k_a, rwkv_r_k, rwkv_ln_w, rwkv_ln_b,
              rwkv_mu_v, rwkv_v0, rwkv_v1, rwkv_v2, w_branch_a, w_branch_b, w_branch_c,
              w_gate, b_gate, w_out, norm_ffn_g, router_group_w, router_group_b,
              router_expert_w, router_expert_b, expert_w_gate, expert_w_up, expert_w_down,
              final_norm_g):
    Bn, S, D = x.shape
    split_at = np.cumsum(IN_SPLIT_WIDTHS)[:-1].tolist()
    v_first = None
    for l in range(DEPTH):
        h = rmsnorm(x, norm_mix_g[l])
        proj = h @ w_in[l]
        u_a, v_a, q_b, k_b, v_b, r_c, k_c, v_c = jnp.split(proj, split_at, axis=-1)
        y_a = chunked_spatial_gating(jax.nn.gelu(u_a), jax.nn.gelu(v_a), gmlp_ln_g[l],
                                     gmlp_ln_b[l], gmlp_ws[l], gmlp_bs[l])
        y_b = dilated_attention_branch(split_heads(q_b, B_HEADS), split_heads(k_b, B_HEADS),
                                       split_heads(v_b, B_HEADS), positions)
        vres = None if l == 0 else (rwkv_mu_v[l - 1], rwkv_v0[l - 1], rwkv_v1[l - 1], rwkv_v2[l - 1])
        y_c, v_c = rwkv7_time_mix(h, r_c, k_c, v_c, v_first, rwkv_mu_rkv[l], rwkv_mu_wag[l],
                                  rwkv_w0[l], rwkv_w1[l], rwkv_w2[l], rwkv_a0[l], rwkv_a1[l],
                                  rwkv_a2[l], rwkv_g1[l], rwkv_g2[l], rwkv_k_k[l], rwkv_k_a[l],
                                  rwkv_r_k[l], rwkv_ln_w[l], rwkv_ln_b[l], vres)
        if l == 0:
            v_first = v_c
        gates = jax.nn.sigmoid(h @ w_gate[l] + b_gate[l]).reshape(Bn, S, N_BRANCHES, D)
        merged = (gates[:, :, 0] * (y_a @ w_branch_a[l])
                  + gates[:, :, 1] * (y_b @ w_branch_b[l])
                  + gates[:, :, 2] * (y_c @ w_branch_c[l]))
        x = x + merged @ w_out[l]
        x = x + hierarchical_moe(rmsnorm(x, norm_ffn_g[l]), router_group_w[l], router_group_b[l],
                                 router_expert_w[l], router_expert_b[l], expert_w_gate[l],
                                 expert_w_up[l], expert_w_down[l])
    return rmsnorm(x, final_norm_g)


_drawn_inputs = setup_inputs


def setup_inputs(seed=0):
    import zlib

    import numpy as np

    out = dict(_drawn_inputs(seed))
    spreads = {}
    factors = {'gmlp_ln_g': 83.167,
     'gmlp_ln_b': 56.442,
     'rwkv_w1': 12.347,
     'rwkv_w2': 11.49,
     'rwkv_ln_w': 30.312,
     'b_gate': 4.177,
     'router_expert_b': 38.123,
     'final_norm_g': 195.404,
     'gmlp_bs': 38.04,
     'rwkv_ln_b': 35.496,
     'router_group_b': 25.616,
     'rwkv_k_k': 6.228,
     'rwkv_mu_v': 3.779,
     'norm_ffn_g': 8.0}
    for name, (base, spread) in spreads.items():
        noise = np.random.default_rng([zlib.crc32(name.encode()), seed]).standard_normal(out[name].shape)
        drawn = base * np.exp(spread * noise) if base else spread * noise
        out[name] = jnp.asarray(drawn.astype(out[name].dtype))
    for name, factor in factors.items():
        out[name] = (out[name] * factor).astype(out[name].dtype)
    return out
```

```python
from contextlib import ExitStack

import numpy as np

import concourse.bass as bass
from concourse import mybir

F32 = mybir.dt.float32
I32 = mybir.dt.int32
ACT = mybir.ActivationFunctionType
ALU = mybir.AluOpType
AX_X = mybir.AxisListType.X

P = 128
S = 256
NT = S // P
D = 1024
KC = D // P
W = 512
LAYERS = 2
HD = 64
AG = 4
BH = 12
BHG = 4
CH = 8
NE = 16
NG = 4
EPG = 4
FF = 512
HALF = 8
RING = 3
DECAY = float(np.float32(np.exp(-0.5)))
NEG = -1e30
ROUND = 12582912.0
LEVELS = 7

U0, V0, Q0, K0, VB0, R0, CK0, CV0, PCOLS = 0, 512, 1024, 1792, 2560, 3328, 3840, 4352, 4864

CONST_AT = {}


def constants():
    j = np.arange(P)[:, None]
    t = np.arange(P)[None, :]
    mid = (j < P // 2).astype(np.float64)
    parts = {
        "ident": (j == t),
        "decay_incl": -DECAY * ((j <= t) - mid),
        "decay_prev": -DECAY * ((j < t) - mid),
        "shift": (j == t - 1).astype(float) - (j == t),
        "edge": (j == P - 1) & (t == 0),
        "low_strict": (j < t),
        "low_incl": (j <= t),
        "after_mid": -DECAY * (1 - mid),
        "before_mid": -DECAY * mid,
    }
    for k in range(LEVELS):
        n = 1 << k
        parts[f"level{k}"] = (j // (2 * n) == t // (2 * n)) & (j % (2 * n) < n) & (t % (2 * n) >= n)
    for tile in range(NT):
        q = tile * P + j
        rows = []
        for window, dil in ((128, 1), (512, 4), (2048, 16)):
            k = np.arange((tile + 1) * P)[None, :]
            ok = (q >= k) & (q - k <= window) & ((q - k) % dil == 0)
            rows.append(np.where(ok, 0.0, NEG))
        parts[f"attend{tile}"] = np.concatenate(rows, 1)
    parts["first"] = np.broadcast_to(4.0 - np.arange(4), (P, 4))
    freq = 500000.0 ** (-np.arange(HALF) / HALF)
    parts["freq"] = np.broadcast_to(freq, (P, HALF))
    parts["eps_rms"] = np.full((P, 1), 1e-6)
    parts["eps_ln"] = np.full((P, 1), 1e-5)
    parts["eps_gn"] = np.full((P, 1), HD * 1e-5)
    parts["zero"] = np.zeros((P, 1))
    at = 0
    for name, a in parts.items():
        CONST_AT[name] = (at, a.shape[1])
        at += a.shape[1]
    table = np.concatenate([np.asarray(a, np.float64) for a in parts.values()], 1).astype(np.float32)
    select = np.zeros((10, 10, P), np.float32)
    select[np.arange(10), np.arange(10)] = 1.0
    return table, select.reshape(10, 10 * P)


TABLE, SELECT = constants()


def two_pi_parts():
    left, parts = 2 * np.pi, []
    for _ in range(3):
        e = np.floor(np.log2(left))
        p = np.floor(left / 2 ** (e - 7)) * 2 ** (e - 7)
        parts.append(float(p))
        left -= p
    return parts + [float(np.float32(left))]


TWO_PI = two_pi_parts()


def layer_blocks():
    out = [("proj", R0, W), ("proj", CK0, W), ("proj", CV0, W), ("lora1",), ("lora2",)]
    out += [("proj", c, min(W, R0 - c)) for c in range(0, R0, W)]
    for b in range(3):
        for half in range(2):
            out += [("gate", 2 * b + half), ("branch", b, half)]
    out += [("out", 0), ("out", 1)]
    return out


BLOCKS = layer_blocks()
NB = len(BLOCKS)
PER_LAYER = NB + 3 * NE
DMAS = {"lora1": 4, "lora2": 4}


def landed_after(layer, n):
    g = layer * PER_LAYER + n
    slot = g % RING
    total = 0
    for l in range(layer + 1):
        for i in range(PER_LAYER):
            if l * PER_LAYER + i > g:
                break
            if (l * PER_LAYER + i) % RING == slot:
                total += 16 * (DMAS.get(BLOCKS[i][0], 1) if i < NB else 1)
    return slot, total


def hybrid_moe_kernel(nc, a):
    ctx = ExitStack()
    with ctx:
        def sb(name, shape, dt=F32):
            return ctx.enter_context(nc.sbuf_tensor(name, shape, dt))

        def sem(name):
            return ctx.enter_context(nc.semaphore(name))

        x = sb("x_res", [P, NT, D])
        hT = sb("hT", [P, KC, S])
        ring = sb("ring", [P, RING, 8 * W])
        proj = sb("proj", [P, NT, PCOLS])
        tab = sb("tab", [P, TABLE.shape[1]])
        sel = sb("sel", [10, 10, P])
        v_first = sb("v_first", [P, NT, W])
        arena = sb("arena", [P, 9216])
        lw = sb("lw", [P, NT, W])
        aa = sb("aa", [P, NT, W])
        gg = sb("gg", [P, NT, W])
        kk = sb("kk", [P, NT, W])
        krT = sb("krT", [P, 4, 2, P])
        tmp = sb("tmp", [P, 3, W])
        bc = sb("bc", [P, 8, W])
        state = sb("state", [P, 4, P])
        bias_rows = sb("bias_rows", [10, W])
        vec_rows = krT[0:52, 0, 0, :]
        vec = sb("vec", [P, 52])
        rw = sb("rw", [P, KC, 20])
        pos_i = sb("pos_i", [P, NT], I32)
        small = sb("small", [P, 400])
        angle = sb("angle", [P, 6, NT * HALF])

        PS = ctx.enter_context(nc.psum_tensor("PS", [P, 8, W], F32))

        def const(name):
            at, n = CONST_AT[name]
            return tab[:, at:at + n]

        ident = const("ident")

        def view(at, *shape):
            n = int(np.prod(shape))
            v = arena[:, at:at + n]
            if len(shape) == 1:
                return v
            names = "abcd"[:len(shape)]
            return v.rearrange(f"p ({' '.join(names)}) -> p {' '.join(names)}",
                               **{k: s for k, s in zip(names[1:], shape[1:])})

        h_nat = view(0, NT, D)
        dhT = view(0, KC, S)
        mix = [view(2048, KC, S), view(4096, KC, S)]
        loraT = [view(6144 + 256 * m, S) for m in range(4)]
        SCb, SCk = view(0, CH, 2, P), view(2048, CH, 2, P)
        X, XT = view(4096, CH, P), view(5120, CH, P)
        Yl = view(6144, CH, P)
        bT, kT_c = view(6144, 4, P), view(6656, 4, P)
        Nl = [view(7168, CH, P), view(8192, CH, P)]
        qT, kT = view(0, 6, S), view(1536, 6, S)
        prob = [view(3072, 768), view(3840, 768)]
        probT = [view(4608, 6, P), view(5376, 6, P)]
        ws = view(6144, AG, P)
        wsT = view(6656, AG, P)
        yb = view(7168, NT, 256)
        vn = view(7680, W)
        yaT, ybT, ycT = view(0, 4, S), view(1024, 2, S), view(1536, 4, S)
        merged = view(2560, NT, D)
        mergedT = view(4608, KC, S)
        gate = [view(6656, W), view(7168, W)]
        hid = [view(2048, W), view(2560, W)]
        hidT = [view(3072, 4, P), view(3584, 4, P)]

        ss, rn = small[:, 0:2], small[:, 2:4]
        kn = small[:, 4:20].rearrange("p (t h) -> p t h", t=NT)
        bonus = small[:, 20:36].rearrange("p (t h) -> p t h", t=NT)
        F = small[:, 36:40]
        gmu = small[:, 40:48]
        gvar = small[:, 48:56]
        nmax = small[:, 56:58]
        den = small[:, 58:60]
        bst, bag = small[:, 60:66], small[:, 66:68]
        lrs = small[:, 68:69]
        combine = small[:, 72:104].rearrange("p (t e) -> p t e", t=NT)
        rt = small[:, 104:400]

        VG, VMU, VFFN, VBS = 0, 8, 40, 48
        MU, LNW, LNB, KK_, KA_, RK_, GLG, GLB = (0, 1, 2), 0, 1, 3, 4, 5, 6, 7

        bank_full = [sem(f"bank_full{b}") for b in range(8)]
        bank_read = [sem(f"bank_read{b}") for b in range(8)]
        landed = [sem(f"landed{r}") for r in range(RING)]
        block_used = sem("block_used")
        const_in = sem("const_in")
        pool_in = sem("pool_in")
        rows_in = sem("rows_in")
        bc_in = sem("bc_in")
        late_in = sem("late_in")
        rw_in = sem("rw_in")
        ws_in = sem("ws_in")
        fin_in = sem("fin_in")
        out_done = sem("out_done")
        v_step = sem("v_step")
        a_step = sem("a_step")
        vec_ready = sem("vec_ready")
        ss_ready = sem("ss_ready")
        rms_ready = sem("rms_ready")
        hnat_ready = sem("hnat_ready")
        hT_v = sem("hT_v")
        hT_a = sem("hT_a")
        mix_ready = sem("mix_ready")
        lora_ready = sem("lora_ready")
        zs_ready = sem("zs_ready")
        rkv_ready = sem("rkv_ready")
        rest_ready = sem("rest_ready")
        mixed = sem("mixed")
        ksq_ready = sem("ksq_ready")
        knorm_ready = sem("knorm_ready")
        exps_ready = sem("exps_ready")
        exps_used = sem("exps_used")
        f_ready = sem("f_ready")
        f_exp = sem("f_exp")
        tilde_ready = sem("tilde_ready")
        crT_ready = sem("crT_ready")
        score_ready = sem("score_ready")
        n_ready = sem("n_ready")
        xt_ready = sem("xt_ready")
        y_ready = sem("y_ready")
        r_ready = sem("r_ready")
        sa_ready = sem("sa_ready")
        state_ready = sem("state_ready")
        gvar_ready = sem("gvar_ready")
        gstd_ready = sem("gstd_ready")
        rot_ready = sem("rot_ready")
        ang_ready = sem("ang_ready")
        sin_ready = sem("sin_ready")
        qkT_ready = sem("qkT_ready")
        p_ready = sem("p_ready")
        e_ready = sem("e_ready")
        pT_ready = sem("pT_ready")
        ln_ready = sem("ln_ready")
        lsd_ready = sem("lsd_ready")
        vn_ready = sem("vn_ready")
        ya_ready = sem("ya_ready")
        yb_ready = sem("yb_ready")
        yc_ready = sem("yc_ready")
        yT_ready = sem("yT_ready")
        gate_ready = sem("gate_ready")
        gate_used = sem("gate_used")
        merged_ready = sem("merged_ready")
        mT_ready = sem("mT_ready")
        logit_ready = sem("logit_ready")
        rexp_ready = sem("rexp_ready")
        silu_ready = sem("silu_ready")
        hid_ready = sem("hid_ready")
        hidT_ready = sem("hidT_ready")
        moe_a = sem("moe_a")
        layer_done = sem("layer_done")
        c_done = sem("c_done")
        gains_used = sem("gains_used")
        fin_done = sem("fin_done")

        A_BANKS, V_BANKS = (0, 1, 2, 3), (4, 5, 6, 7)
        assert set(A_BANKS) | set(V_BANKS) == set(range(8))

        block = ctx.enter_context(nc.Block())

        @block.sync
        def _(sp):
            sp.dma_start(x[:], a["x"].rearrange("b (t p) d -> p (b t) d", p=P)).then_inc(const_in, 16)
            sp.dma_start(tab[:], a["table"]).then_inc(const_in, 16)

            def load(layer, n):
                g = layer * PER_LAYER + n
                slot = g % RING
                if g >= RING:
                    sp.wait_ge(block_used, g - RING + 1)
                kind, *arg = BLOCKS[n]
                r = ring[:, slot, :]
                if kind == "proj":
                    c0, n_ = arg
                    pairs = [(r[:, 0:KC * n_].rearrange("p (c n) -> p c n", c=KC),
                              a["w_in"][layer].rearrange("(c p) n -> p c n", p=P)[:, :, c0:c0 + n_])]
                elif kind == "lora1":
                    v = r[:, 0:KC * 288].rearrange("p (c n) -> p c n", c=KC)
                    pairs, at = [], 0
                    for name, n_ in (("rwkv_w1", 64), ("rwkv_a1", 64), ("rwkv_g1", 128), ("rwkv_v1", 32)):
                        src = a[name][0 if name == "rwkv_v1" else layer]
                        pairs.append((v[:, :, at:at + n_], src.rearrange("(c p) n -> p c n", p=P)))
                        at += n_
                elif kind == "lora2":
                    pairs = []
                    for i, (name, n_) in enumerate((("rwkv_w2", 64), ("rwkv_a2", 64), ("rwkv_g2", 128),
                                                    ("rwkv_v2", 32))):
                        src = a[name][0 if name == "rwkv_v2" else layer]
                        pairs.append((r[0:n_, i * W:(i + 1) * W], src))
                elif kind == "branch":
                    name, c = (("w_branch_a", 4), ("w_branch_b", 2), ("w_branch_c", 4))[arg[0]]
                    c0 = arg[1] * W
                    pairs = [(r[:, 0:c * W].rearrange("p (c n) -> p c n", c=c),
                              a[name][layer].rearrange("(c p) n -> p c n", p=P)[:, :, c0:c0 + W])]
                elif kind == "gate":
                    c0 = arg[0] * W
                    pairs = [(r.rearrange("p (c n) -> p c n", c=KC),
                              a["w_gate"][layer].rearrange("(c p) n -> p c n", p=P)[:, :, c0:c0 + W])]
                else:
                    c0 = arg[0] * W
                    pairs = [(r.rearrange("p (c n) -> p c n", c=KC),
                              a["w_out"][layer].rearrange("(c p) n -> p c n", p=P)[:, :, c0:c0 + W])]
                for dst, src in pairs:
                    sp.dma_start(dst, src).then_inc(landed[slot], 16)

            for layer in range(LAYERS):
                for n in range(NB):
                    load(layer, n)
                g0 = layer * PER_LAYER + NB
                with sp.Fori(0, NE) as e:
                    for k, name in enumerate(("expert_w_gate", "expert_w_up", "expert_w_down")):
                        slot = (g0 + k) % RING
                        sp.wait_ge(block_used, e * 3 + (g0 + k - RING + 1))
                        src = a[name][layer][bass.ds(e, 1)]
                        if k < 2:
                            src = src.rearrange("e (c p) n -> p (e c) n", p=P)
                            dst = ring[:, slot, :].rearrange("p (c n) -> p c n", c=KC)
                        else:
                            src = src.rearrange("e (c p) n -> p (e c) n", p=P)
                            dst = ring[:, slot, :].rearrange("p (c n) -> p c n", c=FF // P)
                        sp.dma_start(dst, src).then_inc(landed[slot], 16)
            sp.wait_ge(fin_done, 1)
            sp.dma_start(a["out"].rearrange("b (t p) d -> p (b t) d", p=P), h_nat).then_inc(out_done, 16)
            sp.wait_ge(out_done, 16)

        @block.gpsimd
        def _(pool):
            pool.dma_start(sel[:], a["select"].rearrange("k (r p) -> k r p", p=P)).then_inc(pool_in, 16)
            pool.dma_start(pos_i[:], a["positions"].rearrange("a (t p) -> p (a t)", p=P),
                           allow_slow_non_contiguous=True).then_inc(pool_in, 16)

            def row_broadcast(slot, src, signal):
                pool.dma_start(bc[:, slot, :], src.partition_broadcast(P)).then_inc(signal, 16)

            halves = 0
            for layer in range(LAYERS):
                if layer:
                    pool.wait_ge(gains_used, layer)
                rows = [(0, 8, a["norm_mix_g"][layer].rearrange("(r p) -> r p", p=P)),
                        (8, 24, a["rwkv_mu_wag"][layer].rearrange("m (r p) -> (m r) p", p=P)),
                        (32, 8, a["rwkv_mu_v"][0].rearrange("(r p) -> r p", p=P)),
                        (40, 8, a["norm_ffn_g"][layer].rearrange("(r p) -> r p", p=P)),
                        (48, 4, a["gmlp_bs"][layer])]
                for r0, n, src in rows:
                    pool.dma_start(vec_rows[r0:r0 + n, :], src).then_inc(rows_in, 16)
                for r0, n, src in ((0, 6, a["b_gate"][layer].rearrange("(r n) -> r n", n=W)),
                                   (6, 1, a["rwkv_w0"][layer:layer + 1]),
                                   (7, 1, a["rwkv_a0"][layer:layer + 1]),
                                   (8, 1, a["rwkv_v0"][0:1])):
                    pool.dma_start(bias_rows[r0:r0 + n, :], src).then_inc(rows_in, 16)
                pool.dma_start(bias_rows[9:10, 0:4], a["router_group_b"][layer:layer + 1]).then_inc(rows_in, 16)
                pool.dma_start(bias_rows[9:10, 4:20], a["router_expert_b"][layer:layer + 1]).then_inc(rows_in, 16)
                for i in range(3):
                    row_broadcast(MU[i], a["rwkv_mu_rkv"][layer, i], bc_in)
                row_broadcast(KK_, a["rwkv_k_k"][layer], bc_in)
                row_broadcast(KA_, a["rwkv_k_a"][layer], bc_in)
                row_broadcast(RK_, a["rwkv_r_k"][layer].rearrange("h d -> (h d)"), bc_in)
                row_broadcast(GLG, a["gmlp_ln_g"][layer], bc_in)
                row_broadcast(GLB, a["gmlp_ln_b"][layer], bc_in)
                pool.dma_start(rw[:, :, 0:4], a["router_group_w"][layer].rearrange("(c p) n -> p c n", p=P))\
                    .then_inc(rw_in, 16)
                pool.dma_start(rw[:, :, 4:20], a["router_expert_w"][layer].rearrange("(c p) n -> p c n", p=P))\
                    .then_inc(rw_in, 16)
                pool.wait_ge(c_done, layer + 1)
                row_broadcast(LNW, a["rwkv_ln_w"][layer], late_in)
                row_broadcast(LNB, a["rwkv_ln_b"][layer], late_in)
                if layer == 0:
                    pool.wait_ge(const_in, 32)
                for c in range(NT):
                    pool.wait_ge(score_ready, layer * NT + c + 1)
                    for k in range(LEVELS):
                        if k == 2:
                            pool.wait_ge(xt_ready, (layer * NT + c) * 2 * LEVELS + 2)
                        elif k > 2:
                            pool.wait_ge(y_ready, ((layer * NT + c) * (LEVELS - 1) + k - 3) * 2 + 2)
                        at, n = CONST_AT[f"level{k}"]
                        m = tab[:, at:at + P].unsqueeze(1).to_broadcast([P, CH, P])
                        pool.tensor_tensor(Nl[k % 2], SCb[:, :, 0, :], m, ALU.mult).then_inc(n_ready, 1)
                pool.wait_ge(yc_ready, layer + 1)
                pool.dma_start(ws, a["gmlp_ws"][layer].rearrange("g t s -> t g s")).then_inc(ws_in, 16)
                if layer == LAYERS - 1:
                    pool.wait_ge(gains_used, LAYERS)
                    pool.dma_start(bc[:, 0:2, :].rearrange("p a n -> p (a n)"),
                                   a["final_norm_g"].partition_broadcast(P)).then_inc(fin_in, 16)

        @block.tensor
        def _(pe):
            jobs = [0] * 8
            used = [0]

            def open_bank(b):
                if jobs[b]:
                    pe.wait_ge(bank_read[b], jobs[b])

            def close_bank(b, mm):
                mm.then_inc(bank_full[b], 1)
                jobs[b] += 1

            def block_in(layer, n):
                slot, value = landed_after(layer, n)
                pe.wait_ge(landed[slot], value)
                return ring[:, slot, :]

            def release():
                pe.drain().then_inc(block_used, 1)

            def transposes(bank, srcs):
                open_bank(bank)
                for i, s in enumerate(srcs):
                    n = s.shape[0]
                    mm = pe.transpose(PS[:, bank, i * P:i * P + n], s, ident[0:n, 0:n])
                close_bank(bank, mm)

            def norm_transposes(n):
                pe.wait_ge(hnat_ready, n)
                for bank in (2, 4, 3, 5):
                    c = 2 * (2, 3, 4, 5).index(bank)
                    transposes(bank, [h_nat[:, t, (c + i) * P:(c + i + 1) * P] for i in range(2) for t in range(NT)])

            dense = [0]

            def dense_group(blk, n, t, bias=None, bank=None):
                b = dense[0] % 2 if bank is None else bank
                dense[0] += bank is None
                open_bank(b)
                wv = blk[:, 0:KC * n].rearrange("p (c n) -> p c n", c=KC)
                src = hT if bank is None else mergedT
                for c in range(KC):
                    mm = pe.matmul(PS[:, b, 0:n], src[:, c, t * P:(t + 1) * P], wv[:, c, :],
                                   start=(c == 0), stop=(c == KC - 1 and bias is None))
                if bias is not None:
                    mm = pe.matmul(PS[:, b, 0:n], sel[0:9, bias, :], bias_rows[0:9, 0:n], start=False, stop=True)
                close_bank(b, mm)

            pe.wait_ge(const_in, 32)
            pe.wait_ge(pool_in, 32)
            for layer in range(LAYERS):
                pe.wait_ge(rows_in, 11 * 16 * (layer + 1))
                transposes(4, [vec_rows])
                norm_transposes(2 * layer + 1)
                pe.wait_ge(hT_v, 2 * layer + 1)
                pe.wait_ge(hT_a, 2 * layer + 1)
                for n in range(3):
                    blk = block_in(layer, n)
                    for t in range(NT):
                        dense_group(blk, W, t)
                    release()
                blk = block_in(layer, 3)
                l1 = blk[:, 0:KC * 288].rearrange("p (c n) -> p c n", c=KC)
                nmix = 3 + layer
                mix0 = 3 * layer
                for m, (at, n) in enumerate(((0, 64), (64, 64), (128, 128), (256, 32))[:nmix]):
                    pe.wait_ge(mix_ready, mix0 + m + 1)
                    b = 2 + m % 2
                    open_bank(b)
                    for c in range(KC):
                        mm = pe.matmul(PS[0:n, b, 0:S], l1[:, c, at:at + n], mix[m % 2][:, c, :],
                                       start=(c == 0), stop=(c == KC - 1))
                    close_bank(b, mm)
                release()
                blk = block_in(layer, 4)
                for m, (n, bias) in enumerate(((64, 6), (64, 7), (128, None), (32, 8))[:nmix]):
                    pe.wait_ge(lora_ready, mix0 + m + 1)
                    for t in range(NT):
                        b = 2 + t
                        open_bank(b)
                        mm = pe.matmul(PS[:, b, :], loraT[m][0:n, t * P:(t + 1) * P], blk[0:n, m * W:(m + 1) * W],
                                       start=True, stop=bias is None)
                        if bias is not None:
                            mm = pe.matmul(PS[:, b, :], sel[0:9, bias, :], bias_rows[0:9, :], start=False, stop=True)
                        close_bank(b, mm)
                release()
                pe.wait_ge(rkv_ready, 6 * (layer + 1))
                for i, c0 in enumerate((R0, CK0, CV0)):
                    for t in (1, 0):
                        b = 4 + t
                        open_bank(b)
                        mm = pe.matmul(PS[:, b, :], const("shift"), proj[:, t, c0:c0 + W], start=True, stop=(t == 0))
                        if t:
                            mm = pe.matmul(PS[:, b, :], const("edge"), proj[:, 0, c0:c0 + W], start=False, stop=True)
                        close_bank(b, mm)
                pe.wait_ge(zs_ready, (6 + 8 * layer) if layer else 6)
                for t in range(NT):
                    for b, m in ((2, "decay_incl"), (3, "decay_prev")):
                        open_bank(b)
                        close_bank(b, pe.matmul(PS[:, b, :], const(m), lw[:, t, :], start=True, stop=True))
                    if t == 0:
                        for q in range(4):
                            if q == 0:
                                open_bank(6)
                            pe.matmul(PS[:, 6, q:q + 1], lw[:, 0, q * P:(q + 1) * P], const("after_mid"),
                                      start=True, stop=False)
                            mm = pe.matmul(PS[:, 6, q:q + 1], lw[:, 1, q * P:(q + 1) * P], const("before_mid"),
                                           start=False, stop=True)
                        close_bank(6, mm)
                for n in range(5, 12):
                    blk = block_in(layer, n)
                    for t in range(NT):
                        dense_group(blk, BLOCKS[n][2], t)
                    release()
                for c in range(NT):
                    g = layer * NT + c
                    pe.wait_ge(tilde_ready, g + 1)
                    for b, src in ((4, kk), (5, proj[:, :, R0:R0 + W]), (6, aa), (7, proj[:, :, CK0:CK0 + W])):
                        transposes(b, [src[:, c, q * P:(q + 1) * P] for q in range(4)])
                    pe.wait_ge(crT_ready, g + 1)
                    for half in range(2):
                        for b, lhs, i in ((4, bT, 0), (5, bT, 1), (6, kT_c, 0), (7, kT_c, 1)):
                            rows = slice(64 * i, 64 * i + 64)
                            open_bank(b)
                            for j in range(2):
                                q = 2 * half + j
                                mm = pe.matmul(PS[:, b, 256 * j:256 * j + 256], lhs[rows, q, :],
                                               krT[rows, q, :, :].rearrange("p a t -> p (a t)"),
                                               start=True, stop=True)
                            close_bank(b, mm)
                    for k in range(LEVELS):
                        n = g * LEVELS + k
                        N = Nl[k % 2]
                        pe.wait_ge(n_ready, n + 1)
                        for h in range(2):
                            if k:
                                pe.wait_ge(xt_ready, g * 2 * LEVELS + 2 * (k - 1) + h + 1)
                            b = 2 + h if k else 4 + 2 * h
                            open_bank(b)
                            for i in range(4):
                                hh = 4 * h + i
                                rhs = X[:, hh, :] if k else ident
                                mm = pe.matmul(PS[:, b, i * P:(i + 1) * P], N[:, hh, :], rhs, start=True, stop=True)
                            close_bank(b, mm)
                        if k == 0:
                            continue
                        for h in range(2):
                            pe.wait_ge(y_ready, (g * (LEVELS - 1) + k - 1) * 2 + h + 1)
                            for b, which in ((4 + 2 * h, "xt"), (5 + 2 * h, "x")):
                                if which == "x" and k == LEVELS - 1:
                                    continue
                                open_bank(b)
                                for i in range(4):
                                    hh = 4 * h + i
                                    l, r = (Yl, XT) if which == "xt" else (XT, Yl)
                                    mm = pe.matmul(PS[:, b, i * P:(i + 1) * P], l[:, hh, :], r[:, hh, :],
                                                   start=True, stop=True)
                                close_bank(b, mm)
                    if c:
                        pe.wait_ge(state_ready, layer + 1)
                    open_bank(2)
                    for hh in range(CH):
                        q = hh // 2
                        o = PS[:, 2, hh * HD:(hh + 1) * HD]
                        vh = proj[:, c, CV0 + hh * HD:CV0 + (hh + 1) * HD]
                        mm = pe.matmul(o, SCk[:, hh, 0, :], vh, start=True, stop=(c == 0))
                        if c:
                            mm = pe.matmul(o, krT[:, q, 0, :], state[:, q, 64 * (hh % 2):64 * (hh % 2) + 64],
                                           start=False, stop=True)
                    close_bank(2, mm)
                    pe.wait_ge(xt_ready, (g + 1) * 2 * LEVELS)
                    pe.wait_ge(r_ready, g + 1)
                    open_bank(3)
                    for hh in range(CH):
                        mm = pe.matmul(PS[:, 3, hh * HD:(hh + 1) * HD], XT[:, hh, :], tmp[:, 0, hh * HD:(hh + 1) * HD],
                                       start=True, stop=True)
                    close_bank(3, mm)
                    pe.wait_ge(sa_ready, g + 1)
                    open_bank(4)
                    for hh in range(CH):
                        q = hh // 2
                        o = PS[:, 4, hh * HD:(hh + 1) * HD]
                        pe.matmul(o, SCb[:, hh, 1, :], tmp[:, 1, hh * HD:(hh + 1) * HD], start=True, stop=False)
                        mm = pe.matmul(o, SCk[:, hh, 1, :], proj[:, c, CV0 + hh * HD:CV0 + (hh + 1) * HD],
                                       start=False, stop=(c == 0))
                        if c:
                            mm = pe.matmul(o, krT[:, q, 1, :], state[:, q, 64 * (hh % 2):64 * (hh % 2) + 64],
                                           start=False, stop=True)
                    close_bank(4, mm)
                    if c == 0:
                        open_bank(5)
                        for q in range(4):
                            cols = slice(q * P, (q + 1) * P)
                            pe.matmul(PS[:, 5, cols], aa[:, 0, cols], tmp[:, 1, cols], start=True, stop=False)
                            mm = pe.matmul(PS[:, 5, cols], proj[:, 0, CK0 + q * P:CK0 + (q + 1) * P],
                                           proj[:, 0, CV0 + q * P:CV0 + (q + 1) * P], start=False, stop=True)
                        close_bank(5, mm)
                pe.wait_ge(rot_ready, layer + 1)
                pe.wait_ge(yc_ready, layer + 1)
                for i, c0 in enumerate((Q0, K0)):
                    for q in range(3):
                        transposes(2 + (3 * i + q) % 2, [proj[:, t, c0 + (2 * q + j) * P:c0 + (2 * q + j + 1) * P]
                                                         for j in range(2) for t in range(NT)])
                pe.wait_ge(qkT_ready, 6 * (layer + 1))
                for job in range(NT * BHG):
                    head, t = job // NT, job % NT
                    n = (t + 1) * P
                    g = layer * NT * BHG + job
                    for gr in range(3):
                        hh = gr * BHG + head
                        rows, q = slice(64 * (hh % 2), 64 * (hh % 2) + 64), hh // 2
                        b = 4 + gr // 2
                        if gr != 1:
                            open_bank(b)
                        at = (gr % 2) * n
                        mm = pe.matmul(PS[:, b, at:at + n], qT[rows, q, t * P:(t + 1) * P], kT[rows, q, 0:n],
                                       start=True, stop=True)
                        if gr:
                            close_bank(b, mm)
                    pe.wait_ge(e_ready, g + 1)
                    keys = [(gr, kt) for gr in range(3) for kt in range(t + 1)]
                    transposes(2, [prob[g % 2][:, i * P:(i + 1) * P] for i in range(min(4, len(keys)))])
                    if len(keys) > 4:
                        transposes(3, [prob[g % 2][:, i * P:(i + 1) * P] for i in range(4, len(keys))])
                    pe.wait_ge(pT_ready, g + 1)
                    b = 6 + g % 2
                    open_bank(b)
                    for i, (gr, kt) in enumerate(keys):
                        hh = gr * BHG + head
                        mm = pe.matmul(PS[:, b, 0:HD], probT[g % 2][:, i, :],
                                       proj[:, kt, VB0 + hh * HD:VB0 + (hh + 1) * HD],
                                       start=(i == 0), stop=(i == len(keys) - 1))
                    close_bank(b, mm)
                pe.wait_ge(ws_in, 16 * (layer + 1))
                transposes(4, [ws[:, g, :] for g in range(AG)])
                for t in range(NT):
                    pe.wait_ge(vn_ready, layer * NT + t + 1)
                    open_bank(5)
                    for g in range(AG):
                        mm = pe.matmul(PS[:, 5, g * P:(g + 1) * P], wsT[:, g, :], vn[:, g * P:(g + 1) * P],
                                       start=True, stop=True)
                    close_bank(5, mm)
                pe.wait_ge(ya_ready, layer + 1)
                pe.wait_ge(yb_ready, layer + 1)
                for i, (src, n) in enumerate(((proj[:, :, U0:U0 + W], 4), (yb, 2), (kk, 4))):
                    for q in range(n // 2):
                        transposes(2 + q % 2, [src[:, t, (2 * q + j) * P:(2 * q + j + 1) * P]
                                               for j in range(2) for t in range(NT)])
                pe.wait_ge(yT_ready, 5 * (layer + 1))
                for br, (yT, n) in enumerate(((yaT, 4), (ybT, 2), (ycT, 4))):
                    for half in range(2):
                        blk = block_in(layer, 12 + 4 * br + 2 * half)
                        for t in range(NT):
                            dense_group(blk, W, t, bias=2 * br + half)
                        release()
                        bblk = block_in(layer, 13 + 4 * br + 2 * half)
                        bw = bblk[:, 0:n * W].rearrange("p (c n) -> p c n", c=n)
                        for t in range(NT):
                            open_bank(4 + t)
                            for c in range(n):
                                mm = pe.matmul(PS[:, 4 + t, :], yT[:, c, t * P:(t + 1) * P], bw[:, c, :],
                                               start=(c == 0), stop=(c == n - 1))
                            close_bank(4 + t, mm)
                        release()
                pe.wait_ge(merged_ready, layer + 1)
                for q in range(4):
                    transposes(2 + q % 2, [merged[:, t, (2 * q + j) * P:(2 * q + j + 1) * P]
                                           for j in range(2) for t in range(NT)])
                pe.wait_ge(mT_ready, 4 * (layer + 1))
                for half in range(2):
                    blk = block_in(layer, 24 + half)
                    for t in range(NT):
                        dense_group(blk, W, t, bank=4 + t)
                    release()
                norm_transposes(2 * layer + 2)
                pe.wait_ge(hT_v, 2 * layer + 2)
                pe.wait_ge(hT_a, 2 * layer + 2)
                pe.wait_ge(rw_in, 32 * (layer + 1))
                for t in range(NT):
                    b = 6 + t
                    open_bank(b)
                    for c in range(KC):
                        pe.matmul(PS[:, b, 0:20], hT[:, c, t * P:(t + 1) * P], rw[:, c, :], start=(c == 0), stop=False)
                    mm = pe.matmul(PS[:, b, 0:20], sel[0:10, 9, :],
                                   bias_rows[0:10, 0:20], start=False, stop=True)
                    close_bank(b, mm)
                acc = {(0, 0): 2, (0, 1): 3, (1, 0): 6, (1, 1): 7}
                for (t, half), b in acc.items():
                    open_bank(b)
                    pe.matmul(PS[:, b, :], ident, x[:, t, half * W:(half + 1) * W], start=True, stop=False)
                g0 = layer * PER_LAYER + NB
                slots = [(g0 + k) % RING for k in range(3)]
                base = [landed_after(layer, NB + k)[1] for k in range(3)]
                full0, full4, full1 = jobs[0], jobs[4], jobs[1]

                def hidden(e, t, k, bank, job0):
                    if t == 0:
                        pe.wait_ge(landed[slots[k]], e * 16 + base[k])
                    pe.wait_ge(bank_read[bank], e * 2 + (job0 + t))
                    wv = ring[:, slots[k], :].rearrange("p (c n) -> p c n", c=KC)
                    for c in range(KC):
                        mm = pe.matmul(PS[:, bank, :], hT[:, c, t * P:(t + 1) * P], wv[:, c, :],
                                       start=(c == 0), stop=(c == KC - 1))
                    mm.then_inc(bank_full[bank], 1)
                    if t == 1:
                        release()

                def down(e, t, last=False):
                    n = layer * 2 * NE + t
                    pe.wait_ge(hid_ready, e * 2 + (n + 1))
                    pe.wait_ge(bank_read[1], e * 2 + (full1 + t))
                    for c in range(4):
                        mm = pe.transpose(PS[:, 1, c * P:(c + 1) * P], hid[t][:, c * P:(c + 1) * P], ident)
                    mm.then_inc(bank_full[1], 1)
                    pe.wait_ge(hidT_ready, e * 2 + (n + 1))
                    if t == 0:
                        pe.wait_ge(landed[slots[2]], e * 16 + base[2])
                    wv = ring[:, slots[2], :].rearrange("p (c n) -> p c n", c=4)
                    for half in range(2):
                        b = acc[t, half]
                        for c in range(4):
                            mm = pe.matmul(PS[:, b, :], hidT[t][:, c, :], wv[:, c, half * W:(half + 1) * W],
                                           start=False, stop=last and c == 3)
                        if last:
                            close_bank(b, mm)
                    if t == 1:
                        release()

                hidden(0, 0, 0, 0, full0)
                hidden(0, 0, 1, 4, full4)
                with pe.Fori(0, NE - 1) as e:
                    hidden(e, 1, 0, 0, full0)
                    hidden(e, 1, 1, 4, full4)
                    down(e, 0)
                    hidden(e + 1, 0, 0, 0, full0)
                    hidden(e + 1, 0, 1, 4, full4)
                    down(e, 1)
                hidden(NE - 1, 1, 0, 0, full0)
                hidden(NE - 1, 1, 1, 4, full4)
                down(NE - 1, 0, last=True)
                down(NE - 1, 1, last=True)
                for b in (0, 1, 4):
                    jobs[b] += 2 * NE

        @block.scalar
        def _(act):
            taken = [0] * 8
            steps = [0]

            def take(b):
                act.wait_ge(bank_full[b], taken[b] + 1)

            def give(b):
                act.sem_inc(bank_read[b], 1)
                taken[b] += 1

            def step(ins):
                steps[0] += 1
                ins.then_inc(a_step, 1)
                act.wait_ge(a_step, steps[0])

            def evac(b, out, func=ACT.Copy, signal=None, n=W, rows=P, scale=1.0, pat=None):
                take(b)
                src = PS[0:rows, b, 0:n]
                step(act.activation(out, src if pat is None else src.rearrange(*pat[0], **pat[1]), func, scale=scale))
                give(b)
                if signal is not None:
                    act.sem_inc(signal, 1)

            def norm(n, col):
                act.wait_ge(ss_ready, n)
                step(act.activation(rn, ss, ACT.Sqrt, bias=const("eps_rms"), scale=1.0 / D))
                act.sem_inc(rms_ready, 1)
                if n > 2 * LAYERS:
                    return
                if col == VG:
                    act.wait_ge(vec_ready, (n + 1) // 2)
                for b in (2, 3):
                    take(b)
                    for i in range(2):
                        c = 2 * (b - 2) + i
                        step(act.activation(hT[:, c, :], PS[:, b, i * S:(i + 1) * S], ACT.Copy,
                                            scale=vec[:, col + c:col + c + 1]))
                    give(b)
                act.sem_inc(hT_a, 1)

            act.wait_ge(const_in, 32)
            act.wait_ge(ang_ready, 1)
            step(act.activation(angle[:, 4, :], angle[:, 2, :], ACT.Sin))
            step(act.activation(angle[:, 5, :], angle[:, 3, :], ACT.Sin))
            act.sem_inc(sin_ready, 1)
            dense = [0]

            def dense_evac(out, func=ACT.Copy, signal=None, n=W):
                b = dense[0] % 2
                dense[0] += 1
                evac(b, out, func, signal, n)

            for layer in range(LAYERS):
                norm(2 * layer + 1, VG)
                for c0 in (R0, CK0, CV0):
                    for t in range(NT):
                        dense_evac(proj[:, t, c0:c0 + W], signal=rkv_ready)
                nmix = 3 + layer
                for m, (n, func) in enumerate(((64, ACT.Tanh), (64, ACT.Copy), (128, ACT.Sigmoid),
                                               (32, ACT.Copy))[:nmix]):
                    evac(2 + m % 2, loraT[m][0:n, :], func, lora_ready, n=S, rows=n)
                for m, (dst, func) in enumerate(((lw, ACT.Sigmoid), (aa, ACT.Sigmoid), (gg, ACT.Copy),
                                                 (tmp, ACT.Sigmoid))[:nmix]):
                    for t in range(NT):
                        evac(2 + t, dst[:, t, :], func, zs_ready)
                act.wait_ge(ksq_ready, layer + 1)
                step(act.activation(kn, kn, ACT.Sqrt))
                act.sem_inc(knorm_ready, 1)

                def exps(t):
                    g = layer * NT + t
                    if g:
                        act.wait_ge(exps_used, g)
                    if t == 0:
                        act.wait_ge(c_done, layer + 1)
                    take(2)
                    step(act.activation(tmp[:, 0, :], PS[:, 2, :], ACT.Exp))
                    step(act.activation(tmp[:, 1, :], PS[:, 2, :], ACT.Exp, scale=-1.0))
                    give(2)
                    take(3)
                    step(act.activation(tmp[:, 2, :], PS[:, 3, :], ACT.Exp))
                    give(3)
                    act.sem_inc(exps_ready, 1)

                exps(0)
                for n in range(5, 12):
                    c0, w_ = BLOCKS[n][1:]
                    for t in range(NT):
                        dense_evac(proj[:, t, c0:c0 + w_], ACT.Gelu_apprx_tanh if c0 < Q0 else ACT.Copy,
                                   rest_ready, n=w_)
                        if (n, t) == (5, 0):
                            exps(1)
                            act.wait_ge(f_ready, layer + 1)
                            step(act.activation(F, F, ACT.Exp))
                            act.sem_inc(f_exp, 1)
                for c in range(NT):
                    g = layer * NT + c
                    for k in range(1, LEVELS):
                        for h in range(2):
                            evac(2 + h, Yl[:, 4 * h:4 * h + 4, :], signal=y_ready,
                                 pat=(("p (h t) -> p h t",), dict(h=4)))
                    act.wait_ge(exps_used, layer * NT + 2)
                    evac(2, tmp[:, 0, :], signal=r_ready)
                    evac(3, tmp[:, 1, :], signal=sa_ready, scale=-1.0)
                    act.wait_ge(gvar_ready, g + 1)
                    step(act.activation(gvar, gvar, ACT.Sqrt, bias=const("eps_gn"), scale=1.0 / HD))
                    act.sem_inc(gstd_ready, 1)
                for i, dst in enumerate((qT, kT)):
                    for q in range(3):
                        evac(2 + (3 * i + q) % 2, dst[:, 2 * q:2 * q + 2, :], signal=qkT_ready,
                             pat=(("p (c t) -> p c t",), dict(c=2)))
                for job in range(NT * BHG):
                    t = job % NT
                    g = layer * NT * BHG + job
                    n = 3 * (t + 1) * P
                    act.wait_ge(p_ready, g + 1)
                    step(act.activation(prob[g % 2][:, 0:n], prob[g % 2][:, 0:n], ACT.Exp,
                                        bias=nmax[:, g % 2:g % 2 + 1], accum_out=den[:, g % 2:g % 2 + 1]))
                    act.sem_inc(e_ready, 1)
                    nk = 3 * (t + 1)
                    evac(2, probT[g % 2][:, 0:min(4, nk), :], n=min(4, nk) * P,
                         pat=(("p (c t) -> p c t",), dict(t=P)))
                    if nk > 4:
                        evac(3, probT[g % 2][:, 4:nk, :], n=(nk - 4) * P, pat=(("p (c t) -> p c t",), dict(t=P)))
                    act.sem_inc(pT_ready, 1)
                for t in range(NT):
                    act.wait_ge(ln_ready, layer * NT + t + 1)
                    step(act.activation(lrs, bag[:, 1:2], ACT.Sqrt, bias=const("eps_ln")))
                    act.sem_inc(lsd_ready, 1)
                for dst, n in ((yaT, 4), (ybT, 2), (ycT, 4)):
                    for q in range(n // 2):
                        evac(2 + q % 2, dst[:, 2 * q:2 * q + 2, :], signal=yT_ready,
                             pat=(("p (c t) -> p c t",), dict(c=2)))
                for i in range(12):
                    g = 12 * layer + i
                    if g >= 2:
                        act.wait_ge(gate_used, g - 1)
                    dense_evac(gate[i % 2], ACT.Sigmoid, gate_ready)
                for q in range(4):
                    evac(2 + q % 2, mergedT[:, 2 * q:2 * q + 2, :], signal=mT_ready,
                         pat=(("p (c t) -> p c t",), dict(c=2)))
                norm(2 * layer + 2, VFFN)
                act.wait_ge(logit_ready, layer + 1)
                step(act.activation(rt[:, 40:50], rt[:, 40:50], ACT.Exp))
                act.sem_inc(rexp_ready, 1)
                f0, f1 = taken[0], taken[1]
                u0 = layer * 2 * NE

                def silu(e, t):
                    act.wait_ge(bank_full[0], e * 2 + (f0 + t + 1))
                    if not (isinstance(e, int) and e == 0):
                        act.wait_ge(bank_full[1], e * 2 + (f1 + t - 1))
                    act.activation(hid[t], PS[:, 0, :], ACT.Silu).then_inc(silu_ready, 1)
                    act.wait_ge(silu_ready, e * 2 + (u0 + t + 1))
                    act.sem_inc(bank_read[0], 1)

                def hidden_T(e, t):
                    act.wait_ge(bank_full[1], e * 2 + (f1 + t + 1))
                    act.activation(hidT[t], PS[:, 1, :].rearrange("p (c t) -> p c t", c=4), ACT.Copy)\
                        .then_inc(hidT_ready, 1)
                    act.wait_ge(hidT_ready, e * 2 + (u0 + t + 1))
                    act.sem_inc(bank_read[1], 1)

                silu(0, 0)
                silu(0, 1)
                hidden_T(0, 0)
                with act.Fori(1, NE) as e:
                    silu(e, 0)
                    hidden_T(e - 1, 1)
                    silu(e, 1)
                    hidden_T(e, 0)
                hidden_T(NE - 1, 1)
                taken[0] += 2 * NE
                taken[1] += 2 * NE
                for half in range(2):
                    evac(2 + half, x[:, 0, half * W:(half + 1) * W])
                act.sem_inc(moe_a, 1)
            norm(2 * LAYERS + 1, None)

        @block.vector
        def _(dve):
            taken = [0] * 8
            steps = [0]

            def take(b):
                dve.wait_ge(bank_full[b], taken[b] + 1)

            def give(b):
                dve.sem_inc(bank_read[b], 1)
                taken[b] += 1

            def step(ins):
                steps[0] += 1
                ins.then_inc(v_step, 1)
                dve.wait_ge(v_step, steps[0])

            def tt(out, i0, i1, op):
                step(dve.tensor_tensor(out, i0, i1, op))

            def stt(out, i0, s, i1, op0, op1):
                step(dve.scalar_tensor_tensor(out=out, in0=i0, scalar=s, in1=i1, op0=op0, op1=op1))

            def ts(out, i0, s1, s2, op0, op1=None):
                if op1 is None:
                    step(dve.tensor_scalar(out, i0, s1, None, op0))
                else:
                    step(dve.tensor_scalar(out, i0, s1, s2, op0, op1))

            def heads(v):
                return v.rearrange("p (h d) -> p h d", d=HD)

            def per_head(v):
                return v.unsqueeze(2).to_broadcast([P, CH, HD])

            def norm(n, col):
                for t in range(NT):
                    step(dve.scalar_tensor_tensor(out=h_nat[:, t, :], in0=x[:, t, :], scalar=1.0, in1=x[:, t, :],
                                                  op0=ALU.mult, op1=ALU.mult, accum_out=ss[:, t:t + 1]))
                dve.sem_inc(ss_ready, 1)
                dve.wait_ge(rms_ready, n)
                step(dve.reciprocal(rn, rn))
                for t in range(NT):
                    ts(h_nat[:, t, :], x[:, t, :], rn[:, t:t + 1], None, ALU.mult)
                if col is None:
                    return
                dve.sem_inc(hnat_ready, 1)
                for b in (4, 5):
                    take(b)
                    for i in range(2):
                        c = 2 * (b - 2) + i
                        ts(hT[:, c, :], PS[:, b, i * S:(i + 1) * S], vec[:, col + c:col + c + 1], None, ALU.mult)
                    give(b)
                dve.sem_inc(hT_v, 1)

            dve.wait_ge(const_in, 32)
            dve.wait_ge(pool_in, 32)
            step(dve.memset(state[:], 0.0))
            step(dve.tensor_copy(small[:, 0:NT], pos_i[:]))
            tt(angle[:, 0, :].rearrange("p (t f) -> p t f", t=NT),
               small[:, 0:NT].unsqueeze(2).to_broadcast([P, NT, HALF]),
               const("freq").unsqueeze(1).to_broadcast([P, NT, HALF]), ALU.mult)
            for i, (turn, shift) in enumerate(((0.0, 0.0), (0.25, np.pi / 2))):
                n, r = angle[:, 1, :], angle[:, 2 + i, :]
                ts(n, angle[:, 0, :], 1.0 / (2 * np.pi), turn, ALU.mult, ALU.add)
                ts(n, n, ROUND, None, ALU.add)
                ts(n, n, -ROUND, None, ALU.add)
                stt(r, n, -TWO_PI[0], angle[:, 0, :], ALU.mult, ALU.add)
                for part in TWO_PI[1:]:
                    stt(r, n, -part, r, ALU.mult, ALU.add)
                ts(r, r, float(np.float32(shift)), float(np.float32(3.1415925)), ALU.add, ALU.min)
                ts(r, r, float(-np.float32(3.1415925)), None, ALU.max)
            dve.sem_inc(ang_ready, 1)

            for layer in range(LAYERS):
                take(4)
                step(dve.tensor_copy(vec[:], PS[:, 4, 0:52]))
                give(4)
                dve.sem_inc(vec_ready, 1)
                norm(2 * layer + 1, VG)
                dve.wait_ge(hT_a, 2 * layer + 1)
                step(dve.tensor_tensor(dhT[:, :, 1:S], hT[:, :, 0:S - 1], hT[:, :, 1:S], ALU.subtract))
                ts(dhT[:, :, 0:1], hT[:, :, 0:1], -1.0, None, ALU.mult)
                for m in range(3 + layer):
                    if m >= 2:
                        dve.wait_ge(lora_ready, 3 * layer + m - 1)
                    for c in range(KC):
                        col = VMU + 8 * m + c
                        stt(mix[m % 2][:, c, :], dhT[:, c, :], vec[:, col:col + 1], hT[:, c, :], ALU.mult, ALU.add)
                    dve.sem_inc(mix_ready, 1)
                dve.wait_ge(bc_in, 8 * 16 * (layer + 1))
                r_, k_, v_ = (proj[:, :, c:c + W] for c in (R0, CK0, CV0))
                dve.wait_ge(zs_ready, 14 if layer else 6)
                for i, t_ in enumerate((r_, k_, v_)):
                    for t in (1, 0):
                        take(4 + t)
                        tt(kk[:, t, :], PS[:, 4 + t, :], bc[:, MU[i], :], ALU.mult)
                        give(4 + t)
                        tt(t_[:, t, :], t_[:, t, :], kk[:, t, :], ALU.add)
                for t in range(NT):
                    if layer == 0:
                        step(dve.tensor_copy(v_first[:, t, :], v_[:, t, :]))
                    else:
                        tt(kk[:, t, :], v_first[:, t, :], v_[:, t, :], ALU.subtract)
                        tt(kk[:, t, :], kk[:, t, :], tmp[:, t, :], ALU.mult)
                        tt(v_[:, t, :], v_[:, t, :], kk[:, t, :], ALU.add)
                dve.sem_inc(c_done, 1)
                sq = view(0, W)
                for t in range(NT):
                    tt(kk[:, t, :], k_[:, t, :], bc[:, KK_, :], ALU.mult)
                    tt(sq, kk[:, t, :], kk[:, t, :], ALU.mult)
                    step(dve.tensor_reduce(kn[:, t, :], heads(sq), AX_X, ALU.add))
                dve.sem_inc(ksq_ready, 1)
                for t in range(NT):
                    stt(sq, aa[:, t, :], -1.0, bc[:, KA_, :], ALU.add, ALU.mult)
                    stt(k_[:, t, :], sq, 1.0, k_[:, t, :], ALU.add, ALU.mult)
                    tt(sq, r_[:, t, :], k_[:, t, :], ALU.mult)
                    tt(sq, sq, bc[:, RK_, :], ALU.mult)
                    step(dve.tensor_reduce(bonus[:, t, :], heads(sq), AX_X, ALU.add))
                dve.wait_ge(knorm_ready, layer + 1)
                ts(kn, kn, 1e-12, None, ALU.max)
                step(dve.reciprocal(kn, kn))
                take(6)
                step(dve.tensor_copy(F, PS[:, 6, 0:4]))
                give(6)
                dve.sem_inc(f_ready, 1)
                for t in range(NT):
                    tt(heads(kk[:, t, :]), heads(kk[:, t, :]), per_head(kn[:, t, :]), ALU.mult)
                    tt(aa[:, t, :], aa[:, t, :], kk[:, t, :], ALU.mult)
                    dve.wait_ge(exps_ready, layer * NT + t + 1)
                    tt(r_[:, t, :], r_[:, t, :], tmp[:, 0, :], ALU.mult)
                    tt(aa[:, t, :], aa[:, t, :], tmp[:, 1, :], ALU.mult)
                    tt(k_[:, t, :], k_[:, t, :], tmp[:, 1, :], ALU.mult)
                    tt(kk[:, t, :], kk[:, t, :], tmp[:, 2, :], ALU.mult)
                    dve.sem_inc(exps_used, 1)
                    dve.sem_inc(tilde_ready, 1)
                low2 = tab[:, CONST_AT["low_strict"][0]:CONST_AT["low_strict"][0] + 2 * P]
                low2 = low2.unsqueeze(1).to_broadcast([P, 2, 2 * P])
                idb = ident.unsqueeze(1).to_broadcast([P, 4, P])
                for c in range(NT):
                    g = layer * NT + c
                    for b, dst in ((4, krT[:, :, 0, :]), (5, krT[:, :, 1, :]), (6, bT), (7, kT_c)):
                        take(b)
                        step(dve.tensor_copy(dst, PS[:, b, :].rearrange("p (q t) -> p q t", q=4)))
                        give(b)
                    dve.sem_inc(crT_ready, 1)
                    for half in range(2):
                        for b, dst, i in ((4, SCb, 0), (5, SCb, 1), (6, SCk, 0), (7, SCk, 1)):
                            take(b)
                            tt(dst[:, 4 * half + i:4 * half + 4:2, :, :].rearrange("p h a t -> p h (a t)"),
                               PS[:, b, :].rearrange("p (h x) -> p h x", h=2), low2, ALU.mult)
                            give(b)
                    dve.sem_inc(score_ready, 1)
                    dve.wait_ge(n_ready, g * LEVELS + 1)
                    for k in range(LEVELS):
                        for h in range(2):
                            hs = slice(4 * h, 4 * h + 4)
                            if k == 0:
                                tt(XT[:, hs, :], idb, Nl[0][:, hs, :], ALU.subtract)
                                take(4 + 2 * h)
                                tt(X[:, hs, :], idb, PS[:, 4 + 2 * h, :].rearrange("p (h t) -> p h t", h=4),
                                   ALU.subtract)
                                give(4 + 2 * h)
                            else:
                                bs = (4 + 2 * h, 5 + 2 * h) if k < LEVELS - 1 else (4 + 2 * h,)
                                for b in bs:
                                    take(b)
                                for b, m in zip(bs, (XT, X)):
                                    tt(m[:, hs, :], m[:, hs, :], PS[:, b, :].rearrange("p (h t) -> p h t", h=4),
                                       ALU.subtract)
                                    give(b)
                            dve.sem_inc(xt_ready, 1)
                    take(4)
                    y = kk[:, c, :]
                    step(dve.tensor_copy(y, PS[:, 4, :]))
                    give(4)
                    if c == 0:
                        take(5)
                        dve.wait_ge(f_exp, layer + 1)
                        for i in range(2):
                            s64 = slice(64 * i, 64 * i + 64)
                            tt(state[s64, :, s64], PS[s64, 5, :].rearrange("p (q v) -> p q v", q=4)[:, :, s64],
                               F[s64, :].unsqueeze(2).to_broadcast([64, 4, 64]), ALU.mult)
                        give(5)
                        dve.sem_inc(state_ready, 1)
                    yh, t2 = heads(y), tmp[:, 2, :]
                    step(dve.tensor_reduce(gmu, yh, AX_X, ALU.add))
                    ts(gmu, gmu, 1.0 / HD, None, ALU.mult)
                    tt(yh, yh, per_head(gmu), ALU.subtract)
                    tt(t2, y, y, ALU.mult)
                    step(dve.tensor_reduce(gvar, heads(t2), AX_X, ALU.add))
                    dve.sem_inc(gvar_ready, 1)
                    dve.wait_ge(gstd_ready, g + 1)
                    step(dve.reciprocal(gvar, gvar))
                    tt(yh, yh, per_head(gvar), ALU.mult)
                    if c == 0:
                        dve.wait_ge(late_in, 32 * (layer + 1))
                    tt(y, y, bc[:, LNW, :], ALU.mult)
                    tt(y, y, bc[:, LNB, :], ALU.add)
                    tt(heads(t2), heads(v_[:, c, :]), per_head(bonus[:, c, :]), ALU.mult)
                    tt(y, y, t2, ALU.add)
                    tt(y, y, gg[:, c, :], ALU.mult)
                dve.sem_inc(yc_ready, 1)
                if layer == 0:
                    dve.wait_ge(sin_ready, 1)
                dve.wait_ge(rest_ready, 14 * (layer + 1))
                t1b, t2b = (tmp[:, i, 0:24 * HALF].rearrange("p (h f) -> p h f", f=HALF) for i in range(2))
                t3b, t4b = (tmp[:, i, 256:256 + 24 * HALF].rearrange("p (h f) -> p h f", f=HALF) for i in range(2))
                for t in range(NT):
                    qk = proj[:, t, Q0:VB0].rearrange("p (h d) -> p h d", d=HD)
                    lo, hi = qk[:, :, 0:HALF], qk[:, :, HALF:2 * HALF]
                    sin = angle[:, 4, t * HALF:(t + 1) * HALF].unsqueeze(1).to_broadcast([P, 24, HALF])
                    cos = angle[:, 5, t * HALF:(t + 1) * HALF].unsqueeze(1).to_broadcast([P, 24, HALF])
                    tt(t1b, lo, cos, ALU.mult)
                    tt(t2b, hi, sin, ALU.mult)
                    tt(t3b, hi, cos, ALU.mult)
                    tt(t4b, lo, sin, ALU.mult)
                    tt(lo, t1b, t2b, ALU.subtract)
                    tt(hi, t3b, t4b, ALU.add)
                dve.sem_inc(rot_ready, 1)
                for job in range(NT * BHG):
                    head, t = job // NT, job % NT
                    g = layer * NT * BHG + job
                    n = (t + 1) * P
                    at, _ = CONST_AT[f"attend{t}"]
                    for b, c0, c1 in ((4, 0, 2 * n), (5, 2 * n, 3 * n)):
                        take(b)
                        stt(prob[g % 2][:, c0:c1], PS[:, b, 0:c1 - c0], HD ** -0.5, tab[:, at + c0:at + c1],
                            ALU.mult, ALU.add)
                        give(b)
                    nm = nmax[:, g % 2:g % 2 + 1]
                    step(dve.tensor_reduce(nm, prob[g % 2][:, 0:3 * n], AX_X, ALU.max))
                    ts(nm, nm, -1.0, None, ALU.mult)
                    dve.sem_inc(p_ready, 1)
                    b = 6 + g % 2
                    take(b)
                    d = den[:, g % 2:g % 2 + 1]
                    step(dve.reciprocal(d, d))
                    ts(yb[:, t, head * HD:(head + 1) * HD], PS[:, b, 0:HD], d, None, ALU.mult)
                    give(b)
                dve.sem_inc(yb_ready, 1)
                take(4)
                inc = const("low_incl").unsqueeze(1).to_broadcast([P, AG, P])
                tt(wsT, PS[:, 4, :].rearrange("p (g t) -> p g t", g=AG), inc, ALU.mult)
                give(4)
                for t in range(NT):
                    v = proj[:, t, V0:V0 + W]
                    step(dve.bn_stats(bst, v))
                    step(dve.bn_aggr(bag, bst))
                    dve.sem_inc(ln_ready, 1)
                    dve.wait_ge(lsd_ready, layer * NT + t + 1)
                    step(dve.reciprocal(lrs, lrs))
                    step(dve.tensor_scalar(vn, v, bag[:, 0:1], lrs, ALU.subtract, ALU.mult))
                    tt(vn, vn, bc[:, GLG, :], ALU.mult)
                    tt(vn, vn, bc[:, GLB, :], ALU.add)
                    dve.sem_inc(vn_ready, 1)
                    take(5)
                    for g in range(AG):
                        u = proj[:, t, U0 + g * P:U0 + (g + 1) * P]
                        stt(u, PS[:, 5, g * P:(g + 1) * P], vec[:, VBS + g:VBS + g + 1], u, ALU.add, ALU.mult)
                    give(5)
                dve.sem_inc(ya_ready, 1)
                dve.wait_ge(yT_ready, 5 * (layer + 1))
                for br in range(3):
                    for half in range(2):
                        for t in range(NT):
                            i = 4 * br + 2 * half + t
                            g = 12 * layer + i
                            dve.wait_ge(gate_ready, g + 1)
                            take(4 + t)
                            m = merged[:, t, half * W:(half + 1) * W]
                            if br == 0:
                                tt(m, gate[i % 2], PS[:, 4 + t, :], ALU.mult)
                            else:
                                tt(tmp[:, t, :], gate[i % 2], PS[:, 4 + t, :], ALU.mult)
                            give(4 + t)
                            dve.sem_inc(gate_used, 1)
                            if br:
                                tt(m, m, tmp[:, t, :], ALU.add)
                dve.sem_inc(merged_ready, 1)
                for half in range(2):
                    for t in range(NT):
                        take(4 + t)
                        xs = x[:, t, half * W:(half + 1) * W]
                        tt(xs, xs, PS[:, 4 + t, :], ALU.add)
                        give(4 + t)
                norm(2 * layer + 2, VFFN)
                lg = rt[:, 0:40].rearrange("p (t n) -> p t n", t=NT)
                for t in range(NT):
                    take(6 + t)
                    step(dve.tensor_copy(lg[:, t, :], PS[:, 6 + t, 0:20]))
                    give(6 + t)
                dve.sem_inc(gains_used, 1)
                first = const("first")
                ex = rt[:, 40:50].rearrange("p (t n) -> p t n", t=NT)
                mg = rt[:, 50:52].rearrange("p (t n) -> p t n", t=NT)
                mx = rt[:, 52:54].rearrange("p (t n) -> p t n", t=NT)
                one = [rt[:, 56 + 8 * i:64 + 8 * i].rearrange("p (t n) -> p t n", t=NT) for i in range(3)]
                pick = rt[:, 80:88].rearrange("p (t n) -> p t n", t=NT)
                m12 = [rt[:, 88 + 2 * i:90 + 2 * i].rearrange("p (t n) -> p t n", t=NT) for i in range(2)]
                prod = rt[:, 96:128].rearrange("p (t g n) -> p t g n", t=NT, g=NG)
                den2 = rt[:, 128:130].rearrange("p (t n) -> p t n", t=NT)
                gpr = rt[:, 130:132].rearrange("p (t n) -> p t n", t=NT)
                fb = first.unsqueeze(1).to_broadcast([P, NT, 4])

                def choose(hot, vals, top):
                    step(dve.tensor_reduce(top, vals, AX_X, ALU.max))
                    tt(hot, vals, top.to_broadcast([P, NT, 4]), ALU.is_equal)
                    tt(hot, hot, fb, ALU.mult)
                    step(dve.tensor_reduce(mx, hot, AX_X, ALU.max))
                    tt(hot, hot, mx.to_broadcast([P, NT, 4]), ALU.is_equal)

                choose(one[0], lg[:, :, 0:4], mg)
                tt(ex[:, :, 0:4], lg[:, :, 0:4], mg.to_broadcast([P, NT, 4]), ALU.subtract)
                for t in range(NT):
                    tt(prod[:, t], lg[:, t, 4:20].rearrange("p (g n) -> p g n", g=NG),
                       one[0][:, t, :].unsqueeze(2).to_broadcast([P, NG, 4]), ALU.mult)
                    step(dve.tensor_reduce(pick[:, t, :], prod[:, t].rearrange("p g n -> p n g"), AX_X, ALU.add))
                choose(one[1], pick, m12[0])
                stt(pick.rearrange("p t n -> p (t n)"), one[1].rearrange("p t n -> p (t n)"), NEG,
                    pick.rearrange("p t n -> p (t n)"), ALU.mult, ALU.add)
                choose(one[2], pick, m12[1])
                tt(ex[:, :, 4:5], m12[1], m12[0], ALU.subtract)
                dve.sem_inc(logit_ready, 1)
                dve.wait_ge(rexp_ready, layer + 1)
                step(dve.tensor_reduce(gpr, ex[:, :, 0:4], AX_X, ALU.add))
                ts(den2, ex[:, :, 4:5], 1.0, None, ALU.add)
                tt(gpr, gpr, den2, ALU.mult)
                step(dve.reciprocal(gpr, gpr))
                tt(one[2], one[2], ex[:, :, 4:5].to_broadcast([P, NT, 4]), ALU.mult)
                tt(one[1], one[1], one[2], ALU.add)
                tt(one[1], one[1], gpr.to_broadcast([P, NT, 4]), ALU.mult)
                for t in range(NT):
                    tt(combine[:, t, :].rearrange("p (g n) -> p g n", g=NG),
                       one[0][:, t, :].unsqueeze(2).to_broadcast([P, NG, 4]),
                       one[1][:, t, :].unsqueeze(1).to_broadcast([P, NG, 4]), ALU.mult)
                f4 = taken[4]
                u0 = layer * 2 * NE
                with dve.Fori(0, NE) as e:
                    for t in range(NT):
                        dve.wait_ge(bank_full[4], e * 2 + (f4 + t + 1))
                        dve.wait_ge(silu_ready, e * 2 + (u0 + t + 1))
                        dve.scalar_tensor_tensor(out=hid[t], in0=PS[:, 4, :], scalar=combine[:, t, bass.ds(e, 1)],
                                                 in1=hid[t], op0=ALU.mult, op1=ALU.mult).then_inc(hid_ready, 1)
                        dve.wait_ge(hid_ready, e * 2 + (u0 + t + 1))
                        dve.sem_inc(bank_read[4], 1)
                taken[4] += 2 * NE
                for half in range(2):
                    take(6 + half)
                    step(dve.tensor_copy(x[:, 1, half * W:(half + 1) * W], PS[:, 6 + half, :]))
                    give(6 + half)
                dve.wait_ge(moe_a, layer + 1)
                dve.sem_inc(layer_done, 1)
            norm(2 * LAYERS + 1, None)
            dve.wait_ge(fin_in, 16)
            fg = bc[:, 0:2, :].rearrange("p a n -> p (a n)")
            for t in range(NT):
                tt(h_nat[:, t, :], h_nat[:, t, :], fg, ALU.mult)
            dve.sem_inc(fin_done, 1)


_INS = ['x', 'positions', 'norm_mix_g', 'w_in', 'gmlp_ln_g', 'gmlp_ln_b', 'gmlp_ws', 'gmlp_bs', 'rwkv_mu_rkv',
        'rwkv_mu_wag', 'rwkv_w0', 'rwkv_w1', 'rwkv_w2', 'rwkv_a0', 'rwkv_a1', 'rwkv_a2', 'rwkv_g1', 'rwkv_g2',
        'rwkv_k_k', 'rwkv_k_a', 'rwkv_r_k', 'rwkv_ln_w', 'rwkv_ln_b', 'rwkv_mu_v', 'rwkv_v0', 'rwkv_v1', 'rwkv_v2',
        'w_branch_a', 'w_branch_b', 'w_branch_c', 'w_gate', 'b_gate', 'w_out', 'norm_ffn_g', 'router_group_w',
        'router_group_b', 'router_expert_w', 'router_expert_b', 'expert_w_gate', 'expert_w_up', 'expert_w_down',
        'final_norm_g']


def kernel(**inputs):
    import numpy as _np
    import concourse.bacc as _bacc
    from concourse import mybir as _mybir
    from concourse.bass_utils import run_bass_kernel_spmd as _run

    nc = _bacc.Bacc("TRN2", target_bir_lowering=False, num_devices=1)
    given = {name: _np.ascontiguousarray(inputs[name]) for name in _INS}
    given["table"], given["select"] = TABLE, SELECT
    arrays, args = {}, {}
    for name, v in given.items():
        arrays[f"in_{name}"] = v
        args[name] = nc.dram_tensor(f"in_{name}", v.shape, _mybir.dt.from_np(v.dtype), kind="ExternalInput").ap()
    args["out"] = nc.dram_tensor("out_0", (1, S, D), F32, kind="ExternalOutput").ap()
    hybrid_moe_kernel(nc, args)
    r = _run(nc, [arrays], core_ids=[0])
    return r.results[0]["out_0"]
```

```python
from contextlib import ExitStack

import numpy as np

import concourse.bass as bass
from concourse import mybir

F32 = mybir.dt.float32
F32R = mybir.dt.float32r
I32 = mybir.dt.int32
ACT = mybir.ActivationFunctionType
ALU = mybir.AluOpType
AX_X = mybir.AxisListType.X

P = 128
S = 256
NT = S // P
D = 1024
KC = D // P
W = 512
LAYERS = 2
HD = 64
AG = 4
BH = 12
BHG = 4
CH = 8
NE = 16
NG = 4
EPG = 4
FF = 512
HALF = 8
RING = 3
DECAY = float(np.float32(np.exp(-0.5)))
NEG = -1e30
ROUND = 12582912.0
LEVELS = 7

U0, V0, Q0, K0, VB0, R0, CK0, CV0, PCOLS = 0, 512, 1024, 1792, 2560, 3328, 3840, 4352, 4864

CONST_AT = {}


def constants():
    j = np.arange(P)[:, None]
    t = np.arange(P)[None, :]
    mid = (j < P // 2).astype(np.float64)
    parts = {
        "ident": (j == t),
        "decay_incl": -DECAY * ((j <= t) - mid),
        "decay_prev": -DECAY * ((j < t) - mid),
        "shift": (j == t - 1).astype(float) - (j == t),
        "edge": (j == P - 1) & (t == 0),
        "low_strict": (j < t),
        "low_incl": (j <= t),
        "after_mid": -DECAY * (1 - mid),
        "before_mid": -DECAY * mid,
    }
    for k in range(LEVELS):
        n = 1 << k
        parts[f"level{k}"] = (j // (2 * n) == t // (2 * n)) & (j % (2 * n) < n) & (t % (2 * n) >= n)
    rows = []
    for window, dil in ((128, 1), (512, 4), (2048, 16)):
        away = j + P - np.arange(2 * P)[None, :]
        rows.append(np.where((away >= 0) & (away <= window) & (away % dil == 0), 0.0, NEG))
    parts["attend"] = np.concatenate(rows, 1)
    parts["ones"] = np.ones((P, P))
    parts["index"] = np.broadcast_to(np.arange(4), (P, 4))
    parts["place"] = np.broadcast_to(np.arange(P), (P, P))
    parts["first"] = np.broadcast_to(4.0 - np.arange(4), (P, 4))
    freq = 500000.0 ** (-np.arange(HALF) / HALF)
    parts["freq"] = np.broadcast_to(freq, (P, HALF))
    parts["eps_rms"] = np.full((P, 1), 1e-6)
    parts["eps_ln"] = np.full((P, 1), 1e-5)
    parts["eps_gn"] = np.full((P, 1), HD * 1e-5)
    parts["zero"] = np.zeros((P, 1))
    at = 0
    for name, a in parts.items():
        CONST_AT[name] = (at, a.shape[1])
        at += a.shape[1]
    table = np.concatenate([np.asarray(a, np.float64) for a in parts.values()], 1).astype(np.float32)
    return table


TABLE = constants()


def two_pi_parts():
    left, parts = 2 * np.pi, []
    for _ in range(3):
        e = np.floor(np.log2(left))
        p = np.floor(left / 2 ** (e - 7)) * 2 ** (e - 7)
        parts.append(float(p))
        left -= p
    return parts + [float(np.float32(left))]


TWO_PI = two_pi_parts()


PIECE = 1024
LOAD = 2 * PIECE
RING = 3
HL = 4
EXPERT_LOADS = 24
EXPERT_PIECES = 48
SEGMENTS = [(0, 0), (1, 0), (0, 1), (2, 0), (1, 1), (0, 2), (2, 1), (1, 2), (0, 3), (2, 2), (1, 3), (2, 3)]


def straight_loads():
    blocks = [("w_in", R0, W), ("w_in", CK0, W), ("w_in", CV0, W)]
    rest = [("w_in", c, min(W, R0 - c)) for c in range(Q0, R0, W)]
    rest = rest[:-2] + [rest[-1], rest[-2]] + [("w_in", c, W) for c in (U0, V0)]
    loads = []

    def dense(b):
        loads.extend(("dense", (*b, j), b[2] * 4 // PIECE) for j in range(2))

    for b in blocks:
        dense(b)
    loads += [("lora1", (0,), 0), ("lora1", (1,), 0), ("lora2", (), 0)]
    for b in rest:
        dense(b)
    for k in range(4):
        dense(("w_gate", k * W, W))
    for br in range(3):
        if br:
            dense(("w_gate", (br + 3) * W, W))
        for half in range(2):
            loads.append(("branch", (br, half), 0))
    for half in range(2):
        dense(("w_out", half * W, W))
    return loads


LOADS = straight_loads()
REST = [a[1:3] for k, a, _ in LOADS if k == "dense" and a[0] == "w_in" and a[3] == 0][3:]
DMAS = {"lora1": 4, "lora2": 4}


def lo_counts(q):
    return q // 3, q - q // 3


CHUNK_BLOCKS = (len(REST) - 3, len(REST) - 2)
REST_QKV = 2 * (len(REST) - 2)
BLOCK_ORDER = {"time": range(0, 3), "rest": range(3, 3 + len(REST)), "gate": range(3 + len(REST), 9 + len(REST)),
               "out": range(9 + len(REST), 11 + len(REST))}
BRANCH_LOADS = [n for n, (kind, _, _) in enumerate(LOADS) if kind == "branch"]
TILE_JOBS = {0: 4, 1: 4, 2: 1, 3: 1, 4: 5, 5: 2, 6: 2, 7: 3}
LAST_JOBS = {0: 4, 1: 4, 2: 1, 3: 1, 4: 5, 5: 1, 6: 1, 7: 2}


class Plan:

    def __init__(self):
        self.loads, self.blocks, self.experts, self.piece_at = [], [], [], []
        landed = [0] * (2 * RING)
        pieces = lo_p = lo_v = raw = 0
        n = 0
        freed = [None] * RING
        for layer in range(LAYERS):
            rows, blocks, first = [], [], pieces
            for kind, arg, np_ in LOADS:
                slot = n % RING
                n += 1
                landed[slot] += 16 * DMAS.get(kind, 1)
                if kind == "dense":
                    if arg[3] == 0:
                        blocks.append([arg[2], pieces, pieces + 2 * np_])
                    row = dict(kind=kind, arg=arg, slot=slot, landed=landed[slot], wait=freed[slot])
                    cols = arg[2] if np_ == 1 else W
                    for i in range(np_):
                        self.piece_at.append((slot, landed[slot], i, cols))
                    pieces += np_
                    lo_p += np_
                    freed[slot] = [("lo_p", lo_p)]
                else:
                    row = dict(kind=kind, arg=arg, slot=slot, landed=landed[slot], wait=freed[slot])
                    raw += 1
                    freed[slot] = [("raw_used", raw)]
                rows.append(row)
            self.loads.append(rows)
            self.blocks.append(blocks)
            slots = [(n + k) % RING for k in range(RING)] + [RING, RING + 1, RING + 2]
            self.experts.append(dict(slots=slots, landed=list(landed), pieces=pieces, lo_p=lo_p, lo_v=lo_v,
                                     first=first))
            for k in range(2 * RING):
                landed[k] += 16 * 4 * (NG + 1)
            pieces += EXPERT_PIECES * (NG + 1)
            self.piece_at += [None] * (EXPERT_PIECES * (NG + 1))
            lo_p += lo_counts(EXPERT_PIECES)[0] * (NG + 1)
            lo_v += lo_counts(EXPERT_PIECES)[1] * (NG + 1)
            freed = [[("lo_p", lo_p), ("lo_v", lo_v)]] * RING


PLAN = Plan()


def raw_slot(ring, proj, slot):
    if slot < RING:
        return ring[:, slot, :]
    flat = proj[:].rearrange("p t n -> p (t n)")
    return flat[:, (slot - RING) * LOAD:(slot - RING + 1) * LOAD]


def hybrid_moe_kernel(nc, a):
    ctx = ExitStack()
    with ctx:
        def sb(name, shape, dt=F32):
            return ctx.enter_context(nc.sbuf_tensor(name, shape, dt))

        def sem(name):
            return ctx.enter_context(nc.semaphore(name))

        x = sb("x_res", [P, NT, D])
        hTh = sb("hTh", [P, KC, S], F32R)
        hTl = sb("hTl", [P, KC, S], F32R)
        ring = sb("ring", [P, RING, LOAD])
        wh = sb("wh", [P, HL, PIECE], F32R)
        wl = sb("wl", [P, HL, PIECE], F32R)
        proj = sb("proj", [P, NT, PCOLS])
        tab = sb("tab", [P, TABLE.shape[1]])
        arena = sb("arena", [P, 9216])
        lw = sb("lw", [P, NT, W])
        aa = sb("aa", [P, NT, W])
        gg = sb("gg", [P, NT, W])
        kk = sb("kk", [P, NT, W])
        at_krT = (nc.sbuf_base + 31) // 32 * 32
        krT = sb("krT", [P, 4, 2, P])
        hidTh = nc.alloc_sbuf_tensor_at("hidTh", [P, 4, P], F32R, offset=at_krT)
        hidTl = nc.alloc_sbuf_tensor_at("hidTl", [P, 4, P], F32R, offset=at_krT + 4 * W)
        tmp2 = sb("tmp2", [P, W])
        tmp = [lw[:, 0, :], lw[:, 1, :], tmp2[:]]
        bc = sb("bc", [P, 6, W])
        state = sb("state", [P, 4, P])
        bias_rows = sb("bias_rows", [10, W])
        vec_rows = state[0:52, 0, :]
        vec = sb("vec", [P, 52])
        rw = sb("rw", [P, KC, 20])
        pos_i = sb("pos_i", [P, NT], I32)
        small = sb("small", [P, 400])
        angle = sb("angle", [P, 6, NT * HALF])
        plan_i = sb("plan_i", [P, 2], I32)
        v_first = nc.dram_tensor("v_first", [P, NT, W], F32, kind="Internal").ap()

        PS = ctx.enter_context(nc.psum_tensor("PS", [P, 8, W], F32))

        def const(name):
            at, n = CONST_AT[name]
            return tab[:, at:at + n]

        ident = const("ident")

        def view(at, *shape):
            n = int(np.prod(shape))
            v = arena[:, at:at + n]
            if len(shape) == 1:
                return v
            names = "abcd"[:len(shape)]
            return v.rearrange(f"p ({' '.join(names)}) -> p {' '.join(names)}",
                               **{k: s for k, s in zip(names[1:], shape[1:])})

        h_nat = view(0, NT, D)
        dhT = view(0, KC, S)
        mix = [view(2048, KC, S), view(4096, KC, S)]
        loraT = [view(6144 + 256 * m, S) for m in range(4)]
        hT = view(7168, KC, S)
        v_gate = view(2048, NT, W)
        v_old = view(0, NT, W)
        exps = [[view(4096 + 1536 * t + W * i, W) for i in range(3)] for t in range(NT)]
        SCb, SCk = view(0, CH, 2, P), view(2048, CH, 2, P)
        X, XT = view(4096, CH, P), view(5120, CH, P)
        Yl = view(6144, CH, P)
        bT, kT_c = view(6144, 4, P), view(6656, 4, P)
        Nl = [view(7168, CH, P), view(8192, CH, P)]
        qT, kT = view(0, 6, S), view(1536, 6, S)
        prob = [view(3072, 768), view(3840, 768)]
        probT = [view(4608, 6, P), view(5376, 6, P)]
        ws = view(6144, AG, P)
        wsT = view(6656, AG, P)
        yb = view(7168, NT, 256)
        vn = view(7680, W)
        yaT, ybT, ycT = view(0, 4, S), view(1024, 2, S), view(1536, 4, S)
        merged = view(2560, NT, D)
        gate = [proj[:, :, R0:R0 + W], proj[:, :, CK0:CK0 + W], proj[:, :, CV0:CV0 + W], aa, gg, view(6656, NT, W)]
        hT_router = view(2048, KC, S)
        hid = [view(2048, W), view(2560, W)]
        pickT = view(3072, NT, P)
        pick01 = view(3328, NT, P)
        group_sum = view(3584, NT, W)

        xTh = hTh[:, 0:4, :].rearrange("p a (b n) -> p (a b) n", b=2)
        xTl = hTl[:, 0:4, :].rearrange("p a (b n) -> p (a b) n", b=2)
        at_experts = []

        def raw_piece(ex, q):
            r = raw_slot(ring, proj, ex["slots"][q // 2 % (2 * RING)])
            if SEGMENTS[q // 4][0] < 2:
                return r[:, (q % 2) * PIECE:(q % 2 + 1) * PIECE]
            return r.rearrange("p (c n) -> p c n", c=2)[:, :, (q % 2) * W:(q % 2 + 1) * W]

        def pieces_of(v, q):
            return v if SEGMENTS[q // 4][0] < 2 else v.rearrange("p (c n) -> p c n", c=2)

        ss, rn = small[:, 0:2], small[:, 2:4]
        kn = small[:, 4:20].rearrange("p (t h) -> p t h", t=NT)
        bonus = small[:, 20:36].rearrange("p (t h) -> p t h", t=NT)
        F = small[:, 36:40]
        gmu = small[:, 40:48]
        gvar = small[:, 48:56]
        nmax = small[:, 56:58]
        den = small[:, 58:60]
        bst, bag = small[:, 60:66], small[:, 66:68]
        lrs = small[:, 68:69]
        combine = small[:, 72:104].rearrange("p (t e) -> p t e", t=NT)
        own = small[:, 104:112].rearrange("p (t n) -> p t n", t=NT)
        weight = small[:, 112:116]
        place = small[:, 116:118]
        inside = small[:, 118:128].rearrange("p (t b) -> p t b", t=NT)
        rt = small[:, 128:400]
        hot = rt[:, 56:64].rearrange("p (t n) -> p t n", t=NT)

        VG, VMU, VFFN, VBS = 0, 8, 40, 48
        MU, KK_, KA_, RK_ = (0, 1, 2), 3, 4, 5
        LNW, LNB, GLG, GLB, FFG = 0, 1, 3, 4, (2, 5)

        bank_full = [sem(f"bank_full{b}") for b in range(8)]
        bank_read = [sem(f"bank_read{b}") for b in range(8)]
        landed = [sem(f"landed{r}") for r in range(2 * RING)]
        hi_ready = sem("hi_ready")
        lo_p = sem("lo_p")
        lo_v = sem("lo_v")
        piece_used = sem("piece_used")
        raw_used = sem("raw_used")
        vf_out = sem("vf_out")
        vf_in = sem("vf_in")
        hTh_ready = sem("hTh_ready")
        hTl_ready = sem("hTl_ready")
        plan_ready = sem("plan_ready")
        pick_ready = sem("pick_ready")
        xTh_ready = sem("xTh_ready")
        g_ready = sem("g_ready")
        exps_ready = sem("exps_ready")
        hidTh_ready = sem("hidTh_ready")
        mTh_ready = sem("mTh_ready")
        stream = {"lo_p": lo_p, "lo_v": lo_v, "raw_used": raw_used}
        const_in = sem("const_in")
        rows_in = sem("rows_in")
        bc_in = sem("bc_in")
        late_in = sem("late_in")
        rw_in = sem("rw_in")
        ws_in = sem("ws_in")
        fin_in = sem("fin_in")
        out_done = sem("out_done")
        v_step = sem("v_step")
        a_step = sem("a_step")
        vec_ready = sem("vec_ready")
        ss_ready = sem("ss_ready")
        rms_ready = sem("rms_ready")
        hnat_ready = sem("hnat_ready")
        hT_v = sem("hT_v")
        hT_a = sem("hT_a")
        mix_ready = sem("mix_ready")
        lora_ready = sem("lora_ready")
        zs_ready = sem("zs_ready")
        rkv_ready = sem("rkv_ready")
        rest_ready = sem("rest_ready")
        mixed = sem("mixed")
        ksq_ready = sem("ksq_ready")
        knorm_ready = sem("knorm_ready")
        f_ready = sem("f_ready")
        f_exp = sem("f_exp")
        tilde_ready = sem("tilde_ready")
        crT_ready = sem("crT_ready")
        score_ready = sem("score_ready")
        n_ready = sem("n_ready")
        xt_ready = sem("xt_ready")
        y_ready = sem("y_ready")
        r_ready = sem("r_ready")
        sa_ready = sem("sa_ready")
        state_ready = sem("state_ready")
        gvar_ready = sem("gvar_ready")
        gstd_ready = sem("gstd_ready")
        rot_ready = sem("rot_ready")
        ang_ready = sem("ang_ready")
        sin_ready = sem("sin_ready")
        qkT_ready = sem("qkT_ready")
        p_ready = sem("p_ready")
        e_ready = sem("e_ready")
        pT_ready = sem("pT_ready")
        ln_ready = sem("ln_ready")
        lsd_ready = sem("lsd_ready")
        vn_ready = sem("vn_ready")
        ya_ready = sem("ya_ready")
        yb_ready = sem("yb_ready")
        yc_ready = sem("yc_ready")
        yT_ready = sem("yT_ready")
        gate_ready = sem("gate_ready")
        merged_ready = sem("merged_ready")
        logit_ready = sem("logit_ready")
        rexp_ready = sem("rexp_ready")
        c_done = sem("c_done")
        gains_used = sem("gains_used")
        tiles_done = sem("tiles_done")
        fin_done = sem("fin_done")

        A_BANKS, V_BANKS = (0, 1, 2, 3), (4, 5, 6, 7)
        assert set(A_BANKS) | set(V_BANKS) == set(range(8))

        def counts(eng):
            return (eng.value_load(plan_i[0:1, 0:1], min_val=0, max_val=S),
                    eng.value_load(plan_i[0:1, 1:2], min_val=0, max_val=NG - 1))

        block = ctx.enter_context(nc.Block())

        @block.sync
        def _(sp):
            sp.dma_start(x[:], a["x"].rearrange("b (t p) d -> p (b t) d", p=P)).then_inc(const_in, 16)
            sp.dma_start(tab[:], a["table"]).then_inc(const_in, 16)
            sp.dma_start(pos_i[:], a["positions"].rearrange("a (t p) -> p (a t)", p=P),
                         allow_slow_non_contiguous=True).then_inc(const_in, 16)

            def rows(layer):
                for r0, n, src in ((0, 8, a["norm_mix_g"][layer].rearrange("(r p) -> r p", p=P)),
                                   (8, 24, a["rwkv_mu_wag"][layer].rearrange("m (r p) -> (m r) p", p=P)),
                                   (32, 8, a["rwkv_mu_v"][0].rearrange("(r p) -> r p", p=P)),
                                   (40, 8, a["norm_ffn_g"][layer].rearrange("(r p) -> r p", p=P)),
                                   (48, 4, a["gmlp_bs"][layer])):
                    sp.dma_start(vec_rows[r0:r0 + n, :], src).then_inc(rows_in, 16)
                for r0, n, src in ((0, 6, a["b_gate"][layer].rearrange("(r n) -> r n", n=W)),
                                   (6, 1, a["rwkv_w0"][layer:layer + 1]),
                                   (7, 1, a["rwkv_a0"][layer:layer + 1]),
                                   (8, 1, a["rwkv_v0"][0:1])):
                    sp.dma_start(bias_rows[r0:r0 + n, :], src).then_inc(rows_in, 16)
                sp.dma_start(bias_rows[9:10, 0:4], a["router_group_b"][layer:layer + 1]).then_inc(rows_in, 16)
                sp.dma_start(bias_rows[9:10, 4:20], a["router_expert_b"][layer:layer + 1]).then_inc(rows_in, 16)

            def gains(layer):
                for slot, src in ((MU[0], a["rwkv_mu_rkv"][layer, 0]), (MU[1], a["rwkv_mu_rkv"][layer, 1]),
                                  (MU[2], a["rwkv_mu_rkv"][layer, 2]), (KK_, a["rwkv_k_k"][layer]),
                                  (KA_, a["rwkv_k_a"][layer]),
                                  (RK_, a["rwkv_r_k"][layer].rearrange("h d -> (h d)"))):
                    sp.dma_start(bc[:, slot, :], src.partition_broadcast(P)).then_inc(bc_in, 16)
                for c0, n, name in ((0, 4, "router_group_w"), (4, 16, "router_expert_w")):
                    sp.dma_start(rw[:, :, c0:c0 + n], a[name][layer].rearrange("(c p) n -> p c n", p=P))\
                        .then_inc(rw_in, 16)

            def load(layer, row):
                kind, arg, slot = row["kind"], row["arg"], row["slot"]
                for name, value in row["wait"] or ():
                    sp.wait_ge(stream[name], value)
                r = ring[:, slot, :]
                if kind == "dense":
                    name, c0, n, j = arg
                    pairs = [(r[:, 0:4 * n].rearrange("p (c n) -> p c n", c=4),
                              a[name][layer].rearrange("(c p) n -> p c n", p=P)[:, 4 * j:4 * j + 4, c0:c0 + n])]
                elif kind == "lora1":
                    v = r[:, 0:4 * 288].rearrange("p (c n) -> p c n", c=4)
                    pairs, at = [], 0
                    for name, n in (("rwkv_w1", 64), ("rwkv_a1", 64), ("rwkv_g1", 128), ("rwkv_v1", 32)):
                        src = a[name][0 if name == "rwkv_v1" else layer].rearrange("(c p) n -> p c n", p=P)
                        pairs.append((v[:, :, at:at + n], src[:, 4 * arg[0]:4 * arg[0] + 4, :]))
                        at += n
                elif kind == "lora2":
                    pairs = []
                    for i, (name, n) in enumerate((("rwkv_w2", 64), ("rwkv_a2", 64), ("rwkv_g2", 128),
                                                   ("rwkv_v2", 32))):
                        src = a[name][0 if name == "rwkv_v2" else layer]
                        pairs.append((r[0:n, i * W:(i + 1) * W], src))
                else:
                    name, c = (("w_branch_a", 4), ("w_branch_b", 2), ("w_branch_c", 4))[arg[0]]
                    c0 = arg[1] * W
                    pairs = [(r[:, 0:c * W].rearrange("p (c n) -> p c n", c=c),
                              a[name][layer].rearrange("(c p) n -> p c n", p=P)[:, :, c0:c0 + W])]
                for dst, src in pairs:
                    sp.dma_start(dst, src).then_inc(landed[slot], 16)

            def expert_loads(layer, i, group, first):
                ex = PLAN.experts[layer]
                n_p, n_v = lo_counts(EXPERT_PIECES)
                start = group * (EPG * D * W)
                for m in range(EXPERT_LOADS):
                    k = m % (2 * RING)
                    which, e = SEGMENTS[m // 2]
                    name = ("expert_w_gate", "expert_w_up", "expert_w_down")[which]
                    at = start + (2 * e + m % 2) * (D * W // 2)
                    due = None
                    if not (first and m < 2 * RING):
                        if m >= 2 * RING:
                            p_, v_ = lo_counts(2 * (m - 2 * RING) + 2)
                        else:
                            p_, v_ = (n - all_ for n, all_ in zip(lo_counts(2 * (m - 2 * RING) + 2 + EXPERT_PIECES),
                                                                  (n_p, n_v)))
                        due = i * n_p + (ex["lo_p"] + p_), i * n_v + (ex["lo_v"] + v_)
                    if not isinstance(group, int):
                        due = tuple(sp.to_reg(v) for v in due)
                    src = a[name][layer].rearrange("e k n -> (e k n)")[bass.ds(at, D * W // 2)]
                    n = (W, W, D)[which]
                    dst = raw_slot(ring, proj, ex["slots"][k]).rearrange("p (c n) -> p c n", n=n)
                    if due:
                        sp.wait_ge(lo_p, due[0])
                        sp.wait_ge(lo_v, due[1])
                    sp.dma_start(dst, src.rearrange("(c p n) -> p c n", p=P, n=n)).then_inc(landed[ex["slots"][k]], 16)

            rows(0)
            for layer in range(LAYERS):
                for n, row in enumerate(PLAN.loads[layer]):
                    load(layer, row)
                    if n == 2 and layer == 0:
                        gains(0)
                    if n == 27:
                        sp.wait_ge(yc_ready, layer + 1)
                        sp.dma_start(ws, a["gmlp_ws"][layer].rearrange("g t s -> t g s")).then_inc(ws_in, 16)
                    if n == 9 and layer:
                        sp.wait_ge(mix_ready, 7)
                        sp.dma_start(v_old, v_first).then_inc(vf_in, 16)
                    if n == 21:
                        if layer == 0:
                            sp.wait_ge(c_done, 1)
                            sp.dma_start(v_first, proj[:, :, CV0:CV0 + W]).then_inc(vf_out, 16)
                        sp.wait_ge(tilde_ready, NT * (layer + 1))
                        for slot, src in ((LNW, a["rwkv_ln_w"][layer]), (LNB, a["rwkv_ln_b"][layer]),
                                          (GLG, a["gmlp_ln_g"][layer]), (GLB, a["gmlp_ln_b"][layer]),
                                          (FFG[0], a["norm_ffn_g"][layer, 0:W]), (FFG[1], a["norm_ffn_g"][layer, W:D])):
                            sp.dma_start(bc[:, slot, :], src.partition_broadcast(P)).then_inc(late_in, 16)
                ex = PLAN.experts[layer]
                sp.wait_ge(lo_p, ex["lo_p"])
                sp.wait_ge(merged_ready, layer + 1)
                if layer == 0:
                    sp.wait_ge(vf_out, 16)
                expert_loads(layer, 0, 0, True)
                sp.wait_ge(gains_used, layer + 1)
                if layer + 1 < LAYERS:
                    rows(layer + 1)
                    gains(layer + 1)
                else:
                    sp.dma_start(bc[:, 0:2, :].rearrange("p a n -> p (a n)"),
                                 a["final_norm_g"].partition_broadcast(P)).then_inc(fin_in, 16)
                with sp.Fori(1, NG) as g:
                    expert_loads(layer, g, g, False)
                sp.wait_ge(plan_ready, layer + 1)
                largest, which = counts(sp)
                with sp.If(largest > P):
                    expert_loads(layer, NG, which, False)
                with sp.Else():
                    sp.wait_ge(tiles_done, layer + 1)
                    for k in range(2 * RING):
                        sp.sem_inc(landed[k], 16 * EXPERT_LOADS // (2 * RING))
            sp.wait_ge(fin_done, 1)
            sp.dma_start(a["out"].rearrange("b (t p) d -> p (b t) d", p=P), h_nat).then_inc(out_done, 16)
            sp.wait_ge(out_done, 16)

        @block.gpsimd
        def _(pool):
            def lo(layer, p):
                slot, _, i, cols = PLAN.piece_at[p]
                pool.wait_ge(hi_ready, p + 1)
                pool.tensor_tensor(wl[:, p % HL, :], ring[:, slot, i * PIECE:(i + 1) * PIECE],
                                   wh[:, p % HL, :].bitcast(F32), ALU.subtract).then_inc(lo_p, 1)

            def expert_lo(layer, i):
                ex = PLAN.experts[layer]
                for q in range(EXPERT_PIECES):
                    if q % 3 == 2:
                        k = (ex["pieces"] + q) % HL
                        pool.wait_ge(hi_ready, i * EXPERT_PIECES + (ex["pieces"] + q + 1))
                        pool.tensor_tensor(pieces_of(wl[:, k, :], q), raw_piece(ex, q),
                                           pieces_of(wh[:, k, :].bitcast(F32), q), ALU.subtract).then_inc(lo_p, 1)

            for layer in range(LAYERS):
                blocks = PLAN.blocks[layer]
                split = 3 + CHUNK_BLOCKS[0]
                for p in range(blocks[0][1], blocks[split][2]):
                    lo(layer, p)
                if layer == 0:
                    pool.wait_ge(const_in, 48)
                for c in range(NT):
                    g = layer * NT + c
                    p1 = blocks[split + c][2]
                    for p in range(p1, p1 + 2):
                        lo(layer, p)
                    pool.wait_ge(score_ready, g + 1)
                    for k in range(LEVELS):
                        if k == 2:
                            pool.wait_ge(xt_ready, g * 2 * LEVELS + 2)
                        elif k > 2:
                            pool.wait_ge(y_ready, (g * (LEVELS - 1) + k - 3) * 2 + 2)
                        at, _ = CONST_AT[f"level{k}"]
                        m = tab[:, at:at + P].unsqueeze(1).to_broadcast([P, CH, P])
                        pool.tensor_tensor(Nl[k % 2], SCb[:, :, 0, :], m, ALU.mult).then_inc(n_ready, 1)
                    for p in range(p1 + 2, p1 + 4):
                        lo(layer, p)
                for p in range(p1 + 4, blocks[-1][2]):
                    lo(layer, p)
                with pool.Fori(0, NG) as i:
                    expert_lo(layer, i)
                pool.wait_ge(plan_ready, layer + 1)
                largest, _ = counts(pool)
                with pool.If(largest > P):
                    expert_lo(layer, NG)
                with pool.Else():
                    pool.wait_ge(tiles_done, layer + 1)
                    pool.sem_inc(lo_p, lo_counts(EXPERT_PIECES)[0])

        @block.tensor
        def _(pe):
            jobs = [0] * 8
            raw = [0]

            def open_bank(b):
                if jobs[b]:
                    pe.wait_ge(bank_read[b], jobs[b])

            def close_bank(b, mm):
                mm.then_inc(bank_full[b], 1)
                jobs[b] += 1

            def raw_load(layer, n):
                row = PLAN.loads[layer][n]
                pe.wait_ge(landed[row["slot"]], row["landed"])
                return ring[:, row["slot"], :]

            def transposes(bank, srcs):
                open_bank(bank)
                for i, s in enumerate(srcs):
                    n = s.shape[0]
                    mm = pe.transpose(PS[:, bank, i * P:i * P + n], s, ident[0:n, 0:n])
                close_bank(bank, mm)

            def norm_transposes(n):
                pe.wait_ge(hnat_ready, n)
                for bank in (2, 4, 3, 5):
                    c = 2 * (2, 3, 4, 5).index(bank)
                    transposes(bank, [h_nat[:, t, (c + i) * P:(c + i + 1) * P] for i in range(2) for t in range(NT)])

            def add_bias(out, row, n, rows=9):
                return pe.matmul(out, ident[0:rows, row:row + 1].to_broadcast([rows, P]), bias_rows[0:rows, 0:n],
                                 start=False, stop=True)

            def dense_piece(layer, blk, j, banks=(0, 1), bias=None):
                n, p0, p1 = PLAN.blocks[layer][blk]
                p = p0 + j
                cp = PIECE // n
                ex = PLAN.experts[layer]
                pe.wait_ge(lo_p, ex["lo_p"] - (ex["pieces"] - 1 - p))
                h_ = wh[:, p % HL, :].rearrange("p (c n) -> p c n", c=cp)
                l_ = wl[:, p % HL, :].rearrange("p (c n) -> p c n", c=cp)
                last = p == p1 - 1
                for t in range(NT):
                    b = banks[t]
                    if j == 0:
                        open_bank(b)
                    out = PS[:, b, 0:n]
                    for i in range(cp):
                        c = j * cp + i
                        xh, xl = hTh[:, c, t * P:(t + 1) * P], hTl[:, c, t * P:(t + 1) * P]
                        pe.matmul(out, xh, h_[:, i, :], start=(c == 0), stop=False)
                        pe.matmul(out, xh, l_[:, i, :], start=False, stop=False)
                        mm = pe.matmul(out, xl, h_[:, i, :], start=False,
                                       stop=(last and i == cp - 1 and bias is None))
                    if last:
                        if bias is not None:
                            mm = add_bias(out, bias, n)
                        close_bank(b, mm)
                if last:
                    pe.drain().then_inc(piece_used, 1)
                else:
                    mm.then_inc(piece_used, 1)

            def dense(layer, blk, banks=(0, 1), bias=None):
                for j in range(PLAN.blocks[layer][blk][2] - PLAN.blocks[layer][blk][1]):
                    dense_piece(layer, blk, j, banks, bias)

            def raw_done(n=1):
                pe.drain().then_inc(raw_used, n)

            pe.wait_ge(const_in, 48)
            for layer in range(LAYERS):
                pe.wait_ge(rows_in, 11 * 16 * (layer + 1))
                transposes(4, [vec_rows])
                norm_transposes(2 * layer + 1)
                pe.wait_ge(hTl_ready, layer + 1)
                for blk in BLOCK_ORDER["time"]:
                    dense(layer, blk)
                l1 = [raw_load(layer, 6 + j)[:, 0:4 * 288].rearrange("p (c n) -> p c n", c=4) for j in range(2)]
                nmix = 3 + layer
                mix0 = 3 * layer
                for m, (at, n) in enumerate(((0, 64), (64, 64), (128, 128), (256, 32))[:nmix]):
                    pe.wait_ge(mix_ready, mix0 + m + 1)
                    b = 2 + m % 2
                    open_bank(b)
                    for c in range(KC):
                        mm = pe.matmul(PS[0:n, b, 0:S], l1[c // 4][:, c % 4, at:at + n], mix[m % 2][:, c, :],
                                       start=(c == 0), stop=(c == KC - 1))
                    close_bank(b, mm)
                raw_done(2)
                blk = raw_load(layer, 8)
                for m, (n, bias) in enumerate(((64, 6), (64, 7), (128, None), (32, 8))[:nmix]):
                    pe.wait_ge(lora_ready, mix0 + m + 1)
                    for t in range(NT):
                        b = 2 + t
                        open_bank(b)
                        mm = pe.matmul(PS[:, b, :], loraT[m][0:n, t * P:(t + 1) * P], blk[0:n, m * W:(m + 1) * W],
                                       start=True, stop=bias is None)
                        if bias is not None:
                            mm = add_bias(PS[:, b, :], bias, W)
                        close_bank(b, mm)
                raw_done()
                pe.wait_ge(rkv_ready, 6 * (layer + 1))
                for i, c0 in enumerate((R0, CK0, CV0)):
                    for t in (1, 0):
                        b = 4 + t
                        open_bank(b)
                        mm = pe.matmul(PS[:, b, :], const("shift"), proj[:, t, c0:c0 + W], start=True, stop=(t == 0))
                        if t:
                            mm = pe.matmul(PS[:, b, :], const("edge"), proj[:, 0, c0:c0 + W], start=False, stop=True)
                        close_bank(b, mm)
                pe.wait_ge(zs_ready, 14 if layer else 6)
                for t in range(NT):
                    if t:
                        open_bank(6)
                        for q in range(4):
                            pe.matmul(PS[:, 6, q:q + 1], lw[:, 0, q * P:(q + 1) * P], const("after_mid"),
                                      start=True, stop=False)
                            mm = pe.matmul(PS[:, 6, q:q + 1], lw[:, 1, q * P:(q + 1) * P], const("before_mid"),
                                           start=False, stop=True)
                        close_bank(6, mm)
                    for b, m in ((2 - 2 * t, "decay_incl"), (3 - 2 * t, "decay_prev")):
                        open_bank(b)
                        close_bank(b, pe.matmul(PS[:, b, :], const(m), lw[:, t, :], start=True, stop=True))
                rest, gates = BLOCK_ORDER["rest"], BLOCK_ORDER["gate"]
                for blk in rest[:CHUNK_BLOCKS[0]]:
                    dense(layer, blk)
                for c in range(NT):
                    g = layer * NT + c
                    pe.wait_ge(tilde_ready, g + 1)
                    for b, src in ((4, kk), (5, proj[:, :, R0:R0 + W]), (6, aa), (7, proj[:, :, CK0:CK0 + W])):
                        transposes(b, [src[:, c, q * P:(q + 1) * P] for q in range(4)])
                    for j in range(2):
                        dense_piece(layer, rest[CHUNK_BLOCKS[c]], j)
                    pe.wait_ge(crT_ready, g + 1)
                    for half in range(2):
                        for b, lhs, i in ((4, bT, 0), (5, bT, 1), (6, kT_c, 0), (7, kT_c, 1)):
                            rows = slice(64 * i, 64 * i + 64)
                            open_bank(b)
                            for j in range(2):
                                q = 2 * half + j
                                mm = pe.matmul(PS[:, b, 256 * j:256 * j + 256], lhs[rows, q, :],
                                               krT[rows, q, :, :].rearrange("p a t -> p (a t)"),
                                               start=True, stop=True)
                            close_bank(b, mm)
                    dense_piece(layer, rest[CHUNK_BLOCKS[c]], 2)
                    for k in range(LEVELS):
                        n = g * LEVELS + k
                        N = Nl[k % 2]
                        pe.wait_ge(n_ready, n + 1)
                        for h in range(2):
                            if k:
                                pe.wait_ge(xt_ready, g * 2 * LEVELS + 2 * (k - 1) + h + 1)
                            b = 2 + h if k else 4 + 2 * h
                            open_bank(b)
                            for i in range(4):
                                hh = 4 * h + i
                                rhs = X[:, hh, :] if k else ident
                                mm = pe.matmul(PS[:, b, i * P:(i + 1) * P], N[:, hh, :], rhs, start=True, stop=True)
                            close_bank(b, mm)
                        if k == 0:
                            continue
                        for h in range(2):
                            pe.wait_ge(y_ready, (g * (LEVELS - 1) + k - 1) * 2 + h + 1)
                            for b, which in ((4 + 2 * h, "xt"), (5 + 2 * h, "x")):
                                if which == "x" and k == LEVELS - 1:
                                    continue
                                open_bank(b)
                                for i in range(4):
                                    hh = 4 * h + i
                                    l, r = (Yl, XT) if which == "xt" else (XT, Yl)
                                    mm = pe.matmul(PS[:, b, i * P:(i + 1) * P], l[:, hh, :], r[:, hh, :],
                                                   start=True, stop=True)
                                close_bank(b, mm)
                    if c:
                        pe.wait_ge(state_ready, layer + 1)
                    open_bank(2)
                    for hh in range(CH):
                        q = hh // 2
                        o = PS[:, 2, hh * HD:(hh + 1) * HD]
                        vh = proj[:, c, CV0 + hh * HD:CV0 + (hh + 1) * HD]
                        mm = pe.matmul(o, SCk[:, hh, 0, :], vh, start=True, stop=(c == 0))
                        if c:
                            mm = pe.matmul(o, krT[:, q, 0, :], state[:, q, 64 * (hh % 2):64 * (hh % 2) + 64],
                                           start=False, stop=True)
                    close_bank(2, mm)
                    pe.wait_ge(xt_ready, (g + 1) * 2 * LEVELS)
                    pe.wait_ge(r_ready, g + 1)
                    open_bank(3)
                    for hh in range(CH):
                        mm = pe.matmul(PS[:, 3, hh * HD:(hh + 1) * HD], XT[:, hh, :], tmp[0][:, hh * HD:(hh + 1) * HD],
                                       start=True, stop=True)
                    close_bank(3, mm)
                    pe.wait_ge(sa_ready, g + 1)
                    open_bank(4)
                    for hh in range(CH):
                        q = hh // 2
                        o = PS[:, 4, hh * HD:(hh + 1) * HD]
                        pe.matmul(o, SCb[:, hh, 1, :], tmp[1][:, hh * HD:(hh + 1) * HD], start=True, stop=False)
                        mm = pe.matmul(o, SCk[:, hh, 1, :], proj[:, c, CV0 + hh * HD:CV0 + (hh + 1) * HD],
                                       start=False, stop=(c == 0))
                        if c:
                            mm = pe.matmul(o, krT[:, q, 1, :], state[:, q, 64 * (hh % 2):64 * (hh % 2) + 64],
                                           start=False, stop=True)
                    close_bank(4, mm)
                    if c == 0:
                        open_bank(5)
                        for q in range(4):
                            cols = slice(q * P, (q + 1) * P)
                            pe.matmul(PS[:, 5, cols], aa[:, 0, cols], tmp[1][:, cols], start=True, stop=False)
                            mm = pe.matmul(PS[:, 5, cols], proj[:, 0, CK0 + q * P:CK0 + (q + 1) * P],
                                           proj[:, 0, CV0 + q * P:CV0 + (q + 1) * P], start=False, stop=True)
                        close_bank(5, mm)
                    dense_piece(layer, rest[CHUNK_BLOCKS[c]], 3)
                dense(layer, rest[-1])
                dense(layer, gates[0], bias=0)
                pe.wait_ge(rot_ready, layer + 1)
                pe.wait_ge(yc_ready, layer + 1)
                for i, c0 in enumerate((Q0, K0)):
                    for q in range(3):
                        transposes(2 + (3 * i + q) % 2, [proj[:, t, c0 + (2 * q + j) * P:c0 + (2 * q + j + 1) * P]
                                                         for j in range(2) for t in range(NT)])
                pe.wait_ge(qkT_ready, 6 * (layer + 1))
                n_jobs = NT * BHG

                def attend_scores(job):
                    head, t = job // NT, job % NT
                    n = (t + 1) * P
                    for gr in range(3):
                        hh = gr * BHG + head
                        rows, q = slice(64 * (hh % 2), 64 * (hh % 2) + 64), hh // 2
                        b = 4 + gr // 2
                        if gr != 1:
                            open_bank(b)
                        at = (gr % 2) * n
                        mm = pe.matmul(PS[:, b, at:at + n], qT[rows, q, t * P:(t + 1) * P], kT[rows, q, 0:n],
                                       start=True, stop=True)
                        if gr:
                            close_bank(b, mm)

                def attend_values(job):
                    head, t = job // NT, job % NT
                    g = layer * n_jobs + job
                    pe.wait_ge(e_ready, g + 1)
                    keys = [(gr, kt) for gr in range(3) for kt in range(t + 1)]
                    transposes(2, [prob[g % 2][:, i * P:(i + 1) * P] for i in range(min(4, len(keys)))])
                    if len(keys) > 4:
                        transposes(3, [prob[g % 2][:, i * P:(i + 1) * P] for i in range(4, len(keys))])
                    pe.wait_ge(pT_ready, g + 1)
                    b = 6 + g % 2
                    open_bank(b)
                    for i, (gr, kt) in enumerate(keys):
                        hh = gr * BHG + head
                        mm = pe.matmul(PS[:, b, 0:HD], probT[g % 2][:, i, :],
                                       proj[:, kt, VB0 + hh * HD:VB0 + (hh + 1) * HD],
                                       start=(i == 0), stop=(i == len(keys) - 1))
                    close_bank(b, mm)

                attend_scores(0)
                for job in range(n_jobs):
                    if job + 1 < n_jobs:
                        attend_scores(job + 1)
                    dense_piece(layer, gates[1 + job // 4], job % 4, bias=1 + job // 4)
                    attend_values(job)
                pe.wait_ge(ws_in, 16 * (layer + 1))
                transposes(4, [ws[:, g, :] for g in range(AG)])
                dense_piece(layer, gates[3], 0, bias=3)
                for t in range(NT):
                    pe.wait_ge(vn_ready, layer * NT + t + 1)
                    open_bank(5)
                    for g in range(AG):
                        mm = pe.matmul(PS[:, 5, g * P:(g + 1) * P], wsT[:, g, :], vn[:, g * P:(g + 1) * P],
                                       start=True, stop=True)
                    close_bank(5, mm)
                    dense_piece(layer, gates[3], 1 + t, bias=3)
                pe.wait_ge(ya_ready, layer + 1)
                pe.wait_ge(yb_ready, layer + 1)
                for i, (src, n) in enumerate(((proj[:, :, U0:U0 + W], 4), (yb, 2), (kk, 4))):
                    for q in range(n // 2):
                        transposes(2 + q % 2, [src[:, t, (2 * q + j) * P:(2 * q + j + 1) * P]
                                               for j in range(2) for t in range(NT)])
                dense_piece(layer, gates[3], 3, bias=3)
                pe.wait_ge(yT_ready, 5 * (layer + 1))
                for br, (yT, n) in enumerate(((yaT, 4), (ybT, 2), (ycT, 4))):
                    if br:
                        dense(layer, gates[br + 3], bias=br + 3)
                    for half in range(2):
                        k = 2 * br + half
                        bw = raw_load(layer, BRANCH_LOADS[k])[:, 0:n * W].rearrange("p (c n) -> p c n", c=n)
                        for t in range(NT):
                            open_bank(4 + t)
                            for c in range(n):
                                mm = pe.matmul(PS[:, 4 + t, :], yT[:, c, t * P:(t + 1) * P], bw[:, c, :],
                                               start=(c == 0), stop=(c == n - 1))
                            close_bank(4 + t, mm)
                        raw_done()
                pe.wait_ge(merged_ready, layer + 1)
                for q in range(4):
                    transposes(2 + q % 2, [merged[:, t, (2 * q + j) * P:(2 * q + j + 1) * P]
                                           for j in range(2) for t in range(NT)])
                pe.wait_ge(bank_read[2], jobs[2])
                pe.wait_ge(bank_read[3], jobs[3])
                for blk in BLOCK_ORDER["out"]:
                    dense(layer, blk, banks=(4, 5))
                norm_transposes(2 * layer + 2)
                pe.wait_ge(hT_v, 2 * layer + 2)
                pe.wait_ge(hT_a, 2 * layer + 2)
                for t in range(NT):
                    b = 6 + t
                    open_bank(b)
                    for c in range(KC):
                        if (t, c) == (0, 0):
                            pe.wait_ge(rw_in, 32 * (layer + 1))
                        pe.matmul(PS[:, b, 0:20], hT_router[:, c, t * P:(t + 1) * P], rw[:, c, :],
                                  start=(c == 0), stop=False)
                    close_bank(b, add_bias(PS[:, b, 0:20], 9, 20, rows=10))
                pe.wait_ge(g_ready, layer + 1)
                open_bank(4)
                pe.matmul(PS[:, 4, 0:4], const("low_strict"), hot[:, 0, :], start=True, stop=True)
                pe.matmul(PS[:, 4, 4:8], const("ones"), hot[:, 0, :], start=True, stop=False)
                pe.matmul(PS[:, 4, 4:8], const("low_strict"), hot[:, 1, :], start=False, stop=True)
                pe.matmul(PS[:, 4, 8:12], const("ones"), hot[:, 0, :], start=True, stop=False)
                close_bank(4, pe.matmul(PS[:, 4, 8:12], const("ones"), hot[:, 1, :], start=False, stop=True))
                ex = PLAN.experts[layer]

                def gather(b, part):
                    for c in range(4 * part, 4 * part + 4):
                        for t in range(NT):
                            mm = pe.matmul(PS[:, b, (c % 4) * P:(c % 4 + 1) * P], h_nat[:, t, c * P:(c + 1) * P],
                                           pick01[:, t, :], start=(t == 0), stop=(t == NT - 1))
                    return mm

                def gather_weights(b):
                    for t in range(NT):
                        mm = pe.matmul(PS[:, b, 0:EPG], pick01[:, t, :], own[:, t, :],
                                       start=(t == 0), stop=(t == NT - 1))
                    return mm

                pe.wait_ge(pick_ready, layer * (NG + 1) + 1)
                for b in (5, 6):
                    open_bank(b)
                    close_bank(b, gather(b, b - 5))
                open_bank(7)
                close_bank(7, gather_weights(7))
                base = list(jobs)
                at_experts.append(base)
                tally = {}

                def signal(ins, s):
                    ins.then_inc(s, 1)
                    tally[s.name] = (s, tally.get(s.name, (s, 0))[1] + 1)

                def group_tile(i, more):
                    def wait_bank(b, n):
                        pe.wait_ge(bank_read[b], i * TILE_JOBS[b] + (base[b] + n))

                    def turn_hidden(e):
                        pe.wait_ge(bank_read[4], i * TILE_JOBS[4] + (base[4] + e + 1))
                        wait_bank(1, e)
                        for c in range(4):
                            mm = pe.transpose(PS[:, 1, c * P:(c + 1) * P], hid[e % 2][:, c * P:(c + 1) * P], ident)
                        signal(mm, bank_full[1])

                    pe.wait_ge(pick_ready, i + (layer * (NG + 1) + 1))
                    wait_bank(7, 0)
                    for t in range(NT):
                        mm = pe.transpose(PS[:, 7, t * P:(t + 1) * P], pick01[:, t, :], ident)
                    signal(mm, bank_full[7])
                    for s, (which, e) in enumerate(SEGMENTS):
                        if which == 0 and e == 0:
                            wait_bank(5, 0)
                            wait_bank(6, 0)
                        if s == 11:
                            if more:
                                pe.wait_ge(pick_ready, i + (layer * (NG + 1) + 2))
                                wait_bank(5, 0)
                                signal(gather(5, 0), bank_full[5])
                            turn_hidden(3)
                            if more:
                                wait_bank(6, 0)
                                signal(gather(6, 1), bank_full[6])
                                wait_bank(7, 1)
                                signal(gather_weights(7), bank_full[7])
                        if which == 2:
                            pe.wait_ge(bank_read[1], i * TILE_JOBS[1] + (base[1] + e + 1))
                        for r in range(4):
                            q = 4 * s + r
                            n_p, n_v = lo_counts(q + 1)
                            if q % 3 == 2:
                                pe.wait_ge(lo_p, i * lo_counts(EXPERT_PIECES)[0] + (ex["lo_p"] + n_p))
                            else:
                                pe.wait_ge(lo_v, i * lo_counts(EXPERT_PIECES)[1] + (ex["lo_v"] + n_v))
                            k = (ex["pieces"] + q) % HL
                            h_ = wh[:, k, :].rearrange("p (c n) -> p c n", c=2)
                            l_ = wl[:, k, :].rearrange("p (c n) -> p c n", c=2)
                            if which < 2:
                                b, n = ((0, e), (4, e))[which]
                                if r == 0:
                                    wait_bank(b, n)
                                full = r == 3
                            else:
                                b = 2 + r % 2
                                if e == 0 and r < 2:
                                    wait_bank(b, 0)
                                full = e == 3 and r >= 2
                            for j in range(2):
                                if which < 2:
                                    xh, xl = xTh[:, 2 * r + j, :], xTl[:, 2 * r + j, :]
                                    first, last = r + j == 0, r == 3 and j == 1
                                else:
                                    c = 2 * (r // 2) + j
                                    xh, xl = hidTh[:, c, :], hidTl[:, c, :]
                                    first, last = e == 0 and c == 0, e == 3 and c == 3
                                pe.matmul(PS[:, b, :], xh, h_[:, j, :], start=first, stop=False)
                                pe.matmul(PS[:, b, :], xh, l_[:, j, :], start=False, stop=False)
                                mm = pe.matmul(PS[:, b, :], xl, h_[:, j, :], start=False, stop=last)
                            if full:
                                signal(mm, bank_full[b])
                                signal(pe.drain(), piece_used)
                            else:
                                signal(mm, piece_used)
                            if which == 0 and r == 1 and e:
                                turn_hidden(e - 1)
                    for half in range(2):
                        pe.wait_ge(bank_read[2 + half], i * TILE_JOBS[2] + (base[2 + half] + 1))
                    for n, b in enumerate((7, 5, 6, 4)):
                        t, half = n // 2, n % 2
                        wait_bank(b, {7: 2, 5: 1, 6: 1, 4: 4}[b] if more else {7: 1, 5: 0, 6: 0, 4: 4}[b])
                        signal(pe.matmul(PS[:, b, :], pickT[:, t, :], group_sum[:, half, :], start=True, stop=True),
                               bank_full[b])

                with pe.Fori(0, NG) as i:
                    group_tile(i, True)
                largest, _ = counts(pe)
                tally.clear()
                with pe.If(largest > P):
                    group_tile(NG, False)
                with pe.Else():
                    pe.wait_ge(tiles_done, layer + 1)
                    for s, n in tally.values():
                        pe.sem_inc(s, n)
                for b in range(8):
                    jobs[b] += NG * TILE_JOBS[b] + LAST_JOBS[b]

        @block.scalar
        def _(act):
            taken = [0] * 8
            steps = [0]
            done = [0]

            def take(b):
                act.wait_ge(bank_full[b], taken[b] + 1)

            def give(b):
                act.sem_inc(bank_read[b], 1)
                taken[b] += 1

            def step(ins):
                steps[0] += 1
                ins.then_inc(a_step, 1)
                act.wait_ge(a_step, steps[0])

            def evac(b, out, func=ACT.Copy, signal=None, n=W, rows=P, scale=1.0, pat=None):
                take(b)
                src = PS[0:rows, b, 0:n]
                step(act.activation(out, src if pat is None else src.rearrange(*pat[0], **pat[1]), func, scale=scale))
                give(b)
                if signal is not None:
                    act.sem_inc(signal, 1)

            def norm(n, kind):
                act.wait_ge(ss_ready, n)
                step(act.activation(rn, ss, ACT.Sqrt, bias=const("eps_rms"), scale=1.0 / D))
                act.sem_inc(rms_ready, 1)
                if kind == "final":
                    return
                if kind == "mix":
                    act.wait_ge(vec_ready, (n + 1) // 2)
                for b in (2, 3):
                    take(b)
                    for i in range(2):
                        c = 2 * (b - 2) + i
                        src = PS[:, b, i * S:(i + 1) * S]
                        if kind == "mix":
                            step(act.activation(hT[:, c, :], src, ACT.Copy, scale=vec[:, VG + c:VG + c + 1]))
                        else:
                            step(act.activation(hT_router[:, c, :], src, ACT.Copy))
                    give(b)
                act.sem_inc(hT_a, 1)

            def hi_upto(layer, p1):
                for p in range(done[0], min(p1, PLAN.blocks[layer][-1][2])):
                    slot, value, i, _ = PLAN.piece_at[p]
                    act.wait_ge(landed[slot], value)
                    if p >= HL:
                        act.wait_ge(piece_used, p - HL + 1)
                    act.activation(wh[:, p % HL, :], ring[:, slot, i * PIECE:(i + 1) * PIECE], ACT.Copy)\
                        .then_inc(hi_ready, 1)
                    done[0] = p + 1

            def dense_evac(layer, blk, outs, func=ACT.Copy, signal=None, ahead=True):
                n, _, p1 = PLAN.blocks[layer][blk]
                if ahead:
                    hi_upto(layer, p1 + 3)
                for t in range(NT):
                    evac(t, outs[t], func, signal, n=n)
                if ahead:
                    hi_upto(layer, p1 + 4)

            act.wait_ge(const_in, 48)
            act.wait_ge(ang_ready, 1)
            step(act.activation(angle[:, 4, :], angle[:, 2, :], ACT.Sin))
            step(act.activation(angle[:, 5, :], angle[:, 3, :], ACT.Sin))
            act.sem_inc(sin_ready, 1)

            for layer in range(LAYERS):
                blocks = PLAN.blocks[layer]
                done[0] = blocks[0][1]
                hi_upto(layer, blocks[0][1] + 2)
                norm(2 * layer + 1, "mix")
                act.wait_ge(hT_v, 2 * layer + 1)
                step(act.activation(hTh[:], hT, ACT.Copy))
                act.sem_inc(hTh_ready, 1)
                hi_upto(layer, blocks[0][2])
                for blk, c0 in zip(BLOCK_ORDER["time"], (R0, CK0, CV0)):
                    dense_evac(layer, blk, [proj[:, t, c0:c0 + W] for t in range(NT)], signal=rkv_ready,
                               ahead=c0 != CV0)
                nmix = 3 + layer
                for m, (n, func) in enumerate(((64, ACT.Tanh), (64, ACT.Copy), (128, ACT.Sigmoid),
                                               (32, ACT.Copy))[:nmix]):
                    evac(2 + m % 2, loraT[m][0:n, :], func, lora_ready, n=S, rows=n)
                for m, (dst, func) in enumerate(((lw, ACT.Sigmoid), (aa, ACT.Sigmoid), (gg, ACT.Copy),
                                                 (v_gate, ACT.Sigmoid))[:nmix]):
                    for t in range(NT):
                        evac(2 + t, dst[:, t, :], func, zs_ready)
                    if m:
                        hi_upto(layer, blocks[3][1] + min(2 * m, HL))
                for t in range(NT):
                    b = 2 - 2 * t
                    take(b)
                    step(act.activation(exps[t][0], PS[:, b, :], ACT.Exp))
                    step(act.activation(exps[t][1], PS[:, b, :], ACT.Exp, scale=-1.0))
                    give(b)
                    evac(b + 1, exps[t][2], ACT.Exp, exps_ready)
                act.wait_ge(f_ready, layer + 1)
                step(act.activation(F, F, ACT.Exp))
                act.sem_inc(f_exp, 1)
                act.wait_ge(ksq_ready, layer + 1)
                step(act.activation(kn, kn, ACT.Sqrt))
                act.sem_inc(knorm_ready, 1)

                def rest_evac(i, ahead=True):
                    c0, n = REST[i]
                    dense_evac(layer, BLOCK_ORDER["rest"][i], [proj[:, t, c0:c0 + n] for t in range(NT)],
                               ACT.Gelu_apprx_tanh if c0 < Q0 else ACT.Copy, rest_ready, ahead=ahead)

                def group_deviation(g):
                    act.wait_ge(gvar_ready, g + 1)
                    step(act.activation(gvar, gvar, ACT.Sqrt, bias=const("eps_gn"), scale=1.0 / HD))
                    act.sem_inc(gstd_ready, 1)

                for i in range(CHUNK_BLOCKS[0]):
                    rest_evac(i)
                for c in range(NT):
                    g = layer * NT + c
                    if c:
                        group_deviation(g - 1)
                    p0 = blocks[3 + CHUNK_BLOCKS[c]][1]
                    hi_upto(layer, p0 + HL + 3)
                    for k in range(1, LEVELS):
                        for h in range(2):
                            evac(2 + h, Yl[:, 4 * h:4 * h + 4, :], signal=y_ready,
                                 pat=(("p (h t) -> p h t",), dict(h=4)))
                    evac(2, tmp[0], signal=r_ready)
                    evac(3, tmp[1], signal=sa_ready, scale=-1.0)
                    rest_evac(CHUNK_BLOCKS[c], ahead=False)
                    hi_upto(layer, p0 + 2 * HL)
                hi_upto(layer, p0 + 2 * HL + 1)
                group_deviation(g)
                rest_evac(len(REST) - 1)
                gates = BLOCK_ORDER["gate"]

                def gate_evac(k):
                    if k == 2:
                        act.wait_ge(yc_ready, layer + 1)
                    dense_evac(layer, gates[k], [gate[k][:, t, :] for t in range(NT)], ACT.Sigmoid, gate_ready,
                               ahead=k in (0, 4, 5))

                gate_evac(0)
                for i, dst in enumerate((qT, kT)):
                    for q in range(3):
                        evac(2 + (3 * i + q) % 2, dst[:, 2 * q:2 * q + 2, :], signal=qkT_ready,
                             pat=(("p (c t) -> p c t",), dict(c=2)))
                n_jobs = NT * BHG

                def exponentials(job):
                    g = layer * n_jobs + job
                    n = 3 * (job % NT + 1) * P
                    act.wait_ge(p_ready, g + 1)
                    step(act.activation(prob[g % 2][:, 0:n], prob[g % 2][:, 0:n], ACT.Exp,
                                        bias=nmax[:, g % 2:g % 2 + 1], accum_out=den[:, g % 2:g % 2 + 1]))
                    act.sem_inc(e_ready, 1)

                def turned(job):
                    g = layer * n_jobs + job
                    nk = 3 * (job % NT + 1)
                    evac(2, probT[g % 2][:, 0:min(4, nk), :], n=min(4, nk) * P,
                         pat=(("p (c t) -> p c t",), dict(t=P)))
                    if nk > 4:
                        evac(3, probT[g % 2][:, 4:nk, :], n=(nk - 4) * P, pat=(("p (c t) -> p c t",), dict(t=P)))
                    act.sem_inc(pT_ready, 1)

                p0 = blocks[gates[1]][1]
                for job in range(n_jobs):
                    exponentials(job)
                    turned(job)
                    hi_upto(layer, p0 + HL + job + 1)
                    if job % 4 == 3:
                        gate_evac(1 + job // 4)
                for t in range(NT):
                    act.wait_ge(ln_ready, layer * NT + t + 1)
                    step(act.activation(lrs, bag[:, 1:2], ACT.Sqrt, bias=const("eps_ln")))
                    act.sem_inc(lsd_ready, 1)
                for dst, n in ((yaT, 4), (ybT, 2), (ycT, 4)):
                    for q in range(n // 2):
                        evac(2 + q % 2, dst[:, 2 * q:2 * q + 2, :], signal=yT_ready,
                             pat=(("p (c t) -> p c t",), dict(c=2)))
                gate_evac(3)
                hi_upto(layer, blocks[gates[4]][1] + HL)
                gate_evac(4)
                gate_evac(5)
                for q in range(4):
                    b = 2 + q % 2
                    take(b)
                    act.activation(hTh[:, 2 * q:2 * q + 2, :], PS[:, b, :].rearrange("p (c t) -> p c t", c=2),
                                   ACT.Copy).then_inc(mTh_ready, 1)
                    taken[b] += 1
                hi_upto(layer, blocks[-1][2])
                norm(2 * layer + 2, "router")
                act.wait_ge(logit_ready, layer + 1)
                step(act.activation(rt[:, 40:50], rt[:, 40:50], ACT.Exp))
                act.sem_inc(rexp_ready, 1)
                ex = PLAN.experts[layer]
                base = at_experts[layer]

                def gathered_hi(b, value):
                    act.wait_ge(bank_full[b], value)
                    return act.activation(xTh[:, 4 * (b - 5):4 * (b - 5) + 4, :],
                                          PS[:, b, :].rearrange("p (c t) -> p c t", c=4), ACT.Copy)

                for b in (5, 6):
                    gathered_hi(b, base[b]).then_inc(xTh_ready, 1)
                tally = {}

                def signal(ins, s):
                    ins.then_inc(s, 1)
                    tally[s.name] = (s, tally.get(s.name, (s, 0))[1] + 1)

                def group_tile(i, more):
                    def full(b, n):
                        act.wait_ge(bank_full[b], i * TILE_JOBS[b] + (base[b] + n + 1))

                    def hi(q):
                        m = q // 2
                        k = m % (2 * RING)
                        slot = ex["slots"][k]
                        if q % 2 == 0:
                            act.wait_ge(landed[slot], i * 64 + (ex["landed"][slot] + 16 * (m // (2 * RING) + 1)))
                        act.wait_ge(piece_used, i * EXPERT_PIECES + (ex["pieces"] + q - HL + 1))
                        w = (ex["pieces"] + q) % HL
                        signal(act.activation(pieces_of(wh[:, w, :], q), raw_piece(ex, q), ACT.Copy), hi_ready)

                    def turned_hi(e):
                        full(1, e)
                        signal(act.activation(hidTh[:], PS[:, 1, :].rearrange("p (c t) -> p c t", c=4), ACT.Copy),
                               hidTh_ready)

                    for q in range(4):
                        hi(q)
                    for s, (which, e) in enumerate(SEGMENTS):
                        ahead = range(4 * s + 4, 4 * s + 8) if s < 11 else ()
                        for q in ahead[0:2]:
                            hi(q)
                        if which == 0 and e:
                            turned_hi(e - 1)
                        for q in ahead[2:3]:
                            hi(q)
                        if which == 0:
                            full(0, e)
                            signal(act.activation(hid[e % 2], PS[:, 0, :], ACT.Silu), bank_read[0])
                        for q in ahead[3:4]:
                            hi(q)
                        if s == 10:
                            if more:
                                signal(gathered_hi(5, i * TILE_JOBS[5] + (base[5] + 1)), xTh_ready)
                            turned_hi(3)
                            if more:
                                signal(gathered_hi(6, i * TILE_JOBS[6] + (base[6] + 1)), xTh_ready)
                    for half in range(2):
                        full(2 + half, 0)
                        signal(act.activation(group_sum[:, half, :], PS[:, 2 + half, :], ACT.Copy),
                               bank_read[2 + half])

                with act.Fori(0, NG) as i:
                    group_tile(i, True)
                largest, _ = counts(act)
                tally.clear()
                with act.If(largest > P):
                    group_tile(NG, False)
                with act.Else():
                    act.wait_ge(tiles_done, layer + 1)
                    for s, n in tally.values():
                        act.sem_inc(s, n)
                for b in range(8):
                    taken[b] = base[b] + NG * TILE_JOBS[b] + LAST_JOBS[b]
            norm(2 * LAYERS + 1, "final")

        @block.vector
        def _(dve):
            taken = [0] * 8
            steps = [0]

            def take(b):
                dve.wait_ge(bank_full[b], taken[b] + 1)

            def give(b):
                dve.sem_inc(bank_read[b], 1)
                taken[b] += 1

            def step(ins):
                steps[0] += 1
                ins.then_inc(v_step, 1)
                dve.wait_ge(v_step, steps[0])

            def tt(out, i0, i1, op):
                step(dve.tensor_tensor(out, i0, i1, op))

            def stt(out, i0, s, i1, op0, op1):
                step(dve.scalar_tensor_tensor(out=out, in0=i0, scalar=s, in1=i1, op0=op0, op1=op1))

            def ts(out, i0, s1, s2, op0, op1=None):
                if op1 is None:
                    step(dve.tensor_scalar(out, i0, s1, None, op0))
                else:
                    step(dve.tensor_scalar(out, i0, s1, s2, op0, op1))

            def heads(v):
                return v.rearrange("p (h d) -> p h d", d=HD)

            def per_head(v):
                return v.unsqueeze(2).to_broadcast([P, CH, HD])

            def norm(n, kind):
                for t in range(NT):
                    step(dve.scalar_tensor_tensor(out=h_nat[:, t, :], in0=x[:, t, :], scalar=1.0, in1=x[:, t, :],
                                                  op0=ALU.mult, op1=ALU.mult, accum_out=ss[:, t:t + 1]))
                dve.sem_inc(ss_ready, 1)
                dve.wait_ge(rms_ready, n)
                step(dve.reciprocal(rn, rn))
                for t in range(NT):
                    if kind == "router":
                        for half in range(2):
                            cols = slice(half * W, (half + 1) * W)
                            stt(h_nat[:, t, cols], x[:, t, cols], rn[:, t:t + 1], bc[:, FFG[half], :],
                                ALU.mult, ALU.mult)
                    else:
                        ts(h_nat[:, t, :], x[:, t, :], rn[:, t:t + 1], None, ALU.mult)
                if kind == "final":
                    return
                dve.sem_inc(hnat_ready, 1)
                for b in (4, 5):
                    take(b)
                    for i in range(2):
                        c = 2 * (b - 2) + i
                        src = PS[:, b, i * S:(i + 1) * S]
                        if kind == "mix":
                            ts(hT[:, c, :], src, vec[:, VG + c:VG + c + 1], None, ALU.mult)
                        else:
                            step(dve.tensor_copy(hT_router[:, c, :], src))
                    give(b)
                dve.sem_inc(hT_v, 1)

            dve.wait_ge(const_in, 48)
            step(dve.tensor_copy(small[:, 0:NT], pos_i[:]))
            tt(angle[:, 0, :].rearrange("p (t f) -> p t f", t=NT),
               small[:, 0:NT].unsqueeze(2).to_broadcast([P, NT, HALF]),
               const("freq").unsqueeze(1).to_broadcast([P, NT, HALF]), ALU.mult)
            for i, (turn, shift) in enumerate(((0.0, 0.0), (0.25, np.pi / 2))):
                n, r = angle[:, 1, :], angle[:, 2 + i, :]
                ts(n, angle[:, 0, :], 1.0 / (2 * np.pi), turn, ALU.mult, ALU.add)
                ts(n, n, ROUND, None, ALU.add)
                ts(n, n, -ROUND, None, ALU.add)
                stt(r, n, -TWO_PI[0], angle[:, 0, :], ALU.mult, ALU.add)
                for part in TWO_PI[1:]:
                    stt(r, n, -part, r, ALU.mult, ALU.add)
                ts(r, r, float(np.float32(shift)), float(np.float32(3.1415925)), ALU.add, ALU.min)
                ts(r, r, float(-np.float32(3.1415925)), None, ALU.max)
            dve.sem_inc(ang_ready, 1)

            for layer in range(LAYERS):
                take(4)
                step(dve.tensor_copy(vec[:], PS[:, 4, 0:52]))
                give(4)
                dve.sem_inc(vec_ready, 1)
                step(dve.memset(state[:], 0.0))
                norm(2 * layer + 1, "mix")
                dve.wait_ge(hT_a, 2 * layer + 1)
                dve.wait_ge(hTh_ready, layer + 1)
                step(dve.tensor_tensor(hTl[:], hT, hTh[:].bitcast(F32), ALU.subtract))
                dve.sem_inc(hTl_ready, 1)
                step(dve.tensor_tensor(dhT[:, :, 1:S], hT[:, :, 0:S - 1], hT[:, :, 1:S], ALU.subtract))
                ts(dhT[:, :, 0:1], hT[:, :, 0:1], -1.0, None, ALU.mult)
                for m in range(3 + layer):
                    if m >= 2:
                        dve.wait_ge(lora_ready, 3 * layer + m - 1)
                    for c in range(KC):
                        col = VMU + 8 * m + c
                        stt(mix[m % 2][:, c, :], dhT[:, c, :], vec[:, col:col + 1], hT[:, c, :], ALU.mult, ALU.add)
                    dve.sem_inc(mix_ready, 1)
                dve.wait_ge(bc_in, 6 * 16 * (layer + 1))
                r_, k_, v_ = (proj[:, :, c:c + W] for c in (R0, CK0, CV0))
                dve.wait_ge(zs_ready, 14 if layer else 6)
                for i, t_ in enumerate((r_, k_, v_)):
                    for t in (1, 0):
                        take(4 + t)
                        tt(kk[:, t, :], PS[:, 4 + t, :], bc[:, MU[i], :], ALU.mult)
                        give(4 + t)
                        tt(t_[:, t, :], t_[:, t, :], kk[:, t, :], ALU.add)
                if layer:
                    dve.wait_ge(vf_in, 16)
                    for t in range(NT):
                        tt(kk[:, t, :], v_old[:, t, :], v_[:, t, :], ALU.subtract)
                        tt(kk[:, t, :], kk[:, t, :], v_gate[:, t, :], ALU.mult)
                        tt(v_[:, t, :], v_[:, t, :], kk[:, t, :], ALU.add)
                dve.sem_inc(c_done, 1)
                take(6)
                step(dve.tensor_copy(F, PS[:, 6, 0:4]))
                give(6)
                dve.sem_inc(f_ready, 1)
                sq = view(1024, W)
                for t in range(NT):
                    tt(kk[:, t, :], k_[:, t, :], bc[:, KK_, :], ALU.mult)
                    tt(sq, kk[:, t, :], kk[:, t, :], ALU.mult)
                    step(dve.tensor_reduce(kn[:, t, :], heads(sq), AX_X, ALU.add))
                dve.sem_inc(ksq_ready, 1)
                for t in range(NT):
                    stt(sq, aa[:, t, :], -1.0, bc[:, KA_, :], ALU.add, ALU.mult)
                    stt(k_[:, t, :], sq, 1.0, k_[:, t, :], ALU.add, ALU.mult)
                    tt(sq, r_[:, t, :], k_[:, t, :], ALU.mult)
                    tt(sq, sq, bc[:, RK_, :], ALU.mult)
                    step(dve.tensor_reduce(bonus[:, t, :], heads(sq), AX_X, ALU.add))
                dve.wait_ge(knorm_ready, layer + 1)
                ts(kn, kn, 1e-12, None, ALU.max)
                step(dve.reciprocal(kn, kn))
                for t in range(NT):
                    tt(heads(kk[:, t, :]), heads(kk[:, t, :]), per_head(kn[:, t, :]), ALU.mult)
                    tt(aa[:, t, :], aa[:, t, :], kk[:, t, :], ALU.mult)
                    dve.wait_ge(exps_ready, layer * NT + t + 1)
                    tt(r_[:, t, :], r_[:, t, :], exps[t][0], ALU.mult)
                    tt(aa[:, t, :], aa[:, t, :], exps[t][1], ALU.mult)
                    tt(k_[:, t, :], k_[:, t, :], exps[t][1], ALU.mult)
                    tt(kk[:, t, :], kk[:, t, :], exps[t][2], ALU.mult)
                    dve.sem_inc(tilde_ready, 1)
                low2 = tab[:, CONST_AT["low_strict"][0]:CONST_AT["low_strict"][0] + 2 * P]
                low2 = low2.unsqueeze(1).to_broadcast([P, 2, 2 * P])
                idb = ident.unsqueeze(1).to_broadcast([P, 4, P])

                def group_norm(c):
                    y, t2 = kk[:, c, :], tmp[2]
                    yh = heads(y)
                    step(dve.tensor_reduce(gmu, yh, AX_X, ALU.add))
                    ts(gmu, gmu, 1.0 / HD, None, ALU.mult)
                    tt(yh, yh, per_head(gmu), ALU.subtract)
                    tt(t2, y, y, ALU.mult)
                    step(dve.tensor_reduce(gvar, heads(t2), AX_X, ALU.add))
                    dve.sem_inc(gvar_ready, 1)
                    dve.wait_ge(gstd_ready, layer * NT + c + 1)
                    step(dve.reciprocal(gvar, gvar))
                    tt(yh, yh, per_head(gvar), ALU.mult)
                    if c == 0:
                        dve.wait_ge(late_in, 6 * 16 * (layer + 1))
                    tt(y, y, bc[:, LNW, :], ALU.mult)
                    tt(y, y, bc[:, LNB, :], ALU.add)
                    tt(heads(t2), heads(v_[:, c, :]), per_head(bonus[:, c, :]), ALU.mult)
                    tt(y, y, t2, ALU.add)
                    tt(y, y, gg[:, c, :], ALU.mult)

                for c in range(NT):
                    g = layer * NT + c
                    for b, dst in ((4, krT[:, :, 0, :]), (5, krT[:, :, 1, :]), (6, bT), (7, kT_c)):
                        take(b)
                        step(dve.tensor_copy(dst, PS[:, b, :].rearrange("p (q t) -> p q t", q=4)))
                        give(b)
                    dve.sem_inc(crT_ready, 1)
                    if c:
                        group_norm(c - 1)
                    for half in range(2):
                        for b, dst, i in ((4, SCb, 0), (5, SCb, 1), (6, SCk, 0), (7, SCk, 1)):
                            take(b)
                            tt(dst[:, 4 * half + i:4 * half + 4:2, :, :].rearrange("p h a t -> p h (a t)"),
                               PS[:, b, :].rearrange("p (h x) -> p h x", h=2), low2, ALU.mult)
                            give(b)
                    dve.sem_inc(score_ready, 1)
                    dve.wait_ge(n_ready, g * LEVELS + 1)
                    for k in range(LEVELS):
                        for h in range(2):
                            hs = slice(4 * h, 4 * h + 4)
                            if k == 0:
                                tt(XT[:, hs, :], idb, Nl[0][:, hs, :], ALU.subtract)
                                take(4 + 2 * h)
                                tt(X[:, hs, :], idb, PS[:, 4 + 2 * h, :].rearrange("p (h t) -> p h t", h=4),
                                   ALU.subtract)
                                give(4 + 2 * h)
                            else:
                                bs = (4 + 2 * h, 5 + 2 * h) if k < LEVELS - 1 else (4 + 2 * h,)
                                for b in bs:
                                    take(b)
                                for b, m in zip(bs, (XT, X)):
                                    tt(m[:, hs, :], m[:, hs, :], PS[:, b, :].rearrange("p (h t) -> p h t", h=4),
                                       ALU.subtract)
                                    give(b)
                            dve.sem_inc(xt_ready, 1)
                    take(4)
                    y = kk[:, c, :]
                    step(dve.tensor_copy(y, PS[:, 4, :]))
                    give(4)
                    if c == 0:
                        take(5)
                        dve.wait_ge(f_exp, layer + 1)
                        for i in range(2):
                            s64 = slice(64 * i, 64 * i + 64)
                            tt(state[s64, :, s64], PS[s64, 5, :].rearrange("p (q v) -> p q v", q=4)[:, :, s64],
                               F[s64, :].unsqueeze(2).to_broadcast([64, 4, 64]), ALU.mult)
                        give(5)
                        dve.sem_inc(state_ready, 1)
                group_norm(NT - 1)
                dve.sem_inc(yc_ready, 1)
                if layer == 0:
                    dve.wait_ge(sin_ready, 1)
                dve.wait_ge(rest_ready, 2 * len(REST) * layer + REST_QKV)
                t1b, t2b = (tmp[i][:, 0:24 * HALF].rearrange("p (h f) -> p h f", f=HALF) for i in range(2))
                t3b, t4b = (tmp[i][:, 256:256 + 24 * HALF].rearrange("p (h f) -> p h f", f=HALF) for i in range(2))
                for t in range(NT):
                    qk = proj[:, t, Q0:VB0].rearrange("p (h d) -> p h d", d=HD)
                    lo_, hi_ = qk[:, :, 0:HALF], qk[:, :, HALF:2 * HALF]
                    sin = angle[:, 4, t * HALF:(t + 1) * HALF].unsqueeze(1).to_broadcast([P, 24, HALF])
                    cos = angle[:, 5, t * HALF:(t + 1) * HALF].unsqueeze(1).to_broadcast([P, 24, HALF])
                    tt(t1b, lo_, cos, ALU.mult)
                    tt(t2b, hi_, sin, ALU.mult)
                    tt(t3b, hi_, cos, ALU.mult)
                    tt(t4b, lo_, sin, ALU.mult)
                    tt(lo_, t1b, t2b, ALU.subtract)
                    tt(hi_, t3b, t4b, ALU.add)
                dve.sem_inc(rot_ready, 1)
                n_jobs = NT * BHG
                at, _ = CONST_AT["attend"]
                masks = tab[:, at:at + 3 * 2 * P].rearrange("p (g k) -> p g k", g=3)

                def scores(job):
                    t = job % NT
                    g = layer * n_jobs + job
                    n = (t + 1) * P
                    if job >= 2:
                        dve.wait_ge(pT_ready, g - 1)
                    for b, g0, g1 in ((4, 0, 2), (5, 2, 3)):
                        take(b)
                        stt(prob[g % 2][:, g0 * n:g1 * n].rearrange("p (g k) -> p g k", k=n),
                            PS[:, b, 0:(g1 - g0) * n].rearrange("p (g k) -> p g k", k=n), HD ** -0.5,
                            masks[:, g0:g1, 2 * P - n:2 * P], ALU.mult, ALU.add)
                        give(b)
                    nm = nmax[:, g % 2:g % 2 + 1]
                    step(dve.tensor_reduce(nm, prob[g % 2][:, 0:3 * n], AX_X, ALU.max))
                    ts(nm, nm, -1.0, None, ALU.mult)
                    dve.sem_inc(p_ready, 1)

                def values(job):
                    head, t = job // NT, job % NT
                    g = layer * n_jobs + job
                    b = 6 + g % 2
                    take(b)
                    d = den[:, g % 2:g % 2 + 1]
                    step(dve.reciprocal(d, d))
                    ts(yb[:, t, head * HD:(head + 1) * HD], PS[:, b, 0:HD], d, None, ALU.mult)
                    give(b)

                scores(0)
                for job in range(n_jobs):
                    if job + 1 < n_jobs:
                        scores(job + 1)
                    values(job)
                dve.sem_inc(yb_ready, 1)
                dve.wait_ge(rest_ready, 2 * len(REST) * (layer + 1))
                take(4)
                inc = const("low_incl").unsqueeze(1).to_broadcast([P, AG, P])
                tt(wsT, PS[:, 4, :].rearrange("p (g t) -> p g t", g=AG), inc, ALU.mult)
                give(4)
                for t in range(NT):
                    v = proj[:, t, V0:V0 + W]
                    step(dve.bn_stats(bst, v))
                    step(dve.bn_aggr(bag, bst))
                    dve.sem_inc(ln_ready, 1)
                    dve.wait_ge(lsd_ready, layer * NT + t + 1)
                    step(dve.reciprocal(lrs, lrs))
                    step(dve.tensor_scalar(vn, v, bag[:, 0:1], lrs, ALU.subtract, ALU.mult))
                    tt(vn, vn, bc[:, GLG, :], ALU.mult)
                    tt(vn, vn, bc[:, GLB, :], ALU.add)
                    dve.sem_inc(vn_ready, 1)
                    take(5)
                    for g in range(AG):
                        u = proj[:, t, U0 + g * P:U0 + (g + 1) * P]
                        stt(u, PS[:, 5, g * P:(g + 1) * P], vec[:, VBS + g:VBS + g + 1], u, ALU.add, ALU.mult)
                    give(5)
                dve.sem_inc(ya_ready, 1)
                dve.wait_ge(yT_ready, 5 * (layer + 1))
                for br in range(3):
                    for half in range(2):
                        for t in range(NT):
                            i = 4 * br + 2 * half + t
                            g = 12 * layer + i
                            dve.wait_ge(gate_ready, g + 1)
                            take(4 + t)
                            m = merged[:, t, half * W:(half + 1) * W]
                            tt(tmp[t] if br else m, gate[2 * br + half][:, t, :], PS[:, 4 + t, :], ALU.mult)
                            give(4 + t)
                            if br:
                                tt(m, m, tmp[t], ALU.add)
                dve.sem_inc(merged_ready, 1)
                for q in range(4):
                    b = 2 + q % 2
                    dve.wait_ge(mTh_ready, 4 * layer + q + 1)
                    step(dve.tensor_tensor(hTl[:, 2 * q:2 * q + 2, :], PS[:, b, :].rearrange("p (c t) -> p c t", c=2),
                                           hTh[:, 2 * q:2 * q + 2, :].bitcast(F32), ALU.subtract))
                    dve.sem_inc(bank_read[b], 1)
                for half in range(2):
                    for t in range(NT):
                        take(4 + t)
                        xs = x[:, t, half * W:(half + 1) * W]
                        tt(xs, xs, PS[:, 4 + t, :], ALU.add)
                        give(4 + t)
                norm(2 * layer + 2, "router")
                lg = rt[:, 0:40].rearrange("p (t n) -> p t n", t=NT)
                for t in range(NT):
                    take(6 + t)
                    step(dve.tensor_copy(lg[:, t, :], PS[:, 6 + t, 0:20]))
                    give(6 + t)
                dve.sem_inc(gains_used, 1)
                ex = rt[:, 40:50].rearrange("p (t n) -> p t n", t=NT)
                mg = rt[:, 50:52].rearrange("p (t n) -> p t n", t=NT)
                mx = rt[:, 52:54].rearrange("p (t n) -> p t n", t=NT)
                one = [hot] + [rt[:, 64 + 8 * i:72 + 8 * i].rearrange("p (t n) -> p t n", t=NT) for i in range(2)]
                pick = rt[:, 80:88].rearrange("p (t n) -> p t n", t=NT)
                m12 = [rt[:, 88 + 2 * i:90 + 2 * i].rearrange("p (t n) -> p t n", t=NT) for i in range(2)]
                prod = rt[:, 96:128].rearrange("p (t g n) -> p t g n", t=NT, g=NG)
                den2 = rt[:, 128:130].rearrange("p (t n) -> p t n", t=NT)
                gpr = rt[:, 130:132].rearrange("p (t n) -> p t n", t=NT)
                ranks = rt[:, 132:140].rearrange("p (t n) -> p t n", t=NT)
                total, big, over = rt[:, 140:144], rt[:, 144:148], rt[:, 148:150]
                place3, over3 = place.unsqueeze(2), over.unsqueeze(2)
                plan_f = rt[:, 152:154]
                fb = const("first").unsqueeze(1).to_broadcast([P, NT, 4])

                def choose(hot_, vals, top):
                    step(dve.tensor_reduce(top, vals, AX_X, ALU.max))
                    tt(hot_, vals, top.to_broadcast([P, NT, 4]), ALU.is_equal)
                    tt(hot_, hot_, fb, ALU.mult)
                    step(dve.tensor_reduce(mx, hot_, AX_X, ALU.max))
                    tt(hot_, hot_, mx.to_broadcast([P, NT, 4]), ALU.is_equal)

                choose(one[0], lg[:, :, 0:4], mg)
                dve.sem_inc(g_ready, 1)
                tt(ex[:, :, 0:4], lg[:, :, 0:4], mg.to_broadcast([P, NT, 4]), ALU.subtract)
                take(4)
                step(dve.tensor_copy(rt[:, 132:144], PS[:, 4, 0:12]))
                give(4)
                tt(ranks, ranks, hot, ALU.mult)
                step(dve.tensor_reduce(place3, ranks, AX_X, ALU.add))
                ts(over, place, float(P), None, ALU.is_ge)
                stt(place, over, -float(P), place, ALU.mult, ALU.add)
                step(dve.tensor_copy(inside[:, :, NG:NG + 1], over3))
                ts(over, over, -1.0, 1.0, ALU.mult, ALU.add)
                tt(inside[:, :, 0:NG], hot, over3.to_broadcast([P, NT, NG]), ALU.mult)
                step(dve.tensor_reduce(plan_f[:, 0:1], total, AX_X, ALU.max))
                ts(big, total, float(P), None, ALU.is_gt)
                tt(big, big, const("index"), ALU.mult)
                step(dve.tensor_reduce(plan_f[:, 1:2], big, AX_X, ALU.max))
                step(dve.tensor_copy(plan_i[:], plan_f))
                dve.sem_inc(plan_ready, 1)
                spot = const("place")

                def pick_tile(b):
                    for t in range(NT):
                        ins = dve.tensor_scalar(pick01[:, t, :], spot, place[:, t:t + 1], inside[:, t, bass.ds(b, 1)],
                                                ALU.is_equal, ALU.mult)
                    return ins

                step(pick_tile(0))
                for t in range(NT):
                    tt(prod[:, t], lg[:, t, 4:20].rearrange("p (g n) -> p g n", g=NG),
                       one[0][:, t, :].unsqueeze(2).to_broadcast([P, NG, 4]), ALU.mult)
                    step(dve.tensor_reduce(pick[:, t, :], prod[:, t].rearrange("p g n -> p n g"), AX_X, ALU.add))
                choose(one[1], pick, m12[0])
                stt(pick.rearrange("p t n -> p (t n)"), one[1].rearrange("p t n -> p (t n)"), NEG,
                    pick.rearrange("p t n -> p (t n)"), ALU.mult, ALU.add)
                choose(one[2], pick, m12[1])
                tt(ex[:, :, 4:5], m12[1], m12[0], ALU.subtract)
                dve.sem_inc(logit_ready, 1)
                dve.wait_ge(rexp_ready, layer + 1)
                step(dve.tensor_reduce(gpr, ex[:, :, 0:4], AX_X, ALU.add))
                ts(den2, ex[:, :, 4:5], 1.0, None, ALU.add)
                tt(gpr, gpr, den2, ALU.mult)
                step(dve.reciprocal(gpr, gpr))
                tt(one[2], one[2], ex[:, :, 4:5].to_broadcast([P, NT, 4]), ALU.mult)
                tt(one[1], one[1], one[2], ALU.add)
                tt(own, one[1], gpr.to_broadcast([P, NT, 4]), ALU.mult)
                dve.sem_inc(pick_ready, 1)
                exp_ = PLAN.experts[layer]
                base = at_experts[layer]

                def gathered_lo(b, value):
                    dve.wait_ge(xTh_ready, value)
                    c = 4 * (b - 5)
                    return dve.tensor_tensor(xTl[:, c:c + 4, :], PS[:, b, :].rearrange("p (c t) -> p c t", c=4),
                                             xTh[:, c:c + 4, :].bitcast(F32), ALU.subtract)

                x0 = layer * 2 * (NG + 1)
                for b in (5, 6):
                    gathered_lo(b, x0 + b - 4).then_inc(bank_read[b], 1)
                dve.wait_ge(bank_full[7], base[7])
                dve.tensor_copy(weight, PS[:, 7, 0:EPG]).then_inc(bank_read[7], 1)
                tally = {}

                def signal(ins, s):
                    ins.then_inc(s, 1)
                    tally[s.name] = (s, tally.get(s.name, (s, 0))[1] + 1)

                def group_tile(i, more):
                    def full(b, n):
                        dve.wait_ge(bank_full[b], i * TILE_JOBS[b] + (base[b] + n + 1))

                    def lo(q):
                        if q % 3 == 2:
                            return
                        w = (exp_["pieces"] + q) % HL
                        dve.wait_ge(hi_ready, i * EXPERT_PIECES + (exp_["pieces"] + q + 1))
                        signal(dve.tensor_tensor(pieces_of(wl[:, w, :], q), raw_piece(exp_, q),
                                                 pieces_of(wh[:, w, :].bitcast(F32), q), ALU.subtract), lo_v)

                    def turned_lo(e):
                        dve.wait_ge(hidTh_ready, i * EPG + (layer * EPG * (NG + 1) + e + 1))
                        signal(dve.tensor_tensor(hidTl[:], PS[:, 1, :].rearrange("p (c t) -> p c t", c=4),
                                                 hidTh[:].bitcast(F32), ALU.subtract), bank_read[1])

                    for q in range(4):
                        lo(q)
                    full(7, 0)
                    signal(dve.tensor_copy(pickT, PS[:, 7, 0:NT * P].rearrange("p (t n) -> p t n", t=NT)),
                           bank_read[7])
                    if more:
                        signal(pick_tile(i + 1), pick_ready)
                    for s, (which, e) in enumerate(SEGMENTS):
                        ahead = range(4 * s + 4, 4 * s + 8) if s < 11 else ()
                        for q in ahead[0:2]:
                            lo(q)
                        if which == 0 and e:
                            turned_lo(e - 1)
                        for q in ahead[2:3]:
                            lo(q)
                        if which == 1:
                            full(4, e)
                            dve.wait_ge(bank_read[0], i * TILE_JOBS[0] + (base[0] + e + 1))
                            if e == 0:
                                dve.wait_ge(bank_read[7], i * TILE_JOBS[7] + base[7])
                            signal(dve.scalar_tensor_tensor(out=hid[e % 2], in0=PS[:, 4, :], scalar=weight[:, e:e + 1],
                                                            in1=hid[e % 2], op0=ALU.mult, op1=ALU.mult), bank_read[4])
                        for q in ahead[3:4]:
                            lo(q)
                        if s == 10:
                            if more:
                                signal(gathered_lo(5, i * 2 + (x0 + 3)), bank_read[5])
                            turned_lo(3)
                            if more:
                                signal(gathered_lo(6, i * 2 + (x0 + 4)), bank_read[6])
                                full(7, 1)
                                signal(dve.tensor_copy(weight, PS[:, 7, 0:EPG]), bank_read[7])
                    for n, b in enumerate((7, 5, 6, 4)):
                        t, half = n // 2, n % 2
                        full(b, {7: 2, 5: 1, 6: 1, 4: 4}[b] if more else {7: 1, 5: 0, 6: 0, 4: 4}[b])
                        xs = x[:, t, half * W:(half + 1) * W]
                        signal(dve.tensor_tensor(xs, xs, PS[:, b, :], ALU.add), bank_read[b])

                with dve.Fori(0, NG) as i:
                    group_tile(i, True)
                dve.wait_ge(bank_read[4], base[4] + NG * TILE_JOBS[4])
                dve.sem_inc(tiles_done, 1)
                largest, _ = counts(dve)
                tally.clear()
                with dve.If(largest > P):
                    group_tile(NG, False)
                with dve.Else():
                    for s, n in tally.values():
                        dve.sem_inc(s, n)
                for b in range(8):
                    taken[b] = base[b] + NG * TILE_JOBS[b] + LAST_JOBS[b]
                dve.wait_ge(bank_read[4], taken[4])
            norm(2 * LAYERS + 1, "final")
            dve.wait_ge(fin_in, 16)
            fg = bc[:, 0:2, :].rearrange("p a n -> p (a n)")
            for t in range(NT):
                tt(h_nat[:, t, :], h_nat[:, t, :], fg, ALU.mult)
            dve.sem_inc(fin_done, 1)


_INS = ['x', 'positions', 'norm_mix_g', 'w_in', 'gmlp_ln_g', 'gmlp_ln_b', 'gmlp_ws', 'gmlp_bs', 'rwkv_mu_rkv',
        'rwkv_mu_wag', 'rwkv_w0', 'rwkv_w1', 'rwkv_w2', 'rwkv_a0', 'rwkv_a1', 'rwkv_a2', 'rwkv_g1', 'rwkv_g2',
        'rwkv_k_k', 'rwkv_k_a', 'rwkv_r_k', 'rwkv_ln_w', 'rwkv_ln_b', 'rwkv_mu_v', 'rwkv_v0', 'rwkv_v1', 'rwkv_v2',
        'w_branch_a', 'w_branch_b', 'w_branch_c', 'w_gate', 'b_gate', 'w_out', 'norm_ffn_g', 'router_group_w',
        'router_group_b', 'router_expert_w', 'router_expert_b', 'expert_w_gate', 'expert_w_up', 'expert_w_down',
        'final_norm_g']


def kernel(**inputs):
    import numpy as _np
    import concourse.bacc as _bacc
    from concourse import mybir as _mybir
    from concourse.bass_utils import run_bass_kernel_spmd as _run

    nc = _bacc.Bacc("TRN2", target_bir_lowering=False, num_devices=1)
    given = {name: _np.ascontiguousarray(inputs[name]) for name in _INS}
    given["table"] = TABLE
    arrays, args = {}, {}
    for name, v in given.items():
        arrays[f"in_{name}"] = v
        args[name] = nc.dram_tensor(f"in_{name}", v.shape, _mybir.dt.from_np(v.dtype), kind="ExternalInput").ap()
    args["out"] = nc.dram_tensor("out_0", (1, S, D), F32, kind="ExternalOutput").ap()
    hybrid_moe_kernel(nc, args)
    r = _run(nc, [arrays], core_ids=[0])
    return r.results[0]["out_0"]
```

```python
from contextlib import ExitStack

import numpy as np

import concourse.bass as bass
from concourse import mybir

F32 = mybir.dt.float32
F32R = mybir.dt.float32r
I32 = mybir.dt.int32
ACT = mybir.ActivationFunctionType
ALU = mybir.AluOpType
AX_X = mybir.AxisListType.X

P = 128
S = 256
NT = S // P
D = 1024
KC = D // P
W = 512
LAYERS = 2
HD = 64
AG = 4
BHG = 4
CH = 8
NG = 4
EPG = 4
HALF = 8
DECAY = float(np.float32(np.exp(-0.5)))
NEG = -1e30
ROUND = 12582912.0
LEVELS = 7

U0, V0, Q0, K0, VB0, R0, CK0, CV0, PCOLS = 0, 512, 1024, 1792, 2560, 3328, 3840, 4352, 4864

CONST_AT = {}


def constants():
    j = np.arange(P)[:, None]
    t = np.arange(P)[None, :]
    mid = (j < P // 2).astype(np.float64)
    freq = 500000.0 ** (-np.arange(HALF) / HALF)
    parts = {
        "ident": (j == t),
        "eps_rms": np.full((P, 1), 1e-6),
        "eps_ln": np.full((P, 1), 1e-5),
        "eps_gn": np.full((P, 1), HD * 1e-5),
        "decay_incl": -DECAY * ((j <= t) - mid),
        "decay_prev": -DECAY * ((j < t) - mid),
        "shift": (j == t - 1).astype(float) - (j == t),
        "edge": (j == P - 1) & (t == 0),
        "low_strict": (j < t),
        "low_incl": (j <= t),
        "after_mid": -DECAY * (1 - mid),
        "before_mid": -DECAY * mid,
    }
    for k in range(LEVELS):
        n = 1 << k
        parts[f"level{k}"] = (j // (2 * n) == t // (2 * n)) & (j % (2 * n) < n) & (t % (2 * n) >= n)
    rows = []
    for window, dil in ((128, 1), (512, 4), (2048, 16)):
        away = j + P - np.arange(2 * P)[None, :]
        rows.append(np.where((away >= 0) & (away <= window) & (away % dil == 0), 0.0, NEG))
    parts["attend"] = np.concatenate(rows, 1)
    parts["ones"] = np.ones((P, P))
    parts["index"] = np.broadcast_to(np.arange(4), (P, 4))
    parts["place"] = np.broadcast_to(np.arange(P), (P, P))
    parts["first"] = np.broadcast_to(4.0 - np.arange(4), (P, 4))
    parts["freq"] = np.broadcast_to(freq, (P, HALF))
    at = 0
    for name, a in parts.items():
        CONST_AT[name] = (at, a.shape[1])
        at += a.shape[1]
    table = np.concatenate([np.asarray(a, np.float64) for a in parts.values()], 1).astype(np.float32)
    return table


TABLE = constants()
FIRST_COLS = P + 3


def two_pi_parts():
    left, parts = 2 * np.pi, []
    for _ in range(3):
        e = np.floor(np.log2(left))
        p = np.floor(left / 2 ** (e - 7)) * 2 ** (e - 7)
        parts.append(float(p))
        left -= p
    return parts + [float(np.float32(left))]


TWO_PI = two_pi_parts()


PIECE = 1024
LOAD = 2 * PIECE
RING = 3
HL = 4
EXPERT_LOADS = 24
EXPERT_PIECES = 48
SEGMENTS = [(0, 0), (1, 0), (0, 1), (2, 0), (1, 1), (0, 2), (2, 1), (1, 2), (0, 3), (2, 2), (1, 3), (2, 3)]


def straight_loads():
    blocks = [("w_in", R0, W), ("w_in", CK0, W), ("w_in", CV0, W)]
    rest = [("w_in", c, min(W, R0 - c)) for c in range(Q0, R0, W)]
    rest = rest[:-2] + [rest[-1], rest[-2]] + [("w_in", c, W) for c in (U0, V0)]
    loads = []

    def dense(b):
        loads.extend(("dense", (*b, j), b[2] * 4 // PIECE) for j in range(2))

    for b in blocks:
        dense(b)
    loads += [("lora1", (0,), 0), ("lora1", (1,), 0), ("lora2", (), 0)]
    for b in rest:
        dense(b)
    for k in range(4):
        dense(("w_gate", k * W, W))
    for br in range(3):
        if br:
            dense(("w_gate", (br + 3) * W, W))
        for half in range(2):
            loads.append(("branch", (br, half), (2, 1, 2)[br]))
    for half in range(2):
        dense(("w_out", half * W, W))
    return loads


LOADS = straight_loads()
REST = [a[1:3] for k, a, _ in LOADS if k == "dense" and a[0] == "w_in" and a[3] == 0][3:]
DMAS = {"lora1": 4, "lora2": 4}


def lo_counts(q):
    return (q + 2) // 3, q - (q + 2) // 3


CHUNK_BLOCKS = (len(REST) - 3, len(REST) - 2)
REST_QKV = 2 * (len(REST) - 2)
BLOCK_ORDER = {"time": range(0, 3), "rest": range(3, 3 + len(REST)), "gate": range(3 + len(REST), 9 + len(REST)),
               "out": range(9 + len(REST), 11 + len(REST))}
TILE_FULL = {0: 0, 1: 4, 2: 0, 3: 0, 4: 1, 5: 2, 6: 2, 7: 3}
LAST_FULL = {0: 0, 1: 4, 2: 0, 3: 0, 4: 1, 5: 1, 6: 2, 7: 2}
TILE_JOBS = {0: 4, 1: 4, 2: 1, 3: 1, 4: 5, 5: 2, 6: 2, 7: 3}
LAST_JOBS = {0: 4, 1: 4, 2: 1, 3: 1, 4: 5, 5: 1, 6: 2, 7: 2}


class Plan:

    def __init__(self):
        self.loads, self.blocks, self.branches, self.experts, self.piece_at = [], [], [], [], []
        landed = [0] * (2 * RING)
        pieces = lo_p = lo_v = raw = 0
        n = 0
        freed = [None] * RING
        for layer in range(LAYERS):
            rows, blocks, branches = [], [], []
            for kind, arg, np_ in LOADS:
                slot = n % RING
                n += 1
                landed[slot] += 16 * DMAS.get(kind, 1)
                if np_:
                    if kind == "branch":
                        branches.append([W, pieces, pieces + np_])
                    elif arg[3] == 0:
                        blocks.append([arg[2], pieces, pieces + 2 * np_])
                    row = dict(kind=kind, arg=arg, slot=slot, landed=landed[slot], wait=freed[slot])
                    for i in range(np_):
                        self.piece_at.append((slot, landed[slot], i))
                    pieces += np_
                    lo_p += np_
                    freed[slot] = [("lo_p", lo_p)]
                else:
                    row = dict(kind=kind, arg=arg, slot=slot, landed=landed[slot], wait=freed[slot])
                    raw += 1
                    freed[slot] = [("raw_used", raw)]
                rows.append(row)
            self.loads.append(rows)
            self.blocks.append(blocks)
            self.branches.append(branches)
            slots = [(n + k) % RING for k in range(RING)] + [RING, RING + 1, RING + 2]
            self.experts.append(dict(slots=slots, landed=list(landed), pieces=pieces, lo_p=lo_p, lo_v=lo_v))
            for k in range(2 * RING):
                landed[k] += 16 * 4 * (NG + 1)
            pieces += EXPERT_PIECES * (NG + 1)
            self.piece_at += [None] * (EXPERT_PIECES * (NG + 1))
            lo_p += lo_counts(EXPERT_PIECES)[0] * (NG + 1)
            lo_v += lo_counts(EXPERT_PIECES)[1] * (NG + 1)
            freed = [[("lo_p", lo_p), ("lo_v", lo_v)]] * RING


PLAN = Plan()


def raw_slot(ring, proj, slot):
    if slot < RING:
        return ring[:, slot, :]
    flat = proj[:].rearrange("p t n -> p (t n)")
    return flat[:, (slot - RING) * LOAD:(slot - RING + 1) * LOAD]


def hybrid_moe_kernel(nc, a):
    ctx = ExitStack()
    with ctx:
        def sb(name, shape, dt=F32):
            return ctx.enter_context(nc.sbuf_tensor(name, shape, dt))

        def sem(name):
            return ctx.enter_context(nc.semaphore(name))

        x = sb("x_res", [P, NT, D])
        hTh = sb("hTh", [P, KC, S], F32R)
        hTl = sb("hTl", [P, KC, S], F32R)
        ring = sb("ring", [P, RING, LOAD])
        wh = sb("wh", [P, HL, PIECE], F32R)
        wl = sb("wl", [P, HL, PIECE], F32R)
        proj = sb("proj", [P, NT, PCOLS])
        tab = sb("tab", [P, TABLE.shape[1]])
        at_arena = (nc.sbuf_base + 31) // 32 * 32
        arena = sb("arena", [P, 9216])
        arena_r = nc.alloc_sbuf_tensor_at("arena_r", [P, 9216], F32R, offset=at_arena)
        lw = sb("lw", [P, NT, W])
        aa = sb("aa", [P, NT, W])
        gg = sb("gg", [P, NT, W])
        kk = sb("kk", [P, NT, W])
        at_krT = (nc.sbuf_base + 31) // 32 * 32
        krT = sb("krT", [P, 4, 2, P])
        hidTh = nc.alloc_sbuf_tensor_at("hidTh", [P, 4, P], F32R, offset=at_krT)
        hidTl = nc.alloc_sbuf_tensor_at("hidTl", [P, 4, P], F32R, offset=at_krT + 4 * W)
        tmp2 = sb("tmp2", [P, W])
        tmp = [lw[:, 0, :], lw[:, 1, :], tmp2[:]]
        bc = sb("bc", [P, 6, W])
        state = sb("state", [P, 4, P])
        bias_rows = sb("bias_rows", [32, W])
        bias_parts = sb("bias_parts", [64, W], F32R)
        selector = sb("selector", [64, 10], F32R)
        vec_rows = state[0:52, 0, :]
        vec = sb("vec", [P, 52])
        rw = sb("rw", [P, KC, 20])
        pos_i = sb("pos_i", [P, NT], I32)
        small = sb("small", [P, 256])
        angle = sb("angle", [P, 6, NT * HALF])
        plan_i = sb("plan_i", [P, 2], I32)
        v_first = nc.dram_tensor("v_first", [P, NT, W], F32, kind="Internal").ap()

        PS = ctx.enter_context(nc.psum_tensor("PS", [P, 8, W], F32))

        def const(name):
            at, n = CONST_AT[name]
            return tab[:, at:at + n]

        ident = const("ident")

        def view(at, *shape, of=arena):
            n = int(np.prod(shape))
            v = of[:, at:at + n]
            if len(shape) == 1:
                return v
            names = "abcd"[:len(shape)]
            return v.rearrange(f"p ({' '.join(names)}) -> p {' '.join(names)}",
                               **{k: s for k, s in zip(names[1:], shape[1:])})

        h_nat = view(0, NT, D)
        dhT = view(0, KC, S)
        mix = [view(2048, KC, S), view(4096, KC, S)]
        loraT = [view(6144 + 256 * m, S) for m in range(4)]
        hT = view(7168, KC, S)
        v_gate = view(2048, NT, W)
        v_old = view(0, NT, W)
        exps = [[view(4096 + 1536 * t + W * i, W) for i in range(3)] for t in range(NT)]
        SCb, SCk = view(0, CH, 2, P), view(2048, CH, 2, P)
        X, XT = view(4096, CH, P), view(5120, CH, P)
        Yl = view(6144, CH, P)
        bT, kT_c = view(6144, 4, P), view(6656, 4, P)
        Nl = [view(7168, CH, P), view(8192, CH, P)]
        qT, kT = view(0, 6, S), view(1536, 6, S)
        prob = [view(3072, 768), view(3840, 768)]
        probT = [view(4608, 6, P), view(5376, 6, P)]
        ws = view(6144, AG, P)
        wsT = view(6656, AG, P)
        yb = view(7168, NT, 256)
        vn = view(7680, W)
        yT_hi = [view(0, 4, S, of=arena_r), view(1024, 2, S, of=arena_r), view(1536, 4, S, of=arena_r)]
        yT_lo = [view(4608, 4, S, of=arena_r), view(7680, 2, S, of=arena_r), view(5632, 4, S, of=arena_r)]
        merged = view(2560, NT, D)
        gate = [proj[:, :, R0:R0 + W], proj[:, :, CK0:CK0 + W], proj[:, :, CV0:CV0 + W], aa, gg, view(6656, NT, W)]
        hT_router = view(2048, KC, S)
        hid = [view(2048, W), view(2560, W)]
        pickT = view(3072, NT, P)
        pick01 = view(3328, NT, P)
        group_sum = view(3584, NT, W)

        xTh = hTh[:, 0:4, :].rearrange("p a (b n) -> p (a b) n", b=2)
        xTl = hTl[:, 0:4, :].rearrange("p a (b n) -> p (a b) n", b=2)
        HALF_COLS = P // 2

        def side_of(v, k, side):
            return v.rearrange("p (a b r) -> p a b r", b=2, r=2 ** k)[:, :, side, :]

        def side_of_heads(v, k, side):
            return v.rearrange("p h (a b r) -> p h a b r", b=2, r=2 ** k)[:, :, :, side, :]

        at_experts = []

        def raw_piece(ex, q):
            r = raw_slot(ring, proj, ex["slots"][q // 2 % (2 * RING)])
            if SEGMENTS[q // 4][0] < 2:
                return r[:, (q % 2) * PIECE:(q % 2 + 1) * PIECE]
            return r.rearrange("p (c n) -> p c n", c=2)[:, :, (q % 2) * W:(q % 2 + 1) * W]

        def pieces_of(v, q):
            return v if SEGMENTS[q // 4][0] < 2 else v.rearrange("p (c n) -> p c n", c=2)

        ss, rn = small[:, 0:2], small[:, 2:4]
        kn = small[:, 4:20].rearrange("p (t h) -> p t h", t=NT)
        bonus = small[:, 20:36].rearrange("p (t h) -> p t h", t=NT)
        F = small[:, 36:40]
        gmu = small[:, 40:48]
        gvar = small[:, 48:56]
        nmax = small[:, 56:58]
        den = small[:, 58:60]
        bst, bag = small[:, 60:66], small[:, 66:68]
        lrs = small[:, 68:69]
        own = small[:, 72:80].rearrange("p (t n) -> p t n", t=NT)
        weight = small[:, 80:84]
        place = small[:, 84:86]
        inside = small[:, 86:96].rearrange("p (t b) -> p t b", t=NT)
        rt = small[:, 96:255]
        spare = small[:, 255:256]
        hot = rt[:, 56:64].rearrange("p (t n) -> p t n", t=NT)

        VG, VMU, VFFN, VBS = 0, 8, 40, 48
        MU, KK_, KA_, RK_ = (0, 1, 2), 3, 4, 5
        LNW, LNB, GLG, GLB, FFG = 0, 1, 3, 4, (2, 5)

        bank_full = [sem(f"bank_full{b}") for b in range(8)]
        bank_read = [sem(f"bank_read{b}") for b in range(8)]
        landed = [sem(f"landed{r}") for r in range(2 * RING)]
        hi_ready = sem("hi_ready")
        lo_p = sem("lo_p")
        lo_v = sem("lo_v")
        piece_used = sem("piece_used")
        raw_used = sem("raw_used")
        vf_out = sem("vf_out")
        vf_in = sem("vf_in")
        hTh_ready = sem("hTh_ready")
        hTl_ready = sem("hTl_ready")
        plan_ready = sem("plan_ready")
        pick_ready = sem("pick_ready")
        own_ready = sem("own_ready")
        x_ready = sem("x_ready")
        rn_ready = sem("rn_ready")
        hnat_a = sem("hnat_a")
        xTh_ready = sem("xTh_ready")
        g_ready = sem("g_ready")
        exps_ready = sem("exps_ready")
        hidTh_ready = sem("hidTh_ready")
        mTh_ready = sem("mTh_ready")
        stream = {"lo_p": lo_p, "lo_v": lo_v, "raw_used": raw_used}
        x_in = sem("x_in")
        const_in = sem("const_in")
        table_in = sem("table_in")
        rows_in = sem("rows_in")
        rows_clear = sem("rows_clear")
        bias_hi = sem("bias_hi")
        bias_lo = sem("bias_lo")
        bc_in = sem("bc_in")
        late_in = sem("late_in")
        rw_in = sem("rw_in")
        ws_in = sem("ws_in")
        fin_in = sem("fin_in")
        out_done = sem("out_done")
        v_step = sem("v_step")
        a_step = sem("a_step")
        vec_ready = sem("vec_ready")
        ss_ready = sem("ss_ready")
        rms_ready = sem("rms_ready")
        hnat_ready = sem("hnat_ready")
        hT_v = sem("hT_v")
        hT_a = sem("hT_a")
        mix_ready = sem("mix_ready")
        lora_ready = sem("lora_ready")
        zs_ready = sem("zs_ready")
        rkv_ready = sem("rkv_ready")
        rest_ready = sem("rest_ready")
        ksq_ready = sem("ksq_ready")
        knorm_ready = sem("knorm_ready")
        f_ready = sem("f_ready")
        f_exp = sem("f_exp")
        tilde_ready = sem("tilde_ready")
        crT_ready = sem("crT_ready")
        score_ready = sem("score_ready")
        n_ready = sem("n_ready")
        xt_ready = sem("xt_ready")
        y_ready = sem("y_ready")
        r_ready = sem("r_ready")
        sa_ready = sem("sa_ready")
        state_ready = sem("state_ready")
        gvar_ready = sem("gvar_ready")
        gstd_ready = sem("gstd_ready")
        rot_ready = sem("rot_ready")
        ang_ready = sem("ang_ready")
        sin_ready = sem("sin_ready")
        qkT_ready = sem("qkT_ready")
        p_ready = sem("p_ready")
        e_ready = sem("e_ready")
        pT_ready = sem("pT_ready")
        ln_ready = sem("ln_ready")
        lsd_ready = sem("lsd_ready")
        vn_ready = sem("vn_ready")
        ya_ready = sem("ya_ready")
        yb_ready = sem("yb_ready")
        yc_ready = sem("yc_ready")
        yTh_ready = sem("yTh_ready")
        yT_ready = sem("yT_ready")
        gate_ready = sem("gate_ready")
        merged_ready = sem("merged_ready")
        logit_ready = sem("logit_ready")
        rexp_ready = sem("rexp_ready")
        c_done = sem("c_done")
        gains_used = sem("gains_used")
        tiles_done = sem("tiles_done")
        fin_done = sem("fin_done")

        def counts(eng):
            return (eng.value_load(plan_i[0:1, 0:1], min_val=0, max_val=S),
                    eng.value_load(plan_i[0:1, 1:2], min_val=0, max_val=NG - 1))

        block = ctx.enter_context(nc.Block())

        @block.sync
        def _(sp):
            sp.dma_start(x[:], a["x"].rearrange("b (t p) d -> p (b t) d", p=P)).then_inc(x_in, 16)
            sp.dma_start(tab[:, 0:FIRST_COLS], a["table"][:, 0:FIRST_COLS]).then_inc(const_in, 16)

            def rows(layer):
                if layer == 0:
                    sp.wait_ge(rows_clear, 1)
                for r0, n, src in ((0, 8, a["norm_mix_g"][layer].rearrange("(r p) -> r p", p=P)),
                                   (8, 24, a["rwkv_mu_wag"][layer].rearrange("m (r p) -> (m r) p", p=P)),
                                   (32, 8, a["rwkv_mu_v"][0].rearrange("(r p) -> r p", p=P)),
                                   (40, 8, a["norm_ffn_g"][layer].rearrange("(r p) -> r p", p=P)),
                                   (48, 4, a["gmlp_bs"][layer])):
                    sp.dma_start(vec_rows[r0:r0 + n, :], src).then_inc(rows_in, 16)
                for r0, n, src in ((0, 6, a["b_gate"][layer].rearrange("(r n) -> r n", n=W)),
                                   (6, 1, a["rwkv_w0"][layer:layer + 1]),
                                   (7, 1, a["rwkv_a0"][layer:layer + 1]),
                                   (8, 1, a["rwkv_v0"][0:1])):
                    sp.dma_start(bias_rows[r0:r0 + n, :], src).then_inc(rows_in, 16)
                sp.dma_start(bias_rows[9:10, 0:4], a["router_group_b"][layer:layer + 1]).then_inc(rows_in, 16)
                sp.dma_start(bias_rows[9:10, 4:20], a["router_expert_b"][layer:layer + 1]).then_inc(rows_in, 16)

            def gains(layer):
                for slot, src in ((MU[0], a["rwkv_mu_rkv"][layer, 0]), (MU[1], a["rwkv_mu_rkv"][layer, 1]),
                                  (MU[2], a["rwkv_mu_rkv"][layer, 2]), (KK_, a["rwkv_k_k"][layer]),
                                  (KA_, a["rwkv_k_a"][layer]),
                                  (RK_, a["rwkv_r_k"][layer].rearrange("h d -> (h d)"))):
                    sp.dma_start(bc[:, slot, :], src.partition_broadcast(P)).then_inc(bc_in, 16)
                for c0, n, name in ((0, 4, "router_group_w"), (4, 16, "router_expert_w")):
                    sp.dma_start(rw[:, :, c0:c0 + n], a[name][layer].rearrange("(c p) n -> p c n", p=P))\
                        .then_inc(rw_in, 16)

            def load(layer, row):
                kind, arg, slot = row["kind"], row["arg"], row["slot"]
                for name, value in row["wait"] or ():
                    sp.wait_ge(stream[name], value)
                r = ring[:, slot, :]
                if kind == "dense":
                    name, c0, n, j = arg
                    pairs = [(r[:, 0:4 * n].rearrange("p (c n) -> p c n", c=4),
                              a[name][layer].rearrange("(c p) n -> p c n", p=P)[:, 4 * j:4 * j + 4, c0:c0 + n])]
                elif kind == "lora1":
                    v = r[:, 0:4 * 288].rearrange("p (c n) -> p c n", c=4)
                    pairs, at = [], 0
                    for name, n in (("rwkv_w1", 64), ("rwkv_a1", 64), ("rwkv_g1", 128), ("rwkv_v1", 32)):
                        src = a[name][0 if name == "rwkv_v1" else layer].rearrange("(c p) n -> p c n", p=P)
                        pairs.append((v[:, :, at:at + n], src[:, 4 * arg[0]:4 * arg[0] + 4, :]))
                        at += n
                elif kind == "lora2":
                    pairs = []
                    for i, (name, n) in enumerate((("rwkv_w2", 64), ("rwkv_a2", 64), ("rwkv_g2", 128),
                                                   ("rwkv_v2", 32))):
                        src = a[name][0 if name == "rwkv_v2" else layer]
                        pairs.append((r[0:n, i * W:(i + 1) * W], src))
                else:
                    name, c = (("w_branch_a", 4), ("w_branch_b", 2), ("w_branch_c", 4))[arg[0]]
                    c0 = arg[1] * W
                    pairs = [(r[:, 0:c * W].rearrange("p (c n) -> p c n", c=c),
                              a[name][layer].rearrange("(c p) n -> p c n", p=P)[:, :, c0:c0 + W])]
                for dst, src in pairs:
                    sp.dma_start(dst, src).then_inc(landed[slot], 16)

            def expert_loads(layer, i, group, first):
                ex = PLAN.experts[layer]
                n_p, n_v = lo_counts(EXPERT_PIECES)
                start = group * (EPG * D * W)
                for m in range(EXPERT_LOADS):
                    k = m % (2 * RING)
                    which, e = SEGMENTS[m // 2]
                    name = ("expert_w_gate", "expert_w_up", "expert_w_down")[which]
                    at = start + (2 * e + m % 2) * (D * W // 2)
                    due = None
                    if not (first and m < 2 * RING):
                        if m >= 2 * RING:
                            p_, v_ = lo_counts(2 * (m - 2 * RING) + 2)
                        else:
                            p_, v_ = (n - all_ for n, all_ in zip(lo_counts(2 * (m - 2 * RING) + 2 + EXPERT_PIECES),
                                                                  (n_p, n_v)))
                        due = i * n_p + (ex["lo_p"] + p_), i * n_v + (ex["lo_v"] + v_)
                    if not isinstance(group, int):
                        due = tuple(sp.to_reg(v) for v in due)
                    src = a[name][layer].rearrange("e k n -> (e k n)")[bass.ds(at, D * W // 2)]
                    n = (W, W, D)[which]
                    dst = raw_slot(ring, proj, ex["slots"][k]).rearrange("p (c n) -> p c n", n=n)
                    if due:
                        sp.wait_ge(lo_p, due[0])
                        sp.wait_ge(lo_v, due[1])
                    sp.dma_start(dst, src.rearrange("(c p n) -> p c n", p=P, n=n)).then_inc(landed[ex["slots"][k]], 16)

            rows(0)
            for layer in range(LAYERS):
                for n, row in enumerate(PLAN.loads[layer]):
                    load(layer, row)
                    if n == 5 and layer == 0:
                        sp.dma_start(tab[:, FIRST_COLS:], a["table"][:, FIRST_COLS:]).then_inc(table_in, 16)
                        sp.dma_start(pos_i[:], a["positions"].rearrange("a (t p) -> p (a t)", p=P),
                                     allow_slow_non_contiguous=True).then_inc(table_in, 16)
                    if n == 6 and layer == 0:
                        gains(0)
                    if n == 27:
                        sp.wait_ge(yc_ready, layer + 1)
                        sp.dma_start(ws, a["gmlp_ws"][layer].rearrange("g t s -> t g s")).then_inc(ws_in, 16)
                    if n == 9 and layer:
                        sp.wait_ge(mix_ready, 7)
                        sp.dma_start(v_old, v_first).then_inc(vf_in, 16)
                    if n == 21:
                        if layer == 0:
                            sp.wait_ge(c_done, 1)
                            sp.dma_start(v_first, proj[:, :, CV0:CV0 + W]).then_inc(vf_out, 16)
                        sp.wait_ge(tilde_ready, NT * (layer + 1))
                        for slot, src in ((LNW, a["rwkv_ln_w"][layer]), (LNB, a["rwkv_ln_b"][layer]),
                                          (GLG, a["gmlp_ln_g"][layer]), (GLB, a["gmlp_ln_b"][layer]),
                                          (FFG[0], a["norm_ffn_g"][layer, 0:W]), (FFG[1], a["norm_ffn_g"][layer, W:D])):
                            sp.dma_start(bc[:, slot, :], src.partition_broadcast(P)).then_inc(late_in, 16)
                ex = PLAN.experts[layer]
                sp.wait_ge(lo_p, ex["lo_p"])
                sp.wait_ge(merged_ready, layer + 1)
                if layer == 0:
                    sp.wait_ge(vf_out, 16)
                expert_loads(layer, 0, 0, True)
                sp.wait_ge(gains_used, layer + 1)
                if layer + 1 < LAYERS:
                    rows(layer + 1)
                    gains(layer + 1)
                else:
                    sp.dma_start(bc[:, 0:2, :].rearrange("p a n -> p (a n)"),
                                 a["final_norm_g"].partition_broadcast(P)).then_inc(fin_in, 16)
                with sp.Fori(1, NG) as g:
                    expert_loads(layer, g, g, False)
                sp.wait_ge(plan_ready, layer + 1)
                largest, which = counts(sp)
                with sp.If(largest > P):
                    expert_loads(layer, NG, which, False)
                with sp.Else():
                    sp.wait_ge(tiles_done, layer + 1)
                    for k in range(2 * RING):
                        sp.sem_inc(landed[k], 16 * EXPERT_LOADS // (2 * RING))
            for t in range(NT):
                sp.wait_ge(fin_done, t + 1)
                sp.dma_start(a["out"].rearrange("b (t p) d -> p (b t) d", p=P)[:, t, :], h_nat[:, t, :])\
                    .then_inc(out_done, 16)
            sp.wait_ge(out_done, 16 * NT)

        @block.gpsimd
        def _(pool):
            def lo(layer, p):
                slot, _, i = PLAN.piece_at[p]
                pool.wait_ge(hi_ready, p + 1)
                pool.tensor_tensor(wl[:, p % HL, :], ring[:, slot, i * PIECE:(i + 1) * PIECE],
                                   wh[:, p % HL, :].bitcast(F32), ALU.subtract).then_inc(lo_p, 1)

            def expert_lo(layer, i):
                ex = PLAN.experts[layer]
                for q in range(EXPERT_PIECES):
                    if q % 3 == 0:
                        k = (ex["pieces"] + q) % HL
                        pool.wait_ge(hi_ready, i * EXPERT_PIECES + (ex["pieces"] + q + 1))
                        pool.tensor_tensor(pieces_of(wl[:, k, :], q), raw_piece(ex, q),
                                           pieces_of(wh[:, k, :].bitcast(F32), q), ALU.subtract).then_inc(lo_p, 1)

            for layer in range(LAYERS):
                blocks = PLAN.blocks[layer]
                split = 3 + CHUNK_BLOCKS[0]
                for p in range(blocks[0][1], blocks[split][2]):
                    lo(layer, p)
                if layer == 0:
                    pool.wait_ge(table_in, 32)
                for c in range(NT):
                    g = layer * NT + c
                    p1 = blocks[split + c][2]
                    lo(layer, p1)
                    pool.wait_ge(score_ready, g + 1)
                    for k in range(LEVELS):
                        if k == 2:
                            pool.wait_ge(xt_ready, g * 2 * LEVELS + 2)
                        elif k > 2:
                            pool.wait_ge(y_ready, (g * (LEVELS - 1) + k - 3) * 2 + 2)
                        at, _ = CONST_AT[f"level{k}"]
                        m = tab[:, at:at + P].unsqueeze(1).to_broadcast([P, CH, P])
                        pool.tensor_tensor(Nl[k % 2], SCb[:, :, 0, :], m, ALU.mult).then_inc(n_ready, 1)
                    for p in range(p1 + 1, p1 + 4):
                        lo(layer, p)
                for p in range(p1 + 4, blocks[-1][2]):
                    lo(layer, p)
                with pool.Fori(0, NG) as i:
                    expert_lo(layer, i)
                pool.wait_ge(plan_ready, layer + 1)
                largest, _ = counts(pool)
                with pool.If(largest > P):
                    expert_lo(layer, NG)
                with pool.Else():
                    pool.wait_ge(tiles_done, layer + 1)
                    pool.sem_inc(lo_p, lo_counts(EXPERT_PIECES)[0])

        @block.tensor
        def _(pe):
            jobs, fulls = [0] * 8, [0] * 8
            raw = [0]

            def open_bank(b):
                if jobs[b]:
                    pe.wait_ge(bank_read[b], jobs[b])

            def close_bank(b, mm):
                mm.then_inc(bank_full[b], 1)
                jobs[b] += 1
                fulls[b] += 1

            def raw_load(layer, n):
                row = PLAN.loads[layer][n]
                pe.wait_ge(landed[row["slot"]], row["landed"])
                return ring[:, row["slot"], :]

            def transposes(bank, srcs):
                open_bank(bank)
                for i, s in enumerate(srcs):
                    n = s.shape[0]
                    mm = pe.transpose(PS[:, bank, i * P:i * P + n], s, ident[0:n, 0:n])
                close_bank(bank, mm)

            def norm_transposes(n, kind):
                for i, bank in enumerate((2, 4, 3, 5)):
                    if i % 2 == 0:
                        pe.wait_ge(hnat_ready, 2 * (n - 1) + i // 2 + 1)
                        if kind == "mix":
                            pe.wait_ge(hnat_a, n + i // 2)
                    transposes(bank, [h_nat[:, t, (2 * i + j) * P:(2 * i + j + 1) * P] for j in range(2)
                                      for t in range(NT)])

            def add_bias(out, row, n):
                return pe.matmul(out, selector[:, row:row + 1].to_broadcast([64, P]), bias_parts[:, 0:n],
                                 start=False, stop=True)

            def dense_piece(layer, blk, j, banks=(0, 1), bias=None, tiles=range(NT), branch=None):
                if branch is None:
                    ah, al = hTh, hTl
                    n, p0, p1 = PLAN.blocks[layer][blk]
                else:
                    ah, al = yT_hi[branch], yT_lo[branch]
                    n, p0, p1 = PLAN.branches[layer][blk]
                p = p0 + j
                cp = PIECE // n
                ex = PLAN.experts[layer]
                pe.wait_ge(lo_p, ex["lo_p"] - (ex["pieces"] - 1 - p))
                h_ = wh[:, p % HL, :].rearrange("p (c n) -> p c n", c=cp)
                l_ = wl[:, p % HL, :].rearrange("p (c n) -> p c n", c=cp)
                last = p == p1 - 1
                for t in tiles:
                    b = banks[t]
                    if j == 0:
                        open_bank(b)
                    out = PS[:, b, 0:n]
                    for i in range(cp):
                        c = j * cp + i
                        xh, xl = ah[:, c, t * P:(t + 1) * P], al[:, c, t * P:(t + 1) * P]
                        pe.matmul(out, xh, h_[:, i, :], start=(c == 0), stop=False)
                        pe.matmul(out, xh, l_[:, i, :], start=False, stop=False)
                        mm = pe.matmul(out, xl, h_[:, i, :], start=False,
                                       stop=(last and i == cp - 1 and bias is None))
                    if last:
                        if bias is not None:
                            mm = add_bias(out, bias, n)
                        if t == NT - 1:
                            jobs[b] += 1
                        else:
                            close_bank(b, mm)
                    if t == NT - 1:
                        mm.then_inc(piece_used, 1)

            def dense(layer, blk, banks=(0, 1), bias=None):
                for j in range(PLAN.blocks[layer][blk][2] - PLAN.blocks[layer][blk][1]):
                    dense_piece(layer, blk, j, banks, bias)

            def raw_done(n=1):
                pe.drain().then_inc(raw_used, n)

            pe.wait_ge(const_in, 16)
            for layer in range(LAYERS):
                pe.wait_ge(rows_in, 11 * 16 * (layer + 1))
                transposes(4, [vec_rows])
                norm_transposes(2 * layer + 1, "mix")
                for j in range(4):
                    pe.wait_ge(hTl_ready, 4 * layer + j + 1)
                    dense_piece(layer, 0, j)
                for blk in BLOCK_ORDER["time"][1:]:
                    dense(layer, blk)
                l1 = [raw_load(layer, 6 + j)[:, 0:4 * 288].rearrange("p (c n) -> p c n", c=4) for j in range(2)]
                nmix = 3 + layer
                mix0 = 3 * layer
                for m, (at, n) in enumerate(((0, 64), (64, 64), (128, 128), (256, 32))[:nmix]):
                    pe.wait_ge(mix_ready, mix0 + m + 1)
                    b = 2 + m % 2
                    open_bank(b)
                    for c in range(KC):
                        mm = pe.matmul(PS[0:n, b, 0:S], l1[c // 4][:, c % 4, at:at + n], mix[m % 2][:, c, :],
                                       start=(c == 0), stop=(c == KC - 1))
                    close_bank(b, mm)
                raw_done(2)
                blk = raw_load(layer, 8)
                pe.wait_ge(bias_lo, layer + 1)
                for m, (n, bias) in enumerate(((64, 6), (64, 7), (128, None), (32, 8))[:nmix]):
                    pe.wait_ge(lora_ready, mix0 + m + 1)
                    for t in range(NT):
                        b = 2 + t
                        open_bank(b)
                        mm = pe.matmul(PS[:, b, :], loraT[m][0:n, t * P:(t + 1) * P], blk[0:n, m * W:(m + 1) * W],
                                       start=True, stop=bias is None)
                        if bias is not None:
                            mm = add_bias(PS[:, b, :], bias, W)
                        close_bank(b, mm)
                raw_done()
                if layer == 0:
                    pe.wait_ge(table_in, 32)
                pe.wait_ge(rkv_ready, 6 * (layer + 1))
                for i, c0 in enumerate((R0, CK0, CV0)):
                    for t in (1, 0):
                        b = 4 + t
                        open_bank(b)
                        mm = pe.matmul(PS[:, b, :], const("shift"), proj[:, t, c0:c0 + W], start=True, stop=(t == 0))
                        if t:
                            mm = pe.matmul(PS[:, b, :], const("edge"), proj[:, 0, c0:c0 + W], start=False, stop=True)
                        close_bank(b, mm)
                pe.wait_ge(zs_ready, 14 if layer else 6)
                for t in range(NT):
                    if t:
                        open_bank(6)
                        for q in range(4):
                            pe.matmul(PS[:, 6, q:q + 1], lw[:, 0, q * P:(q + 1) * P], const("after_mid"),
                                      start=True, stop=False)
                            mm = pe.matmul(PS[:, 6, q:q + 1], lw[:, 1, q * P:(q + 1) * P], const("before_mid"),
                                           start=False, stop=True)
                        close_bank(6, mm)
                    for b, m in ((2 - 2 * t, "decay_incl"), (3 - 2 * t, "decay_prev")):
                        open_bank(b)
                        close_bank(b, pe.matmul(PS[:, b, :], const(m), lw[:, t, :], start=True, stop=True))
                rest, gates = BLOCK_ORDER["rest"], BLOCK_ORDER["gate"]
                for blk in rest[:CHUNK_BLOCKS[0]]:
                    dense(layer, blk)
                for c in range(NT):
                    g = layer * NT + c
                    pe.wait_ge(tilde_ready, g + 1)
                    for b, src in ((4, kk), (5, proj[:, :, R0:R0 + W]), (6, aa), (7, proj[:, :, CK0:CK0 + W])):
                        transposes(b, [src[:, c, q * P:(q + 1) * P] for q in range(4)])
                    dense_piece(layer, rest[CHUNK_BLOCKS[c]], 0)
                    dense_piece(layer, rest[CHUNK_BLOCKS[c]], 1, tiles=(0,))
                    pe.wait_ge(crT_ready, g + 1)
                    for half in range(2):
                        for b, lhs, i in ((4, bT, 0), (5, bT, 1), (6, kT_c, 0), (7, kT_c, 1)):
                            rows = slice(64 * i, 64 * i + 64)
                            open_bank(b)
                            for j in range(2):
                                q = 2 * half + j
                                mm = pe.matmul(PS[:, b, 256 * j:256 * j + 256], lhs[rows, q, :],
                                               krT[rows, q, :, :].rearrange("p a t -> p (a t)"),
                                               start=True, stop=True)
                            close_bank(b, mm)
                    dense_piece(layer, rest[CHUNK_BLOCKS[c]], 1, tiles=(1,))
                    dense_piece(layer, rest[CHUNK_BLOCKS[c]], 2)
                    for k in range(LEVELS):
                        n = g * LEVELS + k
                        N = Nl[k % 2]
                        pe.wait_ge(n_ready, n + 1)
                        for h in range(2):
                            if k:
                                pe.wait_ge(xt_ready, g * 2 * LEVELS + 2 * (k - 1) + h + 1)
                            b = 2 + h if k else 4 + 2 * h
                            open_bank(b)
                            for i in range(4):
                                hh = 4 * h + i
                                rhs = X[:, hh, :] if k else ident
                                mm = pe.matmul(PS[:, b, i * P:(i + 1) * P], N[:, hh, :], rhs, start=True, stop=True)
                            close_bank(b, mm)
                        if k == 0:
                            continue
                        for h in range(2):
                            pe.wait_ge(y_ready, (g * (LEVELS - 1) + k - 1) * 2 + h + 1)
                            for b, which in ((4 + 2 * h, "xt"), (5 + 2 * h, "x")):
                                if which == "x" and k == LEVELS - 1:
                                    continue
                                open_bank(b)
                                for i in range(4):
                                    hh = 4 * h + i
                                    l, r, side = (Yl, XT, 1) if which == "xt" else (XT, Yl, 0)
                                    o = PS[:, b, i * HALF_COLS:(i + 1) * HALF_COLS]
                                    mm = pe.matmul(o.rearrange("p (a r) -> p a r", r=2 ** k), l[:, hh, :],
                                                   side_of(r[:, hh, :], k, side), start=True, stop=True)
                                close_bank(b, mm)
                    if c:
                        pe.wait_ge(state_ready, layer + 1)
                    open_bank(2)
                    for hh in range(CH):
                        q = hh // 2
                        o = PS[:, 2, hh * HD:(hh + 1) * HD]
                        vh = proj[:, c, CV0 + hh * HD:CV0 + (hh + 1) * HD]
                        mm = pe.matmul(o, SCk[:, hh, 0, :], vh, start=True, stop=(c == 0))
                        if c:
                            mm = pe.matmul(o, krT[:, q, 0, :], state[:, q, 64 * (hh % 2):64 * (hh % 2) + 64],
                                           start=False, stop=True)
                    close_bank(2, mm)
                    dense_piece(layer, rest[CHUNK_BLOCKS[c]], 3, tiles=(0,))
                    pe.wait_ge(xt_ready, (g + 1) * 2 * LEVELS)
                    pe.wait_ge(r_ready, g + 1)
                    open_bank(3)
                    for hh in range(CH):
                        mm = pe.matmul(PS[:, 3, hh * HD:(hh + 1) * HD], XT[:, hh, :], tmp[0][:, hh * HD:(hh + 1) * HD],
                                       start=True, stop=True)
                    close_bank(3, mm)
                    dense_piece(layer, rest[CHUNK_BLOCKS[c]], 3, tiles=(1,))
                    pe.wait_ge(sa_ready, g + 1)
                    open_bank(4)
                    for hh in range(CH):
                        q = hh // 2
                        o = PS[:, 4, hh * HD:(hh + 1) * HD]
                        pe.matmul(o, SCb[:, hh, 1, :], tmp[1][:, hh * HD:(hh + 1) * HD], start=True, stop=False)
                        mm = pe.matmul(o, SCk[:, hh, 1, :], proj[:, c, CV0 + hh * HD:CV0 + (hh + 1) * HD],
                                       start=False, stop=(c == 0))
                        if c:
                            mm = pe.matmul(o, krT[:, q, 1, :], state[:, q, 64 * (hh % 2):64 * (hh % 2) + 64],
                                           start=False, stop=True)
                    close_bank(4, mm)
                    if c == 0:
                        open_bank(5)
                        for q in range(4):
                            cols = slice(q * P, (q + 1) * P)
                            pe.matmul(PS[:, 5, cols], aa[:, 0, cols], tmp[1][:, cols], start=True, stop=False)
                            mm = pe.matmul(PS[:, 5, cols], proj[:, 0, CK0 + q * P:CK0 + (q + 1) * P],
                                           proj[:, 0, CV0 + q * P:CV0 + (q + 1) * P], start=False, stop=True)
                        close_bank(5, mm)
                dense(layer, rest[-1])
                dense(layer, gates[0], bias=0)
                pe.wait_ge(ws_in, 16 * (layer + 1))
                transposes(4, [ws[:, g, :] for g in range(AG)])
                pe.wait_ge(rot_ready, layer + 1)
                pe.wait_ge(yc_ready, layer + 1)
                for i, c0 in enumerate((Q0, K0)):
                    for q in range(3):
                        transposes(2 + (3 * i + q) % 2, [proj[:, t, c0 + (2 * q + j) * P:c0 + (2 * q + j + 1) * P]
                                                         for j in range(2) for t in range(NT)])
                filler = [(k, j) for k in (1, 2, 3) for j in range(4)]

                def gate_piece(n, tiles=range(NT)):
                    k, j = filler[n]
                    dense_piece(layer, gates[k], j, bias=k, tiles=tiles)

                for t in range(NT):
                    gate_piece(t)
                    pe.wait_ge(vn_ready, layer * NT + t + 1)
                    open_bank(5)
                    for g in range(AG):
                        mm = pe.matmul(PS[:, 5, g * P:(g + 1) * P], wsT[:, g, :], vn[:, g * P:(g + 1) * P],
                                       start=True, stop=True)
                    close_bank(5, mm)
                gate_piece(NT)
                pe.wait_ge(qkT_ready, 6 * (layer + 1))
                n_jobs = NT * BHG

                def attend_scores(job):
                    head, t = job // NT, job % NT
                    n = (t + 1) * P
                    for gr in range(3):
                        hh = gr * BHG + head
                        rows, q = slice(64 * (hh % 2), 64 * (hh % 2) + 64), hh // 2
                        b = 4 + gr // 2
                        if gr != 1:
                            open_bank(b)
                        at = (gr % 2) * n
                        mm = pe.matmul(PS[:, b, at:at + n], qT[rows, q, t * P:(t + 1) * P], kT[rows, q, 0:n],
                                       start=True, stop=True)
                        if gr:
                            close_bank(b, mm)

                def attend_values(job, between):
                    head, t = job // NT, job % NT
                    g = layer * n_jobs + job
                    pe.wait_ge(e_ready, g + 1)
                    keys = [(gr, kt) for gr in range(3) for kt in range(t + 1)]
                    transposes(2, [prob[g % 2][:, i * P:(i + 1) * P] for i in range(min(4, len(keys)))])
                    if len(keys) > 4:
                        transposes(3, [prob[g % 2][:, i * P:(i + 1) * P] for i in range(4, len(keys))])
                    between()
                    pe.wait_ge(pT_ready, g + 1)
                    b = 6 + g % 2
                    open_bank(b)
                    for i, (gr, kt) in enumerate(keys):
                        hh = gr * BHG + head
                        mm = pe.matmul(PS[:, b, 0:HD], probT[g % 2][:, i, :],
                                       proj[:, kt, VB0 + hh * HD:VB0 + (hh + 1) * HD],
                                       start=(i == 0), stop=(i == len(keys) - 1))
                    close_bank(b, mm)

                attend_scores(0)
                for job in range(n_jobs):
                    if job + 1 < n_jobs:
                        attend_scores(job + 1)
                    gate_piece(NT + 1 + job, tiles=(0,))
                    attend_values(job, between=lambda: gate_piece(NT + 1 + job, tiles=(1,)))
                pe.wait_ge(ya_ready, layer + 1)
                pe.wait_ge(yb_ready, layer + 1)
                for i, (src, n) in enumerate(((proj[:, :, U0:U0 + W], 4), (yb, 2), (kk, 4))):
                    for q in range(n // 2):
                        transposes(2 + q % 2, [src[:, t, (2 * q + j) * P:(2 * q + j + 1) * P]
                                               for j in range(2) for t in range(NT)])
                gate_piece(11)
                pe.wait_ge(yT_ready, 5 * (layer + 1))
                for br in range(3):
                    if br:
                        dense(layer, gates[br + 3], bias=br + 3)
                    for half in range(2):
                        _, p0, p1 = PLAN.branches[layer][2 * br + half]
                        for j in range(p1 - p0):
                            dense_piece(layer, 2 * br + half, j, banks=(4, 5), branch=br)
                pe.wait_ge(merged_ready, layer + 1)
                for q in range(4):
                    transposes(2 + q % 2, [merged[:, t, (2 * q + j) * P:(2 * q + j + 1) * P]
                                           for j in range(2) for t in range(NT)])
                pe.wait_ge(bank_read[2], jobs[2])
                pe.wait_ge(bank_read[3], jobs[3])
                for blk in BLOCK_ORDER["out"]:
                    dense(layer, blk, banks=(4, 5))
                norm_transposes(2 * layer + 2, "router")
                pe.wait_ge(hT_v, 3 * layer + 3)
                pe.wait_ge(hT_a, 2 * layer + 2)
                for t in range(NT):
                    b = 6 + t
                    open_bank(b)
                    for c in range(KC):
                        if (t, c) == (0, 0):
                            pe.wait_ge(rw_in, 32 * (layer + 1))
                        pe.matmul(PS[:, b, 0:20], hT_router[:, c, t * P:(t + 1) * P], rw[:, c, :],
                                  start=(c == 0), stop=False)
                    close_bank(b, add_bias(PS[:, b, 0:20], 9, 20))
                pe.wait_ge(g_ready, layer + 1)
                open_bank(4)
                pe.matmul(PS[:, 4, 0:4], const("low_strict"), hot[:, 0, :], start=True, stop=True)
                pe.matmul(PS[:, 4, 4:8], const("ones"), hot[:, 0, :], start=True, stop=False)
                pe.matmul(PS[:, 4, 4:8], const("low_strict"), hot[:, 1, :], start=False, stop=True)
                pe.matmul(PS[:, 4, 8:12], const("ones"), hot[:, 0, :], start=True, stop=False)
                close_bank(4, pe.matmul(PS[:, 4, 8:12], const("ones"), hot[:, 1, :], start=False, stop=True))
                ex = PLAN.experts[layer]

                def gather(b, chunks):
                    for c in chunks:
                        for t in range(NT):
                            mm = pe.matmul(PS[:, b, (c % 4) * P:(c % 4 + 1) * P], h_nat[:, t, c * P:(c + 1) * P],
                                           pick01[:, t, :], start=(t == 0), stop=(t == NT - 1))
                    return mm

                def gather_weights(b):
                    for t in range(NT):
                        mm = pe.matmul(PS[:, b, 0:EPG], pick01[:, t, :], own[:, t, :],
                                       start=(t == 0), stop=(t == NT - 1))
                    return mm

                pe.wait_ge(pick_ready, layer * (NG + 1) + 1)
                open_bank(5)
                close_bank(5, gather(5, range(4)))
                pe.wait_ge(own_ready, layer + 1)
                open_bank(7)
                close_bank(7, gather_weights(7))
                base = list(jobs)
                at_experts.append((base, list(fulls)))
                tally = {}

                def signal(ins, s):
                    ins.then_inc(s, 1)
                    tally[s.name] = (s, tally.get(s.name, (s, 0))[1] + 1)

                def group_tile(i, more):
                    def wait_bank(b, n):
                        pe.wait_ge(bank_read[b], i * TILE_JOBS[b] + (base[b] + n))

                    def turn_hidden(e):
                        pe.wait_ge(bank_read[4], i * TILE_JOBS[4] + (base[4] + e + 1))
                        wait_bank(1, e)
                        for c in range(4):
                            mm = pe.transpose(PS[:, 1, c * P:(c + 1) * P], hid[e % 2][:, c * P:(c + 1) * P], ident)
                        signal(mm, bank_full[1])

                    pe.wait_ge(pick_ready, i + (layer * (NG + 1) + 1))
                    wait_bank(6, 0)
                    signal(gather(6, range(4, 8)), bank_full[6])
                    wait_bank(7, 0)
                    for t in range(NT):
                        mm = pe.transpose(PS[:, 7, t * P:(t + 1) * P], pick01[:, t, :], ident)
                    signal(mm, bank_full[7])
                    for s, (which, e) in enumerate(SEGMENTS):
                        if which == 0 and e == 0:
                            wait_bank(5, 0)
                        if s == 11:
                            if more:
                                pe.wait_ge(pick_ready, i + (layer * (NG + 1) + 2))
                                wait_bank(5, 0)
                                gather(5, range(2))
                            turn_hidden(3)
                            if more:
                                signal(gather(5, range(2, 4)), bank_full[5])
                                wait_bank(7, 1)
                                signal(gather_weights(7), bank_full[7])
                        if which == 2:
                            pe.wait_ge(bank_read[1], i * TILE_JOBS[1] + (base[1] + e + 1))
                        for r in range(4):
                            if (which, e, r) == (0, 0, 2):
                                wait_bank(6, 1)
                            q = 4 * s + r
                            n_p, n_v = lo_counts(q + 1)
                            if q % 3 == 0:
                                pe.wait_ge(lo_p, i * lo_counts(EXPERT_PIECES)[0] + (ex["lo_p"] + n_p))
                            else:
                                pe.wait_ge(lo_v, i * lo_counts(EXPERT_PIECES)[1] + (ex["lo_v"] + n_v))
                            k = (ex["pieces"] + q) % HL
                            h_ = wh[:, k, :].rearrange("p (c n) -> p c n", c=2)
                            l_ = wl[:, k, :].rearrange("p (c n) -> p c n", c=2)
                            if which < 2:
                                b, n = ((0, e), (4, e))[which]
                                if r == 0:
                                    wait_bank(b, n)
                            else:
                                b = 2 + r % 2
                                if e == 0 and r < 2:
                                    wait_bank(b, 0)
                            for j in range(2):
                                if which < 2:
                                    xh, xl = xTh[:, 2 * r + j, :], xTl[:, 2 * r + j, :]
                                    first, last = r + j == 0, r == 3 and j == 1
                                else:
                                    c = 2 * (r // 2) + j
                                    xh, xl = hidTh[:, c, :], hidTl[:, c, :]
                                    first, last = e == 0 and c == 0, e == 3 and c == 3
                                pe.matmul(PS[:, b, :], xh, h_[:, j, :], start=first, stop=False)
                                pe.matmul(PS[:, b, :], xh, l_[:, j, :], start=False, stop=False)
                                mm = pe.matmul(PS[:, b, :], xl, h_[:, j, :], start=False, stop=last)
                            signal(mm, piece_used)
                            if which == 0 and r == 1 and e:
                                turn_hidden(e - 1)
                    for n, b in enumerate((7, 5, 6, 4)):
                        t, half = n % 2, n // 2
                        if t == 0:
                            pe.wait_ge(bank_read[2 + half], i * TILE_JOBS[2] + (base[2 + half] + 1))
                        wait_bank(b, {7: 2, 5: 1, 6: 1, 4: 4}[b] if more else {7: 1, 5: 0, 6: 1, 4: 4}[b])
                        signal(pe.matmul(PS[:, b, :], pickT[:, t, :], group_sum[:, half, :], start=True, stop=True),
                               bank_full[b])

                with pe.Fori(0, NG) as i:
                    group_tile(i, True)
                largest, _ = counts(pe)
                tally.clear()
                with pe.If(largest > P):
                    group_tile(NG, False)
                with pe.Else():
                    pe.wait_ge(tiles_done, layer + 1)
                    for s, n in tally.values():
                        pe.sem_inc(s, n)
                for b in range(8):
                    jobs[b] += NG * TILE_JOBS[b] + LAST_JOBS[b]
                    fulls[b] += NG * TILE_FULL[b] + LAST_FULL[b]

        @block.scalar
        def _(act):
            taken = [0] * 8
            steps = [0]
            done = [0]

            def take(b):
                taken[b] += 1
                act.wait_ge(bank_full[b], taken[b])

            def give(b):
                act.sem_inc(bank_read[b], 1)

            def step(ins):
                steps[0] += 1
                ins.then_inc(a_step, 1)
                act.wait_ge(a_step, steps[0])

            def load_table(func):
                act.activation(spare, const("eps_rms"), func)

            def evac(b, out, func=ACT.Copy, signal=None, n=W, rows=P, scale=1.0, pat=None, piece=None):
                if piece is None:
                    take(b)
                else:
                    act.wait_ge(piece_used, piece)
                src = PS[0:rows, b, 0:n]
                step(act.activation(out, src if pat is None else src.rearrange(*pat[0], **pat[1]), func, scale=scale))
                give(b)
                if signal is not None:
                    act.sem_inc(signal, 1)

            def norm(n, kind):
                if kind == "router":
                    load_table(ACT.Sqrt)
                act.wait_ge(x_ready, n)
                if n == 1:
                    act.wait_ge(x_in, 16)
                step(act.activation(h_nat[:, 1, :], x[:, 1, :], ACT.Square, accum_out=ss[:, 1:2]))
                act.wait_ge(ss_ready, n)
                if n == 1:
                    act.wait_ge(const_in, 16)
                step(act.activation(rn, ss, ACT.Sqrt, bias=const("eps_rms"), scale=1.0 / D))
                act.sem_inc(rms_ready, 1)
                if kind != "router":
                    act.wait_ge(rn_ready, (n + 1) // 2)
                    for half in range(2):
                        cols = slice(half * W, (half + 1) * W)
                        act.activation(h_nat[:, 1, cols], x[:, 1, cols], ACT.Copy, scale=rn[:, 1:2])\
                            .then_inc(hnat_a, 1)
                if kind == "final":
                    return
                layer = (n - 1) // 2
                if kind == "mix":
                    hi_upto(layer, PLAN.blocks[layer][0][1] + 1)
                    act.wait_ge(vec_ready, layer + 1)
                for i, b in enumerate((2, 3)):
                    take(b)
                    for j in range(2):
                        c = 4 * i + j
                        src = PS[:, b, j * S:(j + 1) * S]
                        if kind == "mix":
                            step(act.activation(hT[:, c, :], src, ACT.Copy, scale=vec[:, VG + c:VG + c + 1]))
                        else:
                            step(act.activation(hT_router[:, c, :], src, ACT.Copy))
                    give(b)
                    if i:
                        act.sem_inc(hT_a, 1)
                    if kind == "mix":
                        act.activation(hTh[:, 4 * i:4 * i + 2, :], hT[:, 4 * i:4 * i + 2, :], ACT.Copy)\
                            .then_inc(hTh_ready, 1)
                        if i == 0:
                            hi_upto(layer, PLAN.blocks[layer][0][1] + 2)
                        act.wait_ge(hT_v, 3 * layer + i + 1)
                        act.activation(hTh[:, 4 * i + 2:4 * i + 4, :], hT[:, 4 * i + 2:4 * i + 4, :], ACT.Copy)\
                            .then_inc(hTh_ready, 1)

            def hi_upto(layer, p1):
                for p in range(done[0], min(p1, PLAN.blocks[layer][-1][2])):
                    slot, value, i = PLAN.piece_at[p]
                    act.wait_ge(landed[slot], value)
                    if p >= HL:
                        act.wait_ge(piece_used, p - HL + 1)
                    act.activation(wh[:, p % HL, :], ring[:, slot, i * PIECE:(i + 1) * PIECE], ACT.Copy)\
                        .then_inc(hi_ready, 1)
                    done[0] = p + 1

            def dense_evac(layer, blk, outs, func=ACT.Copy, signal=None, ahead=True, tiles=range(NT)):
                n, _, p1 = PLAN.blocks[layer][blk]
                if ahead:
                    hi_upto(layer, p1 + 3)
                for t in tiles:
                    evac(t, outs[t], func, signal, n=n, piece=p1 if t == NT - 1 else None)
                if ahead:
                    hi_upto(layer, p1 + 4)

            for layer in range(LAYERS):
                blocks = PLAN.blocks[layer]
                done[0] = blocks[0][1]
                norm(2 * layer + 1, "mix")
                hi_upto(layer, blocks[0][2])
                if layer == 0:
                    for half in range(2):
                        act.activation(selector[32 * half:32 * half + 32, :], ident[0:32, 0:10], ACT.Copy)
                act.wait_ge(rows_in, 11 * 16 * (layer + 1))
                act.activation(bias_parts[0:32, :], bias_rows[:], ACT.Copy).then_inc(bias_hi, 1)
                for blk, c0 in zip(BLOCK_ORDER["time"], (R0, CK0, CV0)):
                    dense_evac(layer, blk, [proj[:, t, c0:c0 + W] for t in range(NT)], signal=rkv_ready,
                               ahead=c0 != CV0)
                nmix = 3 + layer
                for m, (n, func) in enumerate(((64, ACT.Tanh), (64, ACT.Copy), (128, ACT.Sigmoid),
                                               (32, ACT.Copy))[:nmix]):
                    evac(2 + m % 2, loraT[m][0:n, :], func, lora_ready, n=S, rows=n)
                for m, (dst, func) in enumerate(((lw, ACT.Sigmoid), (aa, ACT.Sigmoid), (gg, ACT.Copy),
                                                 (v_gate, ACT.Sigmoid))[:nmix]):
                    for t in range(NT):
                        evac(2 + t, dst[:, t, :], func, zs_ready)
                    if m:
                        hi_upto(layer, blocks[3][1] + min(2 * m, HL))
                for t in range(NT):
                    b = 2 - 2 * t
                    take(b)
                    step(act.activation(exps[t][0], PS[:, b, :], ACT.Exp))
                    step(act.activation(exps[t][1], PS[:, b, :], ACT.Exp, scale=-1.0))
                    give(b)
                    evac(b + 1, exps[t][2], ACT.Exp, exps_ready)
                act.wait_ge(f_ready, layer + 1)
                step(act.activation(F, F, ACT.Exp))
                act.sem_inc(f_exp, 1)
                act.wait_ge(ksq_ready, layer + 1)
                step(act.activation(kn, kn, ACT.Sqrt))
                act.sem_inc(knorm_ready, 1)

                def rest_evac(i, ahead=True):
                    c0, n = REST[i]
                    dense_evac(layer, BLOCK_ORDER["rest"][i], [proj[:, t, c0:c0 + n] for t in range(NT)],
                               ACT.Gelu_apprx_tanh if c0 < Q0 else ACT.Copy, rest_ready, ahead=ahead)

                def group_deviation(g):
                    act.wait_ge(gvar_ready, g + 1)
                    step(act.activation(gvar, gvar, ACT.Sqrt, bias=const("eps_gn"), scale=1.0 / HD))
                    act.sem_inc(gstd_ready, 1)

                if layer == 0:
                    act.wait_ge(ang_ready, 1)
                    act.activation(angle[:, 4, :], angle[:, 2, :], ACT.Sin)
                    act.activation(angle[:, 5, :], angle[:, 3, :], ACT.Sin).then_inc(sin_ready, 1)
                for i in range(CHUNK_BLOCKS[0]):
                    rest_evac(i)
                for c in range(NT):
                    g = layer * NT + c
                    if c:
                        group_deviation(g - 1)
                    p0 = blocks[3 + CHUNK_BLOCKS[c]][1]
                    hi_upto(layer, p0 + HL + 3)
                    for k in range(1, LEVELS):
                        for h in range(2):
                            evac(2 + h, Yl[:, 4 * h:4 * h + 4, :], signal=y_ready,
                                 pat=(("p (h t) -> p h t",), dict(h=4)))
                    evac(2, tmp[0], signal=r_ready)
                    evac(3, tmp[1], signal=sa_ready, scale=-1.0)
                    rest_evac(CHUNK_BLOCKS[c], ahead=False)
                    hi_upto(layer, p0 + 2 * HL)
                hi_upto(layer, p0 + 2 * HL + 1)
                group_deviation(g)
                rest_evac(len(REST) - 1)
                gates = BLOCK_ORDER["gate"]

                def gate_evac(k, tiles=range(NT)):
                    if k == 2:
                        act.wait_ge(yc_ready, layer + 1)
                    dense_evac(layer, gates[k], [gate[k][:, t, :] for t in range(NT)], ACT.Sigmoid, gate_ready,
                               ahead=k in (0, 4, 5), tiles=tiles)

                gate_evac(0)
                def layer_norm_root(t):
                    act.wait_ge(ln_ready, layer * NT + t + 1)
                    step(act.activation(lrs, bag[:, 1:2], ACT.Sqrt, bias=const("eps_ln")))
                    act.sem_inc(lsd_ready, 1)

                layer_norm_root(0)
                for i, dst in enumerate((qT, kT)):
                    for q in range(3):
                        evac(2 + (3 * i + q) % 2, dst[:, 2 * q:2 * q + 2, :], signal=qkT_ready,
                             pat=(("p (c t) -> p c t",), dict(c=2)))
                n_jobs = NT * BHG

                def exponentials(job):
                    g = layer * n_jobs + job
                    n = 3 * (job % NT + 1) * P
                    act.wait_ge(p_ready, g + 1)
                    step(act.activation(prob[g % 2][:, 0:n], prob[g % 2][:, 0:n], ACT.Exp,
                                        bias=nmax[:, g % 2:g % 2 + 1], accum_out=den[:, g % 2:g % 2 + 1]))
                    act.sem_inc(e_ready, 1)

                def turned(job):
                    g = layer * n_jobs + job
                    nk = 3 * (job % NT + 1)
                    evac(2, probT[g % 2][:, 0:min(4, nk), :], n=min(4, nk) * P,
                         pat=(("p (c t) -> p c t",), dict(t=P)))
                    if nk > 4:
                        evac(3, probT[g % 2][:, 4:nk, :], n=(nk - 4) * P, pat=(("p (c t) -> p c t",), dict(t=P)))
                    act.sem_inc(pT_ready, 1)

                p0 = blocks[gates[1]][1]
                hi_upto(layer, p0 + HL + 1)
                layer_norm_root(1)
                hi_upto(layer, p0 + HL + NT + 1)
                for job in range(n_jobs):
                    n = NT + 2 + job
                    exponentials(job)
                    if n % 4 == 0:
                        gate_evac(n // 4, tiles=(0,))
                    turned(job)
                    if n % 4 == 0:
                        gate_evac(n // 4, tiles=(1,))
                    hi_upto(layer, p0 + HL + n)
                for dst, n in zip(yT_hi, (4, 2, 4)):
                    for q in range(n // 2):
                        b = 2 + q % 2
                        take(b)
                        act.activation(dst[:, 2 * q:2 * q + 2, :], PS[:, b, :].rearrange("p (c t) -> p c t", c=2),
                                       ACT.Copy).then_inc(yTh_ready, 1)
                hi_upto(layer, blocks[gates[3]][2] + 3)
                gate_evac(3)
                hi_upto(layer, blocks[gates[4]][1] + HL)
                gate_evac(4)
                gate_evac(5)
                hi_upto(layer, blocks[BLOCK_ORDER["out"][0]][1] + HL)
                for q in range(4):
                    b = 2 + q % 2
                    take(b)
                    act.activation(hTh[:, 2 * q:2 * q + 2, :], PS[:, b, :].rearrange("p (c t) -> p c t", c=2),
                                   ACT.Copy).then_inc(mTh_ready, 1)
                hi_upto(layer, blocks[-1][2])
                norm(2 * layer + 2, "router")
                act.wait_ge(logit_ready, layer + 1)
                step(act.activation(rt[:, 40:50], rt[:, 40:50], ACT.Exp))
                act.sem_inc(rexp_ready, 1)
                ex = PLAN.experts[layer]
                base, base_full = at_experts[layer]

                def gathered_hi(b, value):
                    act.wait_ge(bank_full[b], value)
                    return act.activation(xTh[:, 4 * (b - 5):4 * (b - 5) + 4, :],
                                          PS[:, b, :].rearrange("p (c t) -> p c t", c=4), ACT.Copy)

                gathered_hi(5, base_full[5]).then_inc(xTh_ready, 1)
                tally = {}

                def signal(ins, s):
                    ins.then_inc(s, 1)
                    tally[s.name] = (s, tally.get(s.name, (s, 0))[1] + 1)

                def group_tile(i, more):
                    def full(b, n):
                        act.wait_ge(bank_full[b], i * TILE_FULL[b] + (base_full[b] + n + 1))

                    def through(q):
                        act.wait_ge(piece_used, i * EXPERT_PIECES + (PLAN.experts[layer]["pieces"] + q + 1))

                    def hi(q):
                        m = q // 2
                        k = m % (2 * RING)
                        slot = ex["slots"][k]
                        if q % 2 == 0:
                            act.wait_ge(landed[slot], i * 64 + (ex["landed"][slot] + 16 * (m // (2 * RING) + 1)))
                        act.wait_ge(piece_used, i * EXPERT_PIECES + (ex["pieces"] + q - HL + 1))
                        w = (ex["pieces"] + q) % HL
                        signal(act.activation(pieces_of(wh[:, w, :], q), raw_piece(ex, q), ACT.Copy), hi_ready)

                    def turned_hi(e):
                        full(1, e)
                        signal(act.activation(hidTh[:], PS[:, 1, :].rearrange("p (c t) -> p c t", c=4), ACT.Copy),
                               hidTh_ready)

                    for q in range(2):
                        hi(q)
                    signal(gathered_hi(6, i * TILE_FULL[6] + (base_full[6] + 1)), xTh_ready)
                    for q in range(2, 4):
                        hi(q)
                    for s, (which, e) in enumerate(SEGMENTS):
                        ahead = range(4 * s + 4, 4 * s + 8) if s < 11 else ()
                        for q in ahead[0:2]:
                            hi(q)
                        if which == 0 and e:
                            turned_hi(e - 1)
                        for q in ahead[2:3]:
                            hi(q)
                        if which == 0:
                            through(4 * s + 3)
                            signal(act.activation(hid[e % 2], PS[:, 0, :], ACT.Silu), bank_read[0])
                        for q in ahead[3:4]:
                            hi(q)
                        if s == 10:
                            turned_hi(3)
                            if more:
                                signal(gathered_hi(5, i * TILE_FULL[5] + (base_full[5] + 1)), xTh_ready)
                    for half in range(2):
                        through(EXPERT_PIECES - 2 + half)
                        signal(act.activation(group_sum[:, half, :], PS[:, 2 + half, :], ACT.Copy),
                               bank_read[2 + half])

                with act.Fori(0, NG) as i:
                    group_tile(i, True)
                largest, _ = counts(act)
                tally.clear()
                with act.If(largest > P):
                    group_tile(NG, False)
                with act.Else():
                    act.wait_ge(tiles_done, layer + 1)
                    for s, n in tally.values():
                        act.sem_inc(s, n)
                for b in range(8):
                    taken[b] = base_full[b] + NG * TILE_FULL[b] + LAST_FULL[b]
            norm(2 * LAYERS + 1, "final")

        @block.vector
        def _(dve):
            taken = [0] * 8
            steps = [0]

            def take(b):
                taken[b] += 1
                dve.wait_ge(bank_full[b], taken[b])

            def give(b):
                dve.sem_inc(bank_read[b], 1)

            def step(ins):
                steps[0] += 1
                ins.then_inc(v_step, 1)
                dve.wait_ge(v_step, steps[0])

            def tt(out, i0, i1, op):
                step(dve.tensor_tensor(out, i0, i1, op))

            def stt(out, i0, s, i1, op0, op1):
                step(dve.scalar_tensor_tensor(out=out, in0=i0, scalar=s, in1=i1, op0=op0, op1=op1))

            def ts(out, i0, s1, s2, op0, op1=None):
                if op1 is None:
                    step(dve.tensor_scalar(out, i0, s1, None, op0))
                else:
                    step(dve.tensor_scalar(out, i0, s1, s2, op0, op1))

            def heads(v):
                return v.rearrange("p (h d) -> p h d", d=HD)

            def per_head(v):
                return v.unsqueeze(2).to_broadcast([P, CH, HD])

            def norm(n, kind):
                dve.sem_inc(x_ready, 1)
                if n == 1:
                    dve.wait_ge(x_in, 16)
                step(dve.scalar_tensor_tensor(out=h_nat[:, 0, :], in0=x[:, 0, :], scalar=1.0, in1=x[:, 0, :],
                                              op0=ALU.mult, op1=ALU.mult, accum_out=ss[:, 0:1]))
                dve.sem_inc(ss_ready, 1)
                dve.wait_ge(rms_ready, n)
                step(dve.reciprocal(rn, rn))
                if kind != "router":
                    dve.sem_inc(rn_ready, 1)
                for half in range(2):
                    cols = slice(half * W, (half + 1) * W)
                    if kind == "router":
                        for t in range(NT):
                            stt(h_nat[:, t, cols], x[:, t, cols], rn[:, t:t + 1], bc[:, FFG[half], :],
                                ALU.mult, ALU.mult)
                    else:
                        ts(h_nat[:, 0, cols], x[:, 0, cols], rn[:, 0:1], None, ALU.mult)
                    if kind != "final":
                        dve.sem_inc(hnat_ready, 1)
                if kind == "final":
                    return
                layer = (n - 1) // 2
                if kind == "mix":
                    take(4)
                    step(dve.tensor_copy(vec[:], PS[:, 4, 0:52]))
                    give(4)
                    dve.sem_inc(vec_ready, 1)
                for i, b in enumerate((4, 5)):
                    take(b)
                    for j in range(2):
                        c = 4 * i + 2 + j
                        src = PS[:, b, j * S:(j + 1) * S]
                        if kind == "mix":
                            ts(hT[:, c, :], src, vec[:, VG + c:VG + c + 1], None, ALU.mult)
                        else:
                            step(dve.tensor_copy(hT_router[:, c, :], src))
                    give(b)
                    if kind == "mix":
                        dve.sem_inc(hT_v, 1)
                        for c in (4 * i, 4 * i + 2):
                            dve.wait_ge(hTh_ready, 4 * layer + c // 2 + 1)
                            step(dve.tensor_tensor(hTl[:, c:c + 2, :], hT[:, c:c + 2, :],
                                                   hTh[:, c:c + 2, :].bitcast(F32), ALU.subtract))
                            dve.sem_inc(hTl_ready, 1)
                if kind == "router":
                    dve.sem_inc(hT_v, 1)

            step(dve.memset(bias_rows[:], 0.0))
            dve.sem_inc(rows_clear, 1)

            def angles():
                dve.wait_ge(table_in, 32)
                step(dve.tensor_copy(small[:, 0:NT], pos_i[:]))
                tt(angle[:, 0, :].rearrange("p (t f) -> p t f", t=NT),
                   small[:, 0:NT].unsqueeze(2).to_broadcast([P, NT, HALF]),
                   const("freq").unsqueeze(1).to_broadcast([P, NT, HALF]), ALU.mult)
                for i, (turn, shift) in enumerate(((0.0, 0.0), (0.25, np.pi / 2))):
                    n, r = angle[:, 1, :], angle[:, 2 + i, :]
                    ts(n, angle[:, 0, :], 1.0 / (2 * np.pi), turn, ALU.mult, ALU.add)
                    ts(n, n, ROUND, None, ALU.add)
                    ts(n, n, -ROUND, None, ALU.add)
                    stt(r, n, -TWO_PI[0], angle[:, 0, :], ALU.mult, ALU.add)
                    for part in TWO_PI[1:]:
                        stt(r, n, -part, r, ALU.mult, ALU.add)
                    ts(r, r, float(np.float32(shift)), float(np.float32(3.1415925)), ALU.add, ALU.min)
                    ts(r, r, float(-np.float32(3.1415925)), None, ALU.max)
                dve.sem_inc(ang_ready, 1)

            for layer in range(LAYERS):
                norm(2 * layer + 1, "mix")
                dve.wait_ge(hT_a, 2 * layer + 1)
                step(dve.memset(state[:], 0.0))
                step(dve.tensor_tensor(dhT[:, :, 1:S], hT[:, :, 0:S - 1], hT[:, :, 1:S], ALU.subtract))
                ts(dhT[:, :, 0:1], hT[:, :, 0:1], -1.0, None, ALU.mult)
                dve.wait_ge(bias_hi, layer + 1)
                dve.tensor_tensor(bias_parts[32:64, :], bias_rows[:], bias_parts[0:32, :].bitcast(F32),
                                  ALU.subtract).then_inc(bias_lo, 1)
                for m in range(3 + layer):
                    if m >= 2:
                        dve.wait_ge(lora_ready, 3 * layer + m - 1)
                    for c in range(KC):
                        col = VMU + 8 * m + c
                        stt(mix[m % 2][:, c, :], dhT[:, c, :], vec[:, col:col + 1], hT[:, c, :], ALU.mult, ALU.add)
                    dve.sem_inc(mix_ready, 1)
                if layer == 0:
                    angles()
                dve.wait_ge(bc_in, 6 * 16 * (layer + 1))
                r_, k_, v_ = (proj[:, :, c:c + W] for c in (R0, CK0, CV0))
                dve.wait_ge(zs_ready, 14 if layer else 6)
                for i, t_ in enumerate((r_, k_, v_)):
                    for t in (1, 0):
                        take(4 + t)
                        tt(kk[:, t, :], PS[:, 4 + t, :], bc[:, MU[i], :], ALU.mult)
                        give(4 + t)
                        tt(t_[:, t, :], t_[:, t, :], kk[:, t, :], ALU.add)
                if layer:
                    dve.wait_ge(vf_in, 16)
                    for t in range(NT):
                        tt(kk[:, t, :], v_old[:, t, :], v_[:, t, :], ALU.subtract)
                        tt(kk[:, t, :], kk[:, t, :], v_gate[:, t, :], ALU.mult)
                        tt(v_[:, t, :], v_[:, t, :], kk[:, t, :], ALU.add)
                dve.sem_inc(c_done, 1)
                take(6)
                step(dve.tensor_copy(F, PS[:, 6, 0:4]))
                give(6)
                dve.sem_inc(f_ready, 1)
                sq = view(1024, W)
                for t in range(NT):
                    tt(kk[:, t, :], k_[:, t, :], bc[:, KK_, :], ALU.mult)
                    tt(sq, kk[:, t, :], kk[:, t, :], ALU.mult)
                    step(dve.tensor_reduce(kn[:, t, :], heads(sq), AX_X, ALU.add))
                dve.sem_inc(ksq_ready, 1)
                for t in range(NT):
                    stt(sq, aa[:, t, :], -1.0, bc[:, KA_, :], ALU.add, ALU.mult)
                    stt(k_[:, t, :], sq, 1.0, k_[:, t, :], ALU.add, ALU.mult)
                    tt(sq, r_[:, t, :], k_[:, t, :], ALU.mult)
                    tt(sq, sq, bc[:, RK_, :], ALU.mult)
                    step(dve.tensor_reduce(bonus[:, t, :], heads(sq), AX_X, ALU.add))
                dve.wait_ge(knorm_ready, layer + 1)
                ts(kn, kn, 1e-12, None, ALU.max)
                step(dve.reciprocal(kn, kn))
                for t in range(NT):
                    tt(heads(kk[:, t, :]), heads(kk[:, t, :]), per_head(kn[:, t, :]), ALU.mult)
                    tt(aa[:, t, :], aa[:, t, :], kk[:, t, :], ALU.mult)
                    dve.wait_ge(exps_ready, layer * NT + t + 1)
                    tt(r_[:, t, :], r_[:, t, :], exps[t][0], ALU.mult)
                    tt(aa[:, t, :], aa[:, t, :], exps[t][1], ALU.mult)
                    tt(k_[:, t, :], k_[:, t, :], exps[t][1], ALU.mult)
                    tt(kk[:, t, :], kk[:, t, :], exps[t][2], ALU.mult)
                    dve.sem_inc(tilde_ready, 1)
                low2 = tab[:, CONST_AT["low_strict"][0]:CONST_AT["low_strict"][0] + 2 * P]
                low2 = low2.unsqueeze(1).to_broadcast([P, 2, 2 * P])
                idb = ident.unsqueeze(1).to_broadcast([P, 4, P])

                def group_norm(c, parts):
                    y, t2 = kk[:, c, :], tmp[2]
                    yh = heads(y)
                    if 0 in parts:
                        step(dve.tensor_reduce(gmu, yh, AX_X, ALU.add))
                        ts(gmu, gmu, 1.0 / HD, None, ALU.mult)
                        tt(yh, yh, per_head(gmu), ALU.subtract)
                        tt(t2, y, y, ALU.mult)
                        step(dve.tensor_reduce(gvar, heads(t2), AX_X, ALU.add))
                        dve.sem_inc(gvar_ready, 1)
                    if 1 in parts:
                        dve.wait_ge(gstd_ready, layer * NT + c + 1)
                        step(dve.reciprocal(gvar, gvar))
                        tt(yh, yh, per_head(gvar), ALU.mult)
                    if 2 in parts:
                        if c == 0:
                            dve.wait_ge(late_in, 6 * 16 * (layer + 1))
                        tt(y, y, bc[:, LNW, :], ALU.mult)
                        tt(y, y, bc[:, LNB, :], ALU.add)
                    if 3 in parts:
                        tt(heads(t2), heads(v_[:, c, :]), per_head(bonus[:, c, :]), ALU.mult)
                        tt(y, y, t2, ALU.add)
                    if 4 in parts:
                        tt(y, y, gg[:, c, :], ALU.mult)

                for c in range(NT):
                    g = layer * NT + c
                    for b, dst in ((4, krT[:, :, 0, :]), (5, krT[:, :, 1, :]), (6, bT), (7, kT_c)):
                        take(b)
                        step(dve.tensor_copy(dst, PS[:, b, :].rearrange("p (q t) -> p q t", q=4)))
                        give(b)
                    dve.sem_inc(crT_ready, 1)
                    if c:
                        group_norm(c - 1, (0,))
                    for half in range(2):
                        for b, dst, i in ((4, SCb, 0), (5, SCb, 1), (6, SCk, 0), (7, SCk, 1)):
                            take(b)
                            tt(dst[:, 4 * half + i:4 * half + 4:2, :, :].rearrange("p h a t -> p h (a t)"),
                               PS[:, b, :].rearrange("p (h x) -> p h x", h=2), low2, ALU.mult)
                            give(b)
                    dve.sem_inc(score_ready, 1)
                    dve.wait_ge(n_ready, g * LEVELS + 1)
                    for k in range(LEVELS):
                        for h in range(2):
                            hs = slice(4 * h, 4 * h + 4)
                            if k == 0:
                                tt(XT[:, hs, :], idb, Nl[0][:, hs, :], ALU.subtract)
                                take(4 + 2 * h)
                                tt(X[:, hs, :], idb, PS[:, 4 + 2 * h, :].rearrange("p (h t) -> p h t", h=4),
                                   ALU.subtract)
                                give(4 + 2 * h)
                            else:
                                bs = (4 + 2 * h, 5 + 2 * h) if k < LEVELS - 1 else (4 + 2 * h,)
                                for b in bs:
                                    take(b)
                                for b, m, side in zip(bs, (XT, X), (1, 0)):
                                    v = side_of_heads(m[:, hs, :], k, side)
                                    tt(v, v, PS[:, b, 0:4 * HALF_COLS].rearrange("p (h a r) -> p h a r", h=4, r=2 ** k),
                                       ALU.subtract)
                                    give(b)
                            dve.sem_inc(xt_ready, 1)
                        if c and k in (1, 2, 3, 4):
                            group_norm(c - 1, (k,))
                    take(4)
                    y = kk[:, c, :]
                    step(dve.tensor_copy(y, PS[:, 4, :]))
                    give(4)
                    if c == 0:
                        take(5)
                        dve.wait_ge(f_exp, layer + 1)
                        for i in range(2):
                            s64 = slice(64 * i, 64 * i + 64)
                            tt(state[s64, :, s64], PS[s64, 5, :].rearrange("p (q v) -> p q v", q=4)[:, :, s64],
                               F[s64, :].unsqueeze(2).to_broadcast([64, 4, 64]), ALU.mult)
                        give(5)
                        dve.sem_inc(state_ready, 1)
                group_norm(NT - 1, range(5))
                dve.sem_inc(yc_ready, 1)
                if layer == 0:
                    dve.wait_ge(sin_ready, 1)
                dve.wait_ge(rest_ready, 2 * len(REST) * layer + REST_QKV)
                t1b, t2b = (tmp[i][:, 0:24 * HALF].rearrange("p (h f) -> p h f", f=HALF) for i in range(2))
                t3b, t4b = (tmp[i][:, 256:256 + 24 * HALF].rearrange("p (h f) -> p h f", f=HALF) for i in range(2))
                for t in range(NT):
                    qk = proj[:, t, Q0:VB0].rearrange("p (h d) -> p h d", d=HD)
                    lo_, hi_ = qk[:, :, 0:HALF], qk[:, :, HALF:2 * HALF]
                    sin = angle[:, 4, t * HALF:(t + 1) * HALF].unsqueeze(1).to_broadcast([P, 24, HALF])
                    cos = angle[:, 5, t * HALF:(t + 1) * HALF].unsqueeze(1).to_broadcast([P, 24, HALF])
                    tt(t1b, lo_, cos, ALU.mult)
                    tt(t2b, hi_, sin, ALU.mult)
                    tt(t3b, hi_, cos, ALU.mult)
                    tt(t4b, lo_, sin, ALU.mult)
                    tt(lo_, t1b, t2b, ALU.subtract)
                    tt(hi_, t3b, t4b, ALU.add)
                dve.sem_inc(rot_ready, 1)
                dve.wait_ge(rest_ready, 2 * len(REST) * (layer + 1))
                take(4)
                inc = const("low_incl").unsqueeze(1).to_broadcast([P, AG, P])
                tt(wsT, PS[:, 4, :].rearrange("p (g t) -> p g t", g=AG), inc, ALU.mult)
                give(4)
                for t in range(NT):
                    v = proj[:, t, V0:V0 + W]
                    step(dve.bn_stats(bst, v))
                    step(dve.bn_aggr(bag, bst))
                    dve.sem_inc(ln_ready, 1)
                    dve.wait_ge(lsd_ready, layer * NT + t + 1)
                    step(dve.reciprocal(lrs, lrs))
                    step(dve.tensor_scalar(vn, v, bag[:, 0:1], lrs, ALU.subtract, ALU.mult))
                    tt(vn, vn, bc[:, GLG, :], ALU.mult)
                    tt(vn, vn, bc[:, GLB, :], ALU.add)
                    dve.sem_inc(vn_ready, 1)
                    take(5)
                    for g in range(AG):
                        u = proj[:, t, U0 + g * P:U0 + (g + 1) * P]
                        stt(u, PS[:, 5, g * P:(g + 1) * P], vec[:, VBS + g:VBS + g + 1], u, ALU.add, ALU.mult)
                    give(5)
                dve.sem_inc(ya_ready, 1)
                n_jobs = NT * BHG
                at, _ = CONST_AT["attend"]
                masks = tab[:, at:at + 3 * 2 * P].rearrange("p (g k) -> p g k", g=3)

                def scores(job):
                    t = job % NT
                    g = layer * n_jobs + job
                    n = (t + 1) * P
                    if job >= 2:
                        dve.wait_ge(pT_ready, g - 1)
                    for b, g0, g1 in ((4, 0, 2), (5, 2, 3)):
                        take(b)
                        stt(prob[g % 2][:, g0 * n:g1 * n].rearrange("p (g k) -> p g k", k=n),
                            PS[:, b, 0:(g1 - g0) * n].rearrange("p (g k) -> p g k", k=n), HD ** -0.5,
                            masks[:, g0:g1, 2 * P - n:2 * P], ALU.mult, ALU.add)
                        give(b)
                    nm = nmax[:, g % 2:g % 2 + 1]
                    step(dve.tensor_reduce(nm, prob[g % 2][:, 0:3 * n], AX_X, ALU.max))
                    ts(nm, nm, -1.0, None, ALU.mult)
                    dve.sem_inc(p_ready, 1)

                def values(job):
                    head, t = job // NT, job % NT
                    g = layer * n_jobs + job
                    b = 6 + g % 2
                    take(b)
                    d = den[:, g % 2:g % 2 + 1]
                    step(dve.reciprocal(d, d))
                    ts(yb[:, t, head * HD:(head + 1) * HD], PS[:, b, 0:HD], d, None, ALU.mult)
                    give(b)

                scores(0)
                for job in range(n_jobs):
                    if job + 1 < n_jobs:
                        scores(job + 1)
                    values(job)
                dve.sem_inc(yb_ready, 1)
                i = 5 * layer
                for hi_, lo_, n in zip(yT_hi, yT_lo, (4, 2, 4)):
                    for q in range(n // 2):
                        b = 2 + q % 2
                        i += 1
                        dve.wait_ge(yTh_ready, i)
                        step(dve.tensor_tensor(lo_[:, 2 * q:2 * q + 2, :],
                                               PS[:, b, :].rearrange("p (c t) -> p c t", c=2),
                                               hi_[:, 2 * q:2 * q + 2, :].bitcast(F32), ALU.subtract))
                        give(b)
                        dve.sem_inc(yT_ready, 1)
                for br in range(3):
                    for half in range(2):
                        for t in range(NT):
                            i = 4 * br + 2 * half + t
                            g = 12 * layer + i
                            dve.wait_ge(gate_ready, g + 1)
                            if t == NT - 1:
                                dve.wait_ge(piece_used, PLAN.branches[layer][2 * br + half][2])
                            else:
                                take(4 + t)
                            m = merged[:, t, half * W:(half + 1) * W]
                            tt(tmp[t] if br else m, gate[2 * br + half][:, t, :], PS[:, 4 + t, :], ALU.mult)
                            give(4 + t)
                            if br:
                                tt(m, m, tmp[t], ALU.add)
                dve.sem_inc(merged_ready, 1)
                for q in range(4):
                    b = 2 + q % 2
                    dve.wait_ge(mTh_ready, 4 * layer + q + 1)
                    step(dve.tensor_tensor(hTl[:, 2 * q:2 * q + 2, :], PS[:, b, :].rearrange("p (c t) -> p c t", c=2),
                                           hTh[:, 2 * q:2 * q + 2, :].bitcast(F32), ALU.subtract))
                    dve.sem_inc(bank_read[b], 1)
                for half, blk in enumerate(BLOCK_ORDER["out"]):
                    for t in range(NT):
                        if t == NT - 1:
                            dve.wait_ge(piece_used, PLAN.blocks[layer][blk][2])
                        else:
                            take(4 + t)
                        xs = x[:, t, half * W:(half + 1) * W]
                        tt(xs, xs, PS[:, 4 + t, :], ALU.add)
                        give(4 + t)
                norm(2 * layer + 2, "router")
                lg = rt[:, 0:40].rearrange("p (t n) -> p t n", t=NT)
                for t in range(NT):
                    take(6 + t)
                    step(dve.tensor_copy(lg[:, t, :], PS[:, 6 + t, 0:20]))
                    give(6 + t)
                dve.sem_inc(gains_used, 1)
                ex = rt[:, 40:50].rearrange("p (t n) -> p t n", t=NT)
                mg = rt[:, 50:52].rearrange("p (t n) -> p t n", t=NT)
                mx = rt[:, 52:54].rearrange("p (t n) -> p t n", t=NT)
                one = [hot] + [rt[:, 64 + 8 * i:72 + 8 * i].rearrange("p (t n) -> p t n", t=NT) for i in range(2)]
                pick = rt[:, 80:88].rearrange("p (t n) -> p t n", t=NT)
                m12 = [rt[:, 88 + 2 * i:90 + 2 * i].rearrange("p (t n) -> p t n", t=NT) for i in range(2)]
                prod = rt[:, 96:128].rearrange("p (t g n) -> p t g n", t=NT, g=NG)
                den2 = rt[:, 128:130].rearrange("p (t n) -> p t n", t=NT)
                gpr = rt[:, 130:132].rearrange("p (t n) -> p t n", t=NT)
                ranks = rt[:, 132:140].rearrange("p (t n) -> p t n", t=NT)
                total, big, over = rt[:, 140:144], rt[:, 144:148], rt[:, 148:150]
                place3, over3 = place.unsqueeze(2), over.unsqueeze(2)
                plan_f = rt[:, 152:154]
                fb = const("first").unsqueeze(1).to_broadcast([P, NT, 4])

                def choose(hot_, vals, top):
                    step(dve.tensor_reduce(top, vals, AX_X, ALU.max))
                    tt(hot_, vals, top.to_broadcast([P, NT, 4]), ALU.is_equal)
                    tt(hot_, hot_, fb, ALU.mult)
                    step(dve.tensor_reduce(mx, hot_, AX_X, ALU.max))
                    tt(hot_, hot_, mx.to_broadcast([P, NT, 4]), ALU.is_equal)

                choose(one[0], lg[:, :, 0:4], mg)
                dve.sem_inc(g_ready, 1)
                tt(ex[:, :, 0:4], lg[:, :, 0:4], mg.to_broadcast([P, NT, 4]), ALU.subtract)
                take(4)
                step(dve.tensor_copy(rt[:, 132:144], PS[:, 4, 0:12]))
                give(4)
                tt(ranks, ranks, hot, ALU.mult)
                step(dve.tensor_reduce(place3, ranks, AX_X, ALU.add))
                ts(over, place, float(P), None, ALU.is_ge)
                stt(place, over, -float(P), place, ALU.mult, ALU.add)
                step(dve.tensor_copy(inside[:, :, NG:NG + 1], over3))
                ts(over, over, -1.0, 1.0, ALU.mult, ALU.add)
                tt(inside[:, :, 0:NG], hot, over3.to_broadcast([P, NT, NG]), ALU.mult)
                spot = const("place")

                def pick_tile(b):
                    for t in range(NT):
                        ins = dve.tensor_scalar(pick01[:, t, :], spot, place[:, t:t + 1], inside[:, t, bass.ds(b, 1)],
                                                ALU.is_equal, ALU.mult)
                    return ins

                step(pick_tile(0))
                dve.sem_inc(pick_ready, 1)
                step(dve.tensor_reduce(plan_f[:, 0:1], total, AX_X, ALU.max))
                ts(big, total, float(P), None, ALU.is_gt)
                tt(big, big, const("index"), ALU.mult)
                step(dve.tensor_reduce(plan_f[:, 1:2], big, AX_X, ALU.max))
                step(dve.tensor_copy(plan_i[:], plan_f))
                dve.sem_inc(plan_ready, 1)
                for t in range(NT):
                    tt(prod[:, t], lg[:, t, 4:20].rearrange("p (g n) -> p g n", g=NG),
                       one[0][:, t, :].unsqueeze(2).to_broadcast([P, NG, 4]), ALU.mult)
                    step(dve.tensor_reduce(pick[:, t, :], prod[:, t].rearrange("p g n -> p n g"), AX_X, ALU.add))
                choose(one[1], pick, m12[0])
                stt(pick.rearrange("p t n -> p (t n)"), one[1].rearrange("p t n -> p (t n)"), NEG,
                    pick.rearrange("p t n -> p (t n)"), ALU.mult, ALU.add)
                choose(one[2], pick, m12[1])
                tt(ex[:, :, 4:5], m12[1], m12[0], ALU.subtract)
                dve.sem_inc(logit_ready, 1)
                dve.wait_ge(rexp_ready, layer + 1)
                step(dve.tensor_reduce(gpr, ex[:, :, 0:4], AX_X, ALU.add))
                ts(den2, ex[:, :, 4:5], 1.0, None, ALU.add)
                tt(gpr, gpr, den2, ALU.mult)
                step(dve.reciprocal(gpr, gpr))
                tt(one[2], one[2], ex[:, :, 4:5].to_broadcast([P, NT, 4]), ALU.mult)
                tt(one[1], one[1], one[2], ALU.add)
                tt(own, one[1], gpr.to_broadcast([P, NT, 4]), ALU.mult)
                dve.sem_inc(own_ready, 1)
                exp_ = PLAN.experts[layer]
                base, base_full = at_experts[layer]

                def gathered_lo(b, value):
                    dve.wait_ge(xTh_ready, value)
                    c = 4 * (b - 5)
                    return dve.tensor_tensor(xTl[:, c:c + 4, :], PS[:, b, :].rearrange("p (c t) -> p c t", c=4),
                                             xTh[:, c:c + 4, :].bitcast(F32), ALU.subtract)

                x0 = layer * 2 * (NG + 1)
                gathered_lo(5, x0 + 1).then_inc(bank_read[5], 1)
                dve.wait_ge(bank_full[7], base_full[7])
                dve.tensor_copy(weight, PS[:, 7, 0:EPG]).then_inc(bank_read[7], 1)
                tally = {}

                def signal(ins, s):
                    ins.then_inc(s, 1)
                    tally[s.name] = (s, tally.get(s.name, (s, 0))[1] + 1)

                def group_tile(i, more):
                    def full(b, n):
                        dve.wait_ge(bank_full[b], i * TILE_FULL[b] + (base_full[b] + n + 1))

                    def through(q):
                        dve.wait_ge(piece_used, i * EXPERT_PIECES + (PLAN.experts[layer]["pieces"] + q + 1))

                    def lo(q):
                        if q % 3 == 0:
                            return
                        w = (exp_["pieces"] + q) % HL
                        dve.wait_ge(hi_ready, i * EXPERT_PIECES + (exp_["pieces"] + q + 1))
                        signal(dve.tensor_tensor(pieces_of(wl[:, w, :], q), raw_piece(exp_, q),
                                                 pieces_of(wh[:, w, :].bitcast(F32), q), ALU.subtract), lo_v)

                    def turned_lo(e):
                        dve.wait_ge(hidTh_ready, i * EPG + (layer * EPG * (NG + 1) + e + 1))
                        signal(dve.tensor_tensor(hidTl[:], PS[:, 1, :].rearrange("p (c t) -> p c t", c=4),
                                                 hidTh[:].bitcast(F32), ALU.subtract), bank_read[1])

                    for q in range(2):
                        lo(q)
                    signal(gathered_lo(6, i * 2 + (x0 + 2)), bank_read[6])
                    for q in range(2, 4):
                        lo(q)
                    full(7, 0)
                    signal(dve.tensor_copy(pickT, PS[:, 7, 0:NT * P].rearrange("p (t n) -> p t n", t=NT)),
                           bank_read[7])
                    if more:
                        signal(pick_tile(i + 1), pick_ready)
                    for s, (which, e) in enumerate(SEGMENTS):
                        ahead = range(4 * s + 4, 4 * s + 8) if s < 11 else ()
                        for q in ahead[0:2]:
                            lo(q)
                        if which == 0 and e:
                            turned_lo(e - 1)
                        for q in ahead[2:3]:
                            lo(q)
                        if which == 1:
                            through(4 * s + 3)
                            dve.wait_ge(bank_read[0], i * TILE_JOBS[0] + (base[0] + e + 1))
                            if e == 0:
                                dve.wait_ge(bank_read[7], i * TILE_JOBS[7] + base[7])
                            signal(dve.scalar_tensor_tensor(out=hid[e % 2], in0=PS[:, 4, :], scalar=weight[:, e:e + 1],
                                                            in1=hid[e % 2], op0=ALU.mult, op1=ALU.mult), bank_read[4])
                        for q in ahead[3:4]:
                            lo(q)
                        if s == 10:
                            turned_lo(3)
                            if more:
                                signal(gathered_lo(5, i * 2 + (x0 + 3)), bank_read[5])
                                full(7, 1)
                                signal(dve.tensor_copy(weight, PS[:, 7, 0:EPG]), bank_read[7])
                    for n, b in enumerate((7, 5, 6, 4)):
                        t, half = n % 2, n // 2
                        full(b, {7: 2, 5: 1, 6: 1, 4: 0}[b] if more else {7: 1, 5: 0, 6: 1, 4: 0}[b])
                        xs = x[:, t, half * W:(half + 1) * W]
                        signal(dve.tensor_tensor(xs, xs, PS[:, b, :], ALU.add), bank_read[b])

                with dve.Fori(0, NG) as i:
                    group_tile(i, True)
                dve.wait_ge(bank_read[4], base[4] + NG * TILE_JOBS[4])
                dve.sem_inc(tiles_done, 1)
                largest, _ = counts(dve)
                tally.clear()
                with dve.If(largest > P):
                    group_tile(NG, False)
                with dve.Else():
                    for s, n in tally.values():
                        dve.sem_inc(s, n)
                for b in range(8):
                    taken[b] = base_full[b] + NG * TILE_FULL[b] + LAST_FULL[b]
                dve.wait_ge(bank_read[4], base[4] + NG * TILE_JOBS[4] + LAST_JOBS[4])
            norm(2 * LAYERS + 1, "final")
            dve.wait_ge(fin_in, 16)
            fg = bc[:, 0:2, :].rearrange("p a n -> p (a n)")
            for t in range(NT):
                if t:
                    dve.wait_ge(hnat_a, 2 * LAYERS + 2)
                tt(h_nat[:, t, :], h_nat[:, t, :], fg, ALU.mult)
                dve.sem_inc(fin_done, 1)


_INS = ['x', 'positions', 'norm_mix_g', 'w_in', 'gmlp_ln_g', 'gmlp_ln_b', 'gmlp_ws', 'gmlp_bs', 'rwkv_mu_rkv',
        'rwkv_mu_wag', 'rwkv_w0', 'rwkv_w1', 'rwkv_w2', 'rwkv_a0', 'rwkv_a1', 'rwkv_a2', 'rwkv_g1', 'rwkv_g2',
        'rwkv_k_k', 'rwkv_k_a', 'rwkv_r_k', 'rwkv_ln_w', 'rwkv_ln_b', 'rwkv_mu_v', 'rwkv_v0', 'rwkv_v1', 'rwkv_v2',
        'w_branch_a', 'w_branch_b', 'w_branch_c', 'w_gate', 'b_gate', 'w_out', 'norm_ffn_g', 'router_group_w',
        'router_group_b', 'router_expert_w', 'router_expert_b', 'expert_w_gate', 'expert_w_up', 'expert_w_down',
        'final_norm_g']


def kernel(**inputs):
    import numpy as _np
    import concourse.bacc as _bacc
    from concourse import mybir as _mybir
    from concourse.bass_utils import run_bass_kernel_spmd as _run

    nc = _bacc.Bacc("TRN2", target_bir_lowering=False, num_devices=1)
    given = {name: _np.ascontiguousarray(inputs[name]) for name in _INS}
    given["table"] = TABLE
    arrays, args = {}, {}
    for name, v in given.items():
        arrays[f"in_{name}"] = v
        args[name] = nc.dram_tensor(f"in_{name}", v.shape, _mybir.dt.from_np(v.dtype), kind="ExternalInput").ap()
    args["out"] = nc.dram_tensor("out_0", (1, S, D), F32, kind="ExternalOutput").ap()
    hybrid_moe_kernel(nc, args)
    r = _run(nc, [arrays], core_ids=[0])
    return r.results[0]["out_0"]
```
